# Optimizing a Trainium2 kernel written in Bass

```python
import math
import jax, jax.numpy as jnp
from jax import lax
import numpy as np

D_MODEL = 1024
BATCH = 1
SEQ = 256
DEPTH = 2

D_MIX = D_MODEL
N_DIRS = 2
DN_HEADS = 4
DN_DK = 128
DN_DV = 128
DN_KEY = DN_HEADS * DN_DK
DN_VAL = DN_HEADS * DN_DV
DN_CONV = 5
DN_CHUNK = 64
HY_WIDTH = D_MIX - DN_VAL
HY_ORDER = 2
HY_SHORT = 3
HY_EMB = 33
HY_FILTER_HIDDEN = 64
HY_DIRS = 2
HY_FAST_DECAY_PCT = 0.3
HY_SLOW_DECAY_PCT = 1.5
HY_DECAY_TARGET = 1e-2
D_FF = 2816
RMS_EPS = 1e-6

_O_Q = DN_KEY
_O_K = 2 * DN_KEY
_O_V = _O_K + DN_VAL
_O_Z = _O_V + DN_VAL
_O_B = _O_Z + N_DIRS * DN_HEADS
_O_A = _O_B + N_DIRS * DN_HEADS
D_IN = _O_A + 3 * HY_WIDTH
IN_SPLITS = (_O_Q, _O_K, _O_V, _O_Z, _O_B, _O_A)


def _rmsnorm(x, w):
    xf = x.astype(jnp.float32)
    y = xf * lax.rsqrt(jnp.mean(xf * xf, axis=-1, keepdims=True) + RMS_EPS)
    return (y * w.astype(jnp.float32)).astype(x.dtype)

def _l2norm(t):
    return t * lax.rsqrt(jnp.sum(t * t, axis=-1, keepdims=True) + 1e-6)

def _swiglu(h, w_gate, w_up, w_down):
    return (jax.nn.silu(h @ w_gate) * (h @ w_up)) @ w_down

def _dwconv(x, w):
    k = w.shape[0]
    return lax.conv_general_dilated(
        x, w[:, None, :].astype(x.dtype), window_strides=(1,),
        padding=[(k // 2, k // 2)], dimension_numbers=("NWC", "WIO", "NWC"),
        feature_group_count=x.shape[-1])

def _gated_delta_rule(q, k, v, beta, g):
    b, h, l, dk = q.shape
    dv = v.shape[-1]
    c = DN_CHUNK
    n = l // c
    q = q.reshape(b, h, n, c, dk)
    k = k.reshape(b, h, n, c, dk)
    v = v.reshape(b, h, n, c, dv)
    beta = beta.reshape(b, h, n, c)
    g = jnp.cumsum(g.reshape(b, h, n, c), axis=-1)
    incl = jnp.tril(jnp.ones((c, c), bool))
    strict = jnp.tril(jnp.ones((c, c), bool), -1)
    diff = g[..., :, None] - g[..., None, :]
    decay = jnp.where(incl, jnp.exp(jnp.where(incl, diff, 0.0)), 0.0)
    kb = k * beta[..., None]
    a_mat = jnp.where(strict, jnp.einsum("bhnid,bhnjd->bhnij", kb, k) * decay, 0.0)
    a_mat = a_mat + jnp.eye(c, dtype=q.dtype)
    rhs = jnp.concatenate([v * beta[..., None], kb * jnp.exp(g)[..., None]], axis=-1)
    sol = lax.linalg.triangular_solve(a_mat, rhs, left_side=True, lower=True,
                                      unit_diagonal=True)
    u, w = sol[..., :dv], sol[..., dv:]
    attn = jnp.einsum("bhnid,bhnjd->bhnij", q, k) * decay
    g_last = g[..., -1]
    q_dec = q * jnp.exp(g)[..., None]
    k_dec = k * jnp.exp(g_last[..., None] - g)[..., None]

    def step(state, inp):
        q_i, k_i, u_i, w_i, attn_i, gl_i = inp
        v_new = u_i - jnp.einsum("bhcd,bhde->bhce", w_i, state)
        o_i = (jnp.einsum("bhcd,bhde->bhce", q_i, state)
               + jnp.einsum("bhcs,bhse->bhce", attn_i, v_new))
        state = (state * jnp.exp(gl_i)[..., None, None]
                 + jnp.einsum("bhcd,bhce->bhde", k_i, v_new))
        return state, o_i

    xs = tuple(jnp.moveaxis(t, 2, 0) for t in (q_dec, k_dec, u, w, attn, g_last))
    state0 = jnp.zeros((b, h, dk, dv), q.dtype)
    _, o = lax.scan(step, state0, xs)
    return jnp.moveaxis(o, 0, 2).reshape(b, h, l, dv)

def _deltanet_group(q, k, v, z, beta_logit, alpha, a_log, dt_bias, conv_w, norm_w):
    f32 = jnp.float32
    b, l, _ = q.shape
    qkv = jax.nn.silu(_dwconv(jnp.concatenate([q, k, v], axis=-1), conv_w))
    q, k, v = jnp.split(qkv, [DN_KEY, 2 * DN_KEY], axis=-1)

    def to_heads(t, d):
        return t.reshape(b, l, DN_HEADS, d).transpose(0, 2, 1, 3).astype(f32)

    q = _l2norm(to_heads(q, DN_DK)) * (DN_DK ** -0.5)
    k = _l2norm(to_heads(k, DN_DK))
    v = to_heads(v, DN_DV)
    beta = jax.nn.sigmoid(beta_logit.astype(f32)).reshape(b, l, N_DIRS, DN_HEADS).transpose(2, 0, 3, 1)
    a_in = alpha.astype(f32).reshape(b, l, N_DIRS, DN_HEADS).transpose(2, 0, 3, 1)
    g = -jnp.exp(a_log.astype(f32))[:, None, :, None] * jax.nn.softplus(
        a_in + dt_bias.astype(f32)[:, None, :, None])
    o_fwd = _gated_delta_rule(q, k, v, beta[0], g[0])
    flip = lambda t: jnp.flip(t, axis=2)
    o_bwd = flip(_gated_delta_rule(flip(q), flip(k), flip(v), flip(beta[1]), flip(g[1])))
    o = (o_fwd + o_bwd).transpose(0, 2, 1, 3)
    o = _rmsnorm(o, norm_w) * jax.nn.silu(z.reshape(b, l, DN_HEADS, DN_DV).astype(f32))
    return o.reshape(b, l, DN_VAL).astype(z.dtype)

def _hyena_filter_spectrum(l, w1, b1, w2, b2, w3, b3, freq, wout):
    f32 = jnp.float32
    t = jnp.linspace(0.0, 1.0, l, dtype=f32)[:, None]
    bands = (HY_EMB - 1) // 2
    ang = ((2.0 * math.pi / l) * jnp.arange(l, dtype=f32)[:, None]
           * jnp.linspace(1e-4, bands - 1, bands, dtype=f32)[None, :])
    feats = jnp.concatenate([t, jnp.cos(ang), -jnp.sin(ang)], axis=-1)
    fr = freq.astype(f32)
    hdn = jnp.sin(fr * (feats @ w1.astype(f32) + b1.astype(f32)))
    hdn = jnp.sin(fr * (hdn @ w2.astype(f32) + b2.astype(f32)))
    hdn = jnp.sin(fr * (hdn @ w3.astype(f32) + b3.astype(f32)))
    filt = (hdn @ wout.astype(f32)).reshape(l, HY_DIRS, HY_ORDER, HY_WIDTH)
    max_decay = math.log(HY_DECAY_TARGET) / HY_FAST_DECAY_PCT
    min_decay = math.log(HY_DECAY_TARGET) / HY_SLOW_DECAY_PCT
    deltas = jnp.abs(jnp.linspace(min_decay, max_decay, HY_WIDTH, dtype=f32))
    filt = filt * jnp.exp(-t * deltas)[:, None, None, :]
    fwd, bwd = filt[:, 0], filt[:, 1]
    two_sided = jnp.concatenate(
        [fwd, jnp.zeros((1, HY_ORDER, HY_WIDTH), f32), jnp.flip(bwd[: l - 1], axis=0)], axis=0)
    return jnp.fft.rfft(two_sided, axis=0)

def _fft_conv(z, kspec):
    l = z.shape[1]
    zs = jnp.fft.rfft(z, n=2 * l, axis=1)
    return jnp.fft.irfft(zs * kspec[None], n=2 * l, axis=1)[:, :l]

def _hyena_group(u, conv_w, conv_b, w1, b1, w2, b2, w3, b3, freq, wout, skip, norm_w):
    f32 = jnp.float32
    l = u.shape[1]
    u = _dwconv(u, conv_w) + conv_b
    v, x1, x2 = [t.astype(f32) for t in jnp.split(u, 3, axis=-1)]
    kspec = _hyena_filter_spectrum(l, w1, b1, w2, b2, w3, b3, freq, wout)
    skip = skip.astype(f32)
    zz = v
    for o, gate in enumerate((x1, x2)):
        zz = gate * (_fft_conv(zz, kspec[:, o]) + skip[o] * zz)
    return _rmsnorm(zz, norm_w).astype(u.dtype)

def first_inputs(seed: int = 0) -> dict:
    key = jax.random.key(seed)
    ks = iter(jax.random.split(key, 40))
    f32 = jnp.float32

    def nrm(shape, scale):
        return scale * jax.random.normal(next(ks), shape, f32)

    def gain(shape):
        return 1.0 + 0.02 * jax.random.normal(next(ks), shape, f32)

    x = jax.random.normal(next(ks), (BATCH, SEQ, D_MODEL), f32)
    a_log = jnp.log(jax.random.uniform(next(ks), (DEPTH, N_DIRS, DN_HEADS), f32, 1.0, 16.0))
    dt = jnp.exp(jax.random.uniform(next(ks), (DEPTH, N_DIRS, DN_HEADS), f32,
                                    math.log(1e-3), math.log(1e-1)))
    dt_bias = dt + jnp.log(-jnp.expm1(-dt))
    hf = HY_FILTER_HIDDEN
    return {
        "x": x,
        "ffn1_norm": gain((DEPTH, D_MODEL)),
        "ffn1_w_gate": nrm((DEPTH, D_MODEL, D_FF), D_MODEL ** -0.5),
        "ffn1_w_up": nrm((DEPTH, D_MODEL, D_FF), D_MODEL ** -0.5),
        "ffn1_w_down": nrm((DEPTH, D_FF, D_MODEL), D_FF ** -0.5),
        "mix_norm": gain((DEPTH, D_MODEL)),
        "w_in": nrm((DEPTH, D_MODEL, D_IN), D_MODEL ** -0.5),
        "dn_conv": nrm((DEPTH, DN_CONV, 2 * DN_KEY + DN_VAL), DN_CONV ** -0.5),
        "dn_a_log": a_log,
        "dn_dt_bias": dt_bias,
        "dn_norm": gain((DEPTH, DN_DV)),
        "hy_conv": nrm((DEPTH, HY_SHORT, 3 * HY_WIDTH), HY_SHORT ** -0.5),
        "hy_conv_bias": nrm((DEPTH, 3 * HY_WIDTH), 0.02),
        "hy_f_w1": nrm((DEPTH, HY_EMB, hf), HY_EMB ** -0.5),
        "hy_f_b1": nrm((DEPTH, hf), 0.1),
        "hy_f_w2": nrm((DEPTH, hf, hf), hf ** -0.5),
        "hy_f_b2": nrm((DEPTH, hf), 0.1),
        "hy_f_w3": nrm((DEPTH, hf, hf), hf ** -0.5),
        "hy_f_b3": nrm((DEPTH, hf), 0.1),
        "hy_f_freq": gain((DEPTH, hf)),
        "hy_f_wout": nrm((DEPTH, hf, HY_DIRS * HY_ORDER * HY_WIDTH), 0.05 * hf ** -0.5),
        "hy_skip": nrm((DEPTH, HY_ORDER, HY_WIDTH), 1.0),
        "hy_norm": gain((DEPTH, HY_WIDTH)),
        "w_out": nrm((DEPTH, D_MIX, D_MODEL), D_MIX ** -0.5),
        "ffn2_norm": gain((DEPTH, D_MODEL)),
        "ffn2_w_gate": nrm((DEPTH, D_MODEL, D_FF), D_MODEL ** -0.5),
        "ffn2_w_up": nrm((DEPTH, D_MODEL, D_FF), D_MODEL ** -0.5),
        "ffn2_w_down": nrm((DEPTH, D_FF, D_MODEL), D_FF ** -0.5),
        "final_norm": gain((D_MODEL,)),
    }

def first_block(x, ffn1_norm, ffn1_w_gate, ffn1_w_up, ffn1_w_down, mix_norm, w_in,
              dn_conv, dn_a_log, dn_dt_bias, dn_norm, hy_conv, hy_conv_bias,
              hy_f_w1, hy_f_b1, hy_f_w2, hy_f_b2, hy_f_w3, hy_f_b3, hy_f_freq,
              hy_f_wout, hy_skip, hy_norm, w_out, ffn2_norm, ffn2_w_gate,
              ffn2_w_up, ffn2_w_down, final_norm):
    for i in range(DEPTH):
        x = x + 0.5 * _swiglu(_rmsnorm(x, ffn1_norm[i]), ffn1_w_gate[i], ffn1_w_up[i], ffn1_w_down[i])
        proj = _rmsnorm(x, mix_norm[i]) @ w_in[i]
        q, k, v, z, beta_logit, alpha, hy_in = jnp.split(proj, IN_SPLITS, axis=-1)
        o_dn = _deltanet_group(q, k, v, z, beta_logit, alpha, dn_a_log[i], dn_dt_bias[i],
                               dn_conv[i], dn_norm[i])
        o_hy = _hyena_group(hy_in, hy_conv[i], hy_conv_bias[i], hy_f_w1[i], hy_f_b1[i],
                            hy_f_w2[i], hy_f_b2[i], hy_f_w3[i], hy_f_b3[i], hy_f_freq[i],
                            hy_f_wout[i], hy_skip[i], hy_norm[i])
        x = x + jnp.concatenate([o_dn, o_hy], axis=-1) @ w_out[i]
        x = x + 0.5 * _swiglu(_rmsnorm(x, ffn2_norm[i]), ffn2_w_gate[i], ffn2_w_up[i], ffn2_w_down[i])
    return _rmsnorm(x, final_norm)


DA_HEADS = 4
DA_QK_DIM = 64
DA_V_DIM = 2 * DA_QK_DIM
RET_HEADS = 4
RET_QK_DIM = 64
RET_V_DIM = 64
RET_CHUNK = 128
SC_WIDTH = 256
SC_GROUPS = 4
CONV_W = 3
REL_BUCKETS = 32
REL_MAX_DIST = 128
ROPE_THETA = 10000.0
Q_BLOCK = 128
EPS = 1e-6
N_BRANCH = 3

DA_QK_W = DA_HEADS * 2 * DA_QK_DIM
DA_V_W = DA_HEADS * DA_V_DIM
RET_QK_W = RET_HEADS * RET_QK_DIM
RET_V_W = RET_HEADS * RET_V_DIM
IN_SPLITS_2 = (DA_QK_W, DA_QK_W, DA_V_W,
             RET_QK_W, RET_QK_W, RET_V_W, RET_V_W,
             SC_WIDTH, SC_WIDTH, SC_WIDTH,
             N_BRANCH * D_MODEL)
IN_WIDTH = 2 * DA_QK_W + DA_V_W + 2 * RET_QK_W + 2 * RET_V_W + 3 * SC_WIDTH + N_BRANCH * D_MODEL


def rmsnorm(x, g):
    xf = x.astype(jnp.float32)
    y = xf * lax.rsqrt(jnp.mean(xf * xf, axis=-1, keepdims=True) + EPS)
    return (y * g.astype(jnp.float32)).astype(x.dtype)

def causal_dwconv(x, w, b):
    S = x.shape[1]
    K = w.shape[0]
    xp = jnp.pad(x, ((0, 0), (K - 1, 0), (0, 0)))
    y = b + xp[:, 0:S] * w[0]
    for k in range(1, K):
        y = y + xp[:, k:k + S] * w[k]
    return y

def rel_bucket(n):
    max_exact = REL_BUCKETS // 2
    nf = jnp.maximum(n, 1).astype(jnp.float32)
    large = max_exact + (jnp.log(nf / max_exact) / math.log(REL_MAX_DIST / max_exact)
                         * (REL_BUCKETS - max_exact)).astype(jnp.int32)
    large = jnp.minimum(large, REL_BUCKETS - 1)
    return jnp.where(n < max_exact, n, large)

def rotary(x, pos):
    d = x.shape[-1]
    half = d // 2
    inv = ROPE_THETA ** (-jnp.arange(half, dtype=jnp.float32) / half)
    ang = pos.astype(jnp.float32)[:, None] * inv[None, :]
    cos = jnp.cos(ang)[None, :, None, :]
    sin = jnp.sin(ang)[None, :, None, :]
    xf = x.astype(jnp.float32)
    x1, x2 = xf[..., :half], xf[..., half:]
    return jnp.concatenate([x1 * cos - x2 * sin, x2 * cos + x1 * sin], axis=-1)

def diff_attention(q, k, v, lam, bias_dist):
    B, S, H = q.shape[0], q.shape[1], q.shape[2]
    qh = jnp.transpose(q, (0, 2, 3, 1, 4)).astype(jnp.float32)
    kh = jnp.transpose(k, (0, 2, 3, 1, 4)).astype(jnp.float32)
    vh = jnp.transpose(v, (0, 2, 1, 3)).astype(jnp.float32)
    kpos = jnp.arange(S)
    neg = jnp.finfo(jnp.float32).min

    def block(i):
        start = i * Q_BLOCK
        qb = lax.dynamic_slice_in_dim(qh, start, Q_BLOCK, axis=3)
        dist = (start + jnp.arange(Q_BLOCK))[:, None] - kpos[None, :]
        bias = jnp.transpose(bias_dist[jnp.maximum(dist, 0)], (2, 0, 1)).astype(jnp.float32)
        s = jnp.einsum('bhmqd,bhmkd->bhmqk', qb, kh) + bias[None, :, None]
        s = jnp.where(dist >= 0, s, neg)
        p = jax.nn.softmax(s, axis=-1)
        a = p[:, :, 0] - lam * p[:, :, 1]
        return jnp.einsum('bhqk,bhke->bhqe', a, vh)

    out = lax.map(block, jnp.arange(S // Q_BLOCK))
    return jnp.transpose(out, (1, 0, 3, 2, 4)).reshape(B, S, H, -1)

def retention(q, k, v):
    B, S, H, dk = q.shape
    dv = v.shape[-1]
    C = RET_CHUNK
    N = S // C
    lg = jnp.log(1.0 - 2.0 ** (-5.0 - jnp.arange(H, dtype=jnp.float32)))
    to_chunks = lambda t: jnp.transpose(t.astype(jnp.float32).reshape(B, N, C, H, t.shape[-1]), (0, 3, 1, 2, 4))
    qc, kc, vc = to_chunks(q), to_chunks(k), to_chunks(v)
    idx = jnp.arange(C, dtype=jnp.float32)
    diff = idx[:, None] - idx[None, :]
    d_intra = jnp.where(diff[None] >= 0, jnp.exp(lg[:, None, None] * jnp.maximum(diff, 0.0)[None]), 0.0)
    inner = jnp.einsum('bhncd,bhnjd->bhncj', qc, kc) * d_intra[None, :, None]
    inner = jnp.einsum('bhncj,bhnje->bhnce', inner, vc)
    k_dec = kc * jnp.exp(lg[:, None] * (C - 1 - idx)[None])[None, :, None, :, None]
    kv = jnp.einsum('bhncd,bhnce->nbhde', k_dec, vc)
    chunk_decay = jnp.exp(lg * C)[None, :, None, None]

    def step(R, kv_n):
        return R * chunk_decay + kv_n, R

    _, R_prev = lax.scan(step, jnp.zeros((B, H, dk, dv), jnp.float32), kv)
    q_dec = qc * jnp.exp(lg[:, None] * (idx + 1.0)[None])[None, :, None, :, None]
    cross = jnp.einsum('bhncd,nbhde->bhnce', q_dec, R_prev)
    o = inner + cross
    return jnp.transpose(o, (0, 2, 3, 1, 4)).reshape(B, S, H, dv)

def second_inputs(seed: int = 0) -> dict:
    key = jax.random.key(seed)
    ks = jax.random.split(key, 24)
    f32 = jnp.float32
    nrm = lambda k, shape, s: jax.random.normal(k, shape, f32) * s
    gain = lambda k, shape: 1.0 + 0.05 * jax.random.normal(k, shape, f32)
    return {
        "x": nrm(ks[0], (BATCH, SEQ, D_MODEL), 1.0),
        "rel_bias": nrm(ks[1], (REL_BUCKETS, DA_HEADS), 0.5),
        "norm_mix_g": gain(ks[2], (DEPTH, D_MODEL)),
        "w_in": nrm(ks[3], (DEPTH, D_MODEL, IN_WIDTH), D_MODEL ** -0.5),
        "b_gate": nrm(ks[4], (DEPTH, N_BRANCH * D_MODEL), 0.02),
        "da_q_norm_g": gain(ks[5], (DEPTH, DA_QK_DIM)),
        "da_k_norm_g": gain(ks[6], (DEPTH, DA_QK_DIM)),
        "da_lambda": nrm(ks[7], (DEPTH, 4, DA_QK_DIM), 0.1),
        "da_subln_g": gain(ks[8], (DEPTH, DA_V_DIM)),
        "ret_norm_g": gain(ks[9], (DEPTH, RET_V_DIM)),
        "sc_conv_w": nrm(ks[10], (DEPTH, CONV_W, SC_WIDTH), CONV_W ** -0.5),
        "sc_conv_b": nrm(ks[11], (DEPTH, SC_WIDTH), 0.02),
        "w_branch_da": nrm(ks[12], (DEPTH, DA_V_W, D_MODEL), DA_V_W ** -0.5),
        "w_branch_ret": nrm(ks[13], (DEPTH, RET_V_W, D_MODEL), RET_V_W ** -0.5),
        "w_branch_sc": nrm(ks[14], (DEPTH, SC_WIDTH, D_MODEL), SC_WIDTH ** -0.5),
        "w_out": nrm(ks[15], (DEPTH, D_MODEL, D_MODEL), 0.5 * D_MODEL ** -0.5),
        "norm_ffn_g": gain(ks[16], (DEPTH, D_MODEL)),
        "w_ffn_in": nrm(ks[17], (DEPTH, D_MODEL, 2 * D_FF), D_MODEL ** -0.5),
        "ffn_conv_w": nrm(ks[18], (DEPTH, CONV_W, D_FF), CONV_W ** -0.5),
        "ffn_conv_b": nrm(ks[19], (DEPTH, D_FF), 0.02),
        "w_ffn_out": nrm(ks[20], (DEPTH, D_FF, D_MODEL), 0.5 * D_FF ** -0.5),
    }

def second_block(x, rel_bias, norm_mix_g, w_in, b_gate, da_q_norm_g, da_k_norm_g, da_lambda,
              da_subln_g, ret_norm_g, sc_conv_w, sc_conv_b, w_branch_da, w_branch_ret,
              w_branch_sc, w_out, norm_ffn_g, w_ffn_in, ffn_conv_w, ffn_conv_b, w_ffn_out):
    B, S, D = x.shape
    pos = jnp.arange(S)
    bias_dist = rel_bias[rel_bucket(pos)]
    offs = np.cumsum(IN_SPLITS_2)[:-1].tolist()
    for l in range(DEPTH):
        h = rmsnorm(x, norm_mix_g[l])
        proj = jnp.einsum('bsd,de->bse', h, w_in[l])
        (da_q, da_k, da_v, r_q, r_k, r_v, r_g,
         sc_b, sc_c, sc_x, gate_pre) = jnp.split(proj, offs, axis=-1)

        lam_init = 0.8 - 0.6 * math.exp(-0.3 * l)
        lp = da_lambda[l].astype(jnp.float32)
        lam = jnp.exp(jnp.sum(lp[0] * lp[1])) - jnp.exp(jnp.sum(lp[2] * lp[3])) + lam_init
        q = rmsnorm(da_q.reshape(B, S, DA_HEADS, 2, DA_QK_DIM), da_q_norm_g[l]) * (DA_QK_DIM ** -0.5)
        k = rmsnorm(da_k.reshape(B, S, DA_HEADS, 2, DA_QK_DIM), da_k_norm_g[l])
        v = da_v.reshape(B, S, DA_HEADS, DA_V_DIM)
        o_da = diff_attention(q, k, v, lam, bias_dist)
        o_da = (rmsnorm(o_da, da_subln_g[l]) * (1.0 - lam_init)).astype(x.dtype).reshape(B, S, DA_V_W)

        rq = rotary(r_q.reshape(B, S, RET_HEADS, RET_QK_DIM), pos)
        rk = rotary(r_k.reshape(B, S, RET_HEADS, RET_QK_DIM), pos) * (RET_QK_DIM ** -0.5)
        rv = r_v.reshape(B, S, RET_HEADS, RET_V_DIM)
        o_ret = rmsnorm(retention(rq, rk, rv), ret_norm_g[l]).reshape(B, S, RET_V_W)
        o_ret = (o_ret * jax.nn.silu(r_g.astype(jnp.float32))).astype(x.dtype)

        o_sc = sc_b * causal_dwconv(sc_c * sc_x, sc_conv_w[l], sc_conv_b[l])

        gates = jax.nn.sigmoid((gate_pre + b_gate[l]).astype(jnp.float32)).astype(x.dtype)
        gates = gates.reshape(B, S, N_BRANCH, D)
        y = (gates[:, :, 0] * jnp.einsum('bse,ed->bsd', o_da, w_branch_da[l])
             + gates[:, :, 1] * jnp.einsum('bse,ed->bsd', o_ret, w_branch_ret[l])
             + gates[:, :, 2] * jnp.einsum('bse,ed->bsd', o_sc, w_branch_sc[l]))
        x = x + jnp.einsum('bsd,de->bse', y, w_out[l])

        h = rmsnorm(x, norm_ffn_g[l])
        gu = jnp.einsum('bsd,df->bsf', h, w_ffn_in[l])
        g_ff, u_ff = gu[..., :D_FF], gu[..., D_FF:]
        g_ff = causal_dwconv(g_ff, ffn_conv_w[l], ffn_conv_b[l])
        x = x + jnp.einsum('bsf,fd->bsd', jax.nn.silu(g_ff) * u_ff, w_ffn_out[l])
    return x


def setup_inputs(seed=0):
    out = dict(first_inputs(seed))
    for name, value in second_inputs(seed + 1).items():
        if name != "x":
            out[name + "_2"] = value
    return out


def reference(
    x, ffn1_norm, ffn1_w_gate, ffn1_w_up, ffn1_w_down, mix_norm, w_in, dn_conv, dn_a_log,
    dn_dt_bias, dn_norm, hy_conv, hy_conv_bias, hy_f_w1, hy_f_b1, hy_f_w2, hy_f_b2, hy_f_w3,
    hy_f_b3, hy_f_freq, hy_f_wout, hy_skip, hy_norm, w_out, ffn2_norm, ffn2_w_gate, ffn2_w_up,
    ffn2_w_down, final_norm, rel_bias_2, norm_mix_g_2, w_in_2, b_gate_2, da_q_norm_g_2,
    da_k_norm_g_2, da_lambda_2, da_subln_g_2, ret_norm_g_2, sc_conv_w_2, sc_conv_b_2,
    w_branch_da_2, w_branch_ret_2, w_branch_sc_2, w_out_2, norm_ffn_g_2, w_ffn_in_2,
    ffn_conv_w_2, ffn_conv_b_2, w_ffn_out_2,
):
    x = first_block(
        x, ffn1_norm, ffn1_w_gate, ffn1_w_up, ffn1_w_down, mix_norm, w_in, dn_conv, dn_a_log,
        dn_dt_bias, dn_norm, hy_conv, hy_conv_bias, hy_f_w1, hy_f_b1, hy_f_w2, hy_f_b2, hy_f_w3,
        hy_f_b3, hy_f_freq, hy_f_wout, hy_skip, hy_norm, w_out, ffn2_norm, ffn2_w_gate,
        ffn2_w_up, ffn2_w_down, final_norm,
    )
    return second_block(
        x, rel_bias_2, norm_mix_g_2, w_in_2, b_gate_2, da_q_norm_g_2, da_k_norm_g_2,
        da_lambda_2, da_subln_g_2, ret_norm_g_2, sc_conv_w_2, sc_conv_b_2, w_branch_da_2,
        w_branch_ret_2, w_branch_sc_2, w_out_2, norm_ffn_g_2, w_ffn_in_2, ffn_conv_w_2,
        ffn_conv_b_2, w_ffn_out_2,
    )


_drawn_inputs = setup_inputs


def setup_inputs(seed=0):
    import zlib

    import numpy as np

    out = dict(_drawn_inputs(seed))
    spreads = {}
    factors = {'dn_norm': 3.93,
     'hy_f_freq': 8.0,
     'hy_norm': 2.749,
     'ffn2_norm': 4.392,
     'b_gate_2': 8.0,
     'da_q_norm_g_2': 4.211,
     'da_k_norm_g_2': 4.69,
     'da_subln_g_2': 4.041,
     'ret_norm_g_2': 5.753,
     'sc_conv_b_2': 6.973,
     'ffn_conv_b_2': 7.08}
    for name, (base, spread) in spreads.items():
        noise = np.random.default_rng([zlib.crc32(name.encode()), seed]).standard_normal(out[name].shape)
        drawn = base * np.exp(spread * noise) if base else spread * noise
        out[name] = __import__('jax').numpy.asarray(drawn.astype(out[name].dtype))
    for name, factor in factors.items():
        out[name] = (out[name] * factor).astype(out[name].dtype)
    return out
```

```python
import math
from contextlib import ExitStack

import numpy as np

import concourse.bass as bass
import concourse.mybir as mybir

F32 = mybir.dt.float32
F32R = mybir.dt.float32r
F16 = mybir.dt.float16
ALU = mybir.AluOpType
ACT = mybir.ActivationFunctionType
AX_X = mybir.AxisListType.X

P = 128
D = 1024
L = 256
RB = L // P
KC = D // P
DEPTH = 2
FF = 2816
NF = FF // P
EPS = 1e-6
KB = 1024

HEADS, DIRS, DN = 4, 2, 512
HYW, EMB, HID = 512, 33, 64
CONV1, CONV_HY = 5, 3
D_IN = 4 * DN + 2 * DIRS * HEADS + 3 * HYW
COL_BA = 4 * DN
COL_HY = COL_BA + 2 * DIRS * HEADS
LEVELS = 7
DA_W, RET_W, SC_W = 512, 256, 256
IN2 = 3 * DA_W + 4 * RET_W + 3 * SC_W + 3 * D
BUCKETS, MAX_DIST = 32, 128
HK = 384
MASKED = -1e30

RAW, SLOTS = 3, 4
HALF = 1024
AHEAD = 3


def kinds1():
    ffn = ["A"] * (2 * NF) + ["B"] * NF
    return ffn + ["A"] * 28 + ["B"] * 8 + ffn


def kinds2():
    return ["A"] * 50 + ["B"] * 16 + ["A"] * (2 * NF) + ["B"] * NF


KIND1, KIND2 = kinds1(), kinds2()
H1, H2 = len(KIND1), len(KIND2)
assert H1 % (2 * RAW) == 0 and H1 % SLOTS == 0 and H2 % (2 * RAW) == 0 and H2 % SLOTS == 0


def constants():
    f8 = np.float64
    i, j = np.arange(P)[:, None], np.arange(P)[None, :]
    c = {}
    blockones = (i // 64 == j // 64)
    flip = (i + j == P - 1)
    rot = np.zeros((P, P))
    for d in range(P):
        if d % 64 < 32:
            rot[d + 32, d] = -1
        else:
            rot[d - 32, d] = 1
    mats = [np.eye(P), np.ones((P, P)), blockones, flip, rot, i <= j, i >= j]
    c["mats"] = np.stack(mats, 1).astype(np.float32)
    neg = np.stack([np.where(i <= j, 0, -60000.0), np.where(i >= j, 0, -60000.0)], 1)
    lev = []
    for d in range(DIRS):
        for b in range(LEVELS):
            s = 1 << b
            a = (i // s % 2 == 0) & (j // s == i // s + 1)
            lev.append(a if d == 0 else a.T)
    c["masks"] = np.concatenate([neg, np.stack(lev, 1)], 1).astype(np.float16)
    t, f = np.arange(L, dtype=f8)[:, None], np.arange(L, dtype=f8)[None, :]
    th = 2 * math.pi / (2 * L)
    nyq = np.where(f == 0, np.cos(math.pi * t), 0)
    def six(tt, sign, nq):
        co, si = np.cos(th * tt * f), -sign * np.sin(th * tt * f)
        si[:, 0] = 0
        con = co.copy()
        con[:, 0] = nq
        sin_n = si.copy()
        sin_n[:, 0] = nq
        return [co[:, :P], co[:, P:], si[:, :P], si[:, P:], con[:, :P], sin_n[:, :P]]
    fwd = np.stack(six(t, 1, np.cos(math.pi * t[:, 0])), 1)
    bwd = np.stack(six(t + 1, -1, np.cos(math.pi * (t[:, 0] + 1))), 1)
    bwd[L - 1] = 0
    inv_re = np.cos(th * f.T * t.T) * np.where(f.T == 0, 1, 2) / (2 * L)
    inv_im = -np.sin(th * f.T * t.T) * 2 / (2 * L)
    inv_im[0] = np.cos(math.pi * t[:, 0]) / (2 * L)
    inv = np.concatenate([inv_re, inv_im], 0)
    lay = lambda a: a.reshape(a.shape[0] // P, P, -1).transpose(1, 0, 2)
    c["dft"] = np.concatenate([lay(fwd).reshape(P, -1), lay(bwd[:, :5]).reshape(P, -1),
                               lay(inv).reshape(P, -1)], 1).astype(np.float32)
    tt = np.linspace(0.0, 1.0, L)[:, None]
    bands = (EMB - 1) // 2
    ang = (2 * math.pi / L) * t * np.linspace(1e-4, bands - 1, bands)[None]
    c["feats"] = np.concatenate([tt, np.cos(ang), -np.sin(ang)], 1).T.astype(np.float32).copy()
    deltas = np.abs(np.linspace(math.log(1e-2) / 1.5, math.log(1e-2) / 0.3, HYW))
    c["decay"] = lay(np.exp(-tt * deltas)).astype(np.float32)
    inv_f = 10000.0 ** (-np.arange(32, dtype=f8) / 32)
    an = inv_f[np.arange(P) % 32][:, None] * np.arange(L)[None]
    co, si = np.cos(an), np.sin(an)
    c["rotary"] = np.stack([co, si, co / 8, si / 8], 1).astype(np.float32)
    lg = np.log(1.0 - 2.0 ** (-5.0 - np.arange(4)))
    dm = np.zeros((P, 4, 3 * P))
    for h in range(4):
        dg = np.where(j >= i, np.exp(lg[h] * np.maximum(j - i, 0)), 0)
        dm[:, h] = np.concatenate([dg, np.exp(lg[h] * (P + j - i)), dg], 1)
    c["retdecay"] = dm.astype(np.float32)
    n = np.arange(L)
    half = BUCKETS // 2
    large = half + (np.log(np.maximum(n, 1) / half) / math.log(MAX_DIST / half) * (BUCKETS - half)).astype(int)
    bucket = np.where(n < half, n, np.minimum(large, BUCKETS - 1))
    oh = np.zeros((BUCKETS, HK))
    oh[bucket[L - 1 - np.arange(L)], np.arange(L)] = 1
    c["onehot"] = oh.astype(np.float32)
    li = np.array([0.8 - 0.6 * math.exp(-0.3 * l) for l in range(DEPTH)])
    c["lam"] = np.stack([li, 1 - li], 1).astype(np.float32)
    return c


class Signal:

    def __init__(self, sem, per, start=0):
        self.sem, self.per, self.start = sem, per, start

    def due(self, l, k):
        return l * self.per + (self.start + k)


class Chain:

    def __init__(self, sem, start, per):
        self.sem, self.start, self.per, self.n = sem, start, per, 0

    def step(self, l):
        self.n += 1
        return l * self.per + (self.start + self.n)


def emit(nc, ins, out, count):
    steps = {}
    with ExitStack() as ctx:
        def sem(name):
            return ctx.enter_context(nc.semaphore(name))

        def sb(name, shape, dt=F32):
            return ctx.enter_context(nc.sbuf_tensor(name, shape, dt))

        def psum(name, shape):
            return ctx.enter_context(nc.psum_tensor(name, shape, F32))

        raw = sb("raw", [P, RAW, 2 * HALF])
        w_hi = sb("w_hi", [P, SLOTS, HALF], F32R)
        w_lo = sb("w_lo", [P, SLOTS, HALF], F32R)
        x = sb("x", [P, RB, D])
        xT_hi = sb("xT_hi", [P, KC, L], F32R)
        xT_lo = sb("xT_lo", [P, KC, L], F32R)
        gain = sb("gain", [P, D])
        mats = sb("mats", [P, 7, P])
        masks = sb("masks", [P, 2 + DIRS * LEVELS, P], F16)
        hankel = sb("hankel", [P, 4, L])
        rows = sb("rows", [P, P])
        cols = sb("cols", [P, P])
        relb = sb("relb", [BUCKETS, 4])
        stat = sb("stat", [P, 48])
        small = sb("small", [P, 400])
        w_ba = sb("w_ba", [P, KC, 16])
        wba_hi = sb("wba_hi", [P, KC, 16], F32R)
        wba_lo = sb("wba_lo", [P, KC, 16], F32R)
        ident, ones, blockones = mats[:, 0, :], mats[:, 1, :], mats[:, 2, :]
        flip, rot = mats[:, 3, :], mats[:, 4, :]
        cum = [mats[:, 5, :], mats[:, 6, :]]
        eps = stat[:, 0:1]
        eps64 = stat[:, 1:2]
        eps128 = stat[:, 2:3]
        one = stat[:, 3:4]
        ss, lnv, r0 = stat[:, 4:6], stat[:, 6:8], stat[:, 8:10]
        nv, ny, rstd = stat[:, 10:12], stat[:, 12:14], stat[:, 14:16]

        ARENA = 107 * KB
        slab = sb("slab", [P, ARENA // 4])
        at0 = nc.sbuf_base - ARENA

        def at(name, kb, shape, dt=F32):
            n = 4 * int(np.prod(shape[1:]))
            assert kb * KB + n <= ARENA, name
            return nc.alloc_sbuf_tensor_at(name, shape, dt, offset=at0 + int(kb * KB))

        hT_hi = at("hT_hi", 0, [P, NF, L], F32R)
        hT_lo = at("hT_lo", 22, [P, NF, L], F32R)
        sg = at("sg", 44, [P, 2, L])
        hfull = at("hfull", 46, [P, 2, L])
        xn = at("xn", 87, [P, RB, D])
        gconv = at("gconv", 48, [P, 2, L])
        spec = at("spec", 0, [P, 2, 5, HYW])
        filt = at("filt", 20, [P, RB, 4, HYW])
        qkvT = at("qkvT", 20, [P, 12, L])
        zT = at("zT", 32, [P, 4, L])
        hyT = at("hyT", 36, [P, 12, L])
        Ysp = at("Ysp", 36, [P, 4, HYW])
        ytmp = at("ytmp", 44, [P, 2, HYW])
        dft = at("dft", 48, [P, 3840])
        dft_f = dft[:, 0:1536].rearrange("p (r b f) -> p r b f", r=RB, b=6)
        dft_b = dft[:, 1536:2816].rearrange("p (r b f) -> p r b f", r=RB, b=5)
        dft_i = dft[:, 2816:3840].rearrange("p (b t) -> p b t", b=4)
        wfilt = at("wfilt", 63, [HID, 4 * HYW])
        decay = at("decay", 71, [P, RB, HYW])
        hynat = at("hynat", 63, [P, RB, 3, HYW])
        featsT = at("featsT", 99.0, [EMB, L])
        fw = at("fw", 100.0, [HID, 4, HID])
        hdn = at("hdn", 101.0, [HID, L])
        farg = at("farg", 102.0, [HID, 2, L])
        skip = at("skip", 83, [P, 2, HYW])
        zz = at("zz", 103, [P, RB, HYW])
        knat = at("knat", 75, [P, RB, HEADS, P])
        vnat = at("vnat", 79, [P, RB, HEADS, P])
        sq = at("sq", 87, [P, 8, L])
        rr = at("rr", 95, [P, 8, L])
        attnT = at("attnT", 83, [P, 4, 4, P])
        DT = at("DT", 91, [P, 4, 4, P])
        MT = at("MT", 0, [P, 4, 4, P])
        T = at("T", 8, [P, 4, 4, P])
        U = at("U", 36, [P, 4, 4, P])
        Pp = at("Pp", 63, [P, 4, 4, P])
        Mm = at("Mm", 99, [P, 4, 4, P])
        qdecT = at("qdecT", 44, [P, 2, 4, P])
        v1 = at("v1", 16, [P, 2, 4, P])
        kdec = at("kdec", 63, [P, 2, 4, P])
        Sst = at("Sst", 67, [P, 2, 4, P])
        Rr = at("Rr", 71, [P, 2, 4, P])
        v2 = at("v2", 0, [P, 2, 4, P])
        osq = at("osq", 4, [P, 4, L])
        orr = at("orr", 8, [P, 4, L])
        oy = at("oy", 12, [P, 4, L])
        brow = at("brow", 79, [4, HK])
        onehot = at("onehot", 80.5, [BUCKETS, HK])
        gates = at("gates", 0, [P, 24, L])
        qkT = at("qkT", 24, [P, 8, L])
        v_da = at("v_da", 32, [P, RB, DA_W])
        rqk = at("rqk", 36, [P, 4, L])
        rqkr = at("rqkr", 40, [P, 4, L])
        v_ret = at("v_ret", 44, [P, RB, RET_W])
        rg = at("rg", 46, [P, 2, L])
        rgs = at("rgs", 48, [P, 2, L])
        scb = at("scb", 50, [P, 2, L])
        scc = at("scc", 52, [P, 2, L])
        scx = at("scx", 54, [P, 2, L])
        sco = at("sco", 56, [P, 2, L])
        rtmp = at("rtmp", 58, [P, 2, L])
        prob = at("prob", 60, [P, 8, 3 * P])
        aT = at("aT", 72, [P, 4, 3 * P])
        iT = at("iT", 60, [P, 4, 3 * P])
        sq2 = at("sq2", 84, [P, 8, L])
        rr2 = at("rr2", 92, [P, 8, L])
        rotary = at("rotary", 100, [P, 4, L])
        retdecay = at("retdecay", 78, [P, 4, 3 * P])
        yT_hi = at("yT_hi", 60, [P, KC, L], F32R)
        yT_lo = at("yT_lo", 68, [P, KC, L], F32R)
        yacc = at("yacc", 84, [P, KC, L])
        ytm = at("ytm", 92, [P, 2, L])

        psA = psum("psA", [P, 4, 512])
        psB = psum("psB", [P, 4, 512])

        def pair(name, per1, per2, start=0, between=0):
            h = sem(name)
            return (Signal(h, per1, start), Signal(h, per2, start + DEPTH * per1 + between))

        raw_loaded = [pair(f"raw_loaded{i}", H1 // 2 // RAW * 16, H2 // 2 // RAW * 16) for i in range(RAW)]
        hi_done = pair("hi_done", H1, H2)
        lo_done = pair("lo_done", H1, H2, start=2 * RAW)
        half_used = pair("half_used", H1, H2, start=SLOTS)
        x_ready = pair("x_ready", 12, 8, start=16, between=4)
        gain_loaded = pair("gain_loaded", 48, 32, between=16)
        param_loaded = sem("param_loaded")
        const_loaded = sem("const_loaded")
        bias_loaded = sem("bias_loaded")
        bias_mm = sem("bias_mm")
        hankel_loaded = sem("hankel_loaded")
        bias_row = sem("bias_row")
        bias_stored = sem("bias_stored")
        setup = sem("setup")
        out_stored = sem("out_stored")
        n_ss = pair("norm_squares", 6, 4, between=2)
        n_r0 = pair("norm_root", 3, 2, between=1)
        n_xn = pair("norm_scaled", 6, 4, start=1)
        n_tp = pair("norm_turned", 12, 8)
        n_hi = pair("norm_hi", 12, 8)
        n_lo = pair("norm_lo", 12, 8)
        f_conv = pair("ffn_conv", 0, NF)
        f_act = pair("ffn_silu", 2 * NF, NF)
        f_prod = pair("ffn_product", 2 * NF, NF)
        f_hi = pair("ffn_hi", 2 * NF, NF)
        f_lo = pair("ffn_lo", 2 * NF, NF)

        def one_stack(per):
            return {k: Signal(sem(k), n) for k, n in per.items()}

        NPAR1, NPAR2 = 20, 14
        s1 = one_stack(dict(
            cols_tp=1, cols=1, wba=1, mlp_mm=3, mlp_arg=3, mlp_sin=3, filt_mm=8, filt=8, spec_mm=10, spec=10,
            conv=24, qkv_silu=12, z_silu=4, ba_mm=1, hy_turned=6, hy_nat=6,
            z_mm=8, y_spec=4, inv_mm=4, zz=4, hy_ss=2, hy_r0=1, hy_zn=1, hy_back=2, y_hi=5, y_lo=5,
            qk_sq=1, qk_mm=1, qk_root=1, qk_norm=1, kv_turned=4, kv_nat=4,
            g_arg=1, g_exp=1, g_sum=1, g_ln=1, g_ready=1, g_cum=1, g_col=1, g_decays=1, g_neg=1,
            row_mm=4, row_arg=4, row_exp=4, q_exp=2, q_dec=2, kk_mm=1, attn=4, mt=4,
            masked=28, p_mm=28, p_copy=24, tp_mm=24, t_new=24, u_tp=20, u_act=20, u_dve=8,
            v1_mm=2, v1=2, k_dec=2, s_mm=2, s_copy=2, ks_mm=2, rest=2, v2_mm=2, v2=2, o_mm=2,
            o_sq=1, o_ss=1, o_root=1, o_y=1))
        s2 = one_stack(dict(
            cols2_tp=1, cols2=1, lam_sum=1, lam_exp=1, lam=1, ev_act=38, ev_dve=12, rg_sig=2, sc_y=1,
            a_sq=1, a_mm=1, a_root=1, a_qk=1, rot_mm=1, rot=1, sc_mm=8, sc_max=8, sc_exp=8, sc_a=4,
            a_turned=4, a_copy=4, oa_mm=2, oa_sq=1, oa_ss=1, oa_root=1, oa_y=1,
            rs_mm=4, rs_dec=4, or_mm=1, or_sq=1, or_ss=1, or_root=1, or_y=1,
            o_hi=3, o_lo=3, br=24, yb_hi=8, yb_lo=8))

        def chain(name):
            h = sem(name)
            n1, n2, mid = count.get(name, (1, 1, 0))
            return (Chain(h, 0, n1), Chain(h, DEPTH * n1 + mid, n2), Chain(h, DEPTH * n1, 0))

        act_chain, dve_chain = chain("act_chain"), chain("dve_chain")

        def raw_half(s, kind):
            u = raw[:, (s // 2) % RAW, :]
            if kind == "A":
                return u.rearrange("p (c n) -> p c n", c=KC)[:, :, (s % 2) * P:(s % 2 + 1) * P]
            return u[:, (s % 2) * HALF:(s % 2 + 1) * HALF]

        def split_half(t, s, kind):
            v = t[:, s % SLOTS, :]
            return v.rearrange("p (c n) -> p c n", c=KC) if kind == "A" else v

        def product(o, a_hi, a_lo, b_hi, b_lo, start, stop, skip=False):
            nc.tensor.matmul(o, a_lo, b_hi, start=start, stop=False, skip_group_check=skip)
            nc.tensor.matmul(o, a_hi, b_lo, start=False, stop=False, skip_group_check=skip)
            return nc.tensor.matmul(o, a_hi, b_hi, start=False, stop=stop, skip_group_check=skip)

        def layer(ap, l):
            v = ap[bass.ds(l, 1)]
            return v.rearrange("o a -> (o a)") if len(ap.shape) == 2 else v.rearrange("o a b -> (o a) b")

        scratch = nc.dram_tensor("bias_rows", (4, HK), F32, kind="Internal").ap()
        block = ctx.enter_context(nc.Block())

        @block.sync
        def _(sp):
            def unit(l, st, u, src):
                sp.wait_ge(lo_done[st].sem, lo_done[st].due(l, 2 * u + 2 - 2 * RAW))
                dst = raw[:, u % RAW, :].rearrange("p (c n) -> p c n", c=src.shape[1])
                sp.dma_start(dst, src).then_inc(raw_loaded[u % RAW][st].sem, 16)

            def columns(w, l, c0):
                return w[bass.ds(l, 1), :, c0:c0 + 2 * P].rearrange("o (c p) n -> p (o c) n", p=P)

            def two_rows(w, l, r0):
                return w[bass.ds(l, 1), r0:r0 + 2 * P, :].rearrange("o (c p) n -> p (o c) n", p=P)

            def param(dst, src):
                sp.dma_start(dst, src).then_inc(param_loaded, 16)

            def load_gain(st, l, q, w):
                sp.wait_ge(n_xn[st].sem, n_xn[st].due(l, 2 * q))
                sp.dma_start(gain[:, :], layer(w, l).partition_broadcast(P)).then_inc(gain_loaded[st].sem, 16)

            def ffn_units(st, l, u0, wg, wu, wd, up0=0, next_gain=None):
                for j in range(NF // 2):
                    unit(l, st, u0 + 2 * j, columns(wg, l, 2 * P * j))
                    unit(l, st, u0 + 2 * j + 1, columns(wu, l, up0 + 2 * P * j))
                    if next_gain is not None and j == 4:
                        load_gain(st, l, 1, next_gain)
                for j in range(NF // 2):
                    unit(l, st, u0 + NF + j, two_rows(wd, l, 2 * P * j))

            xin = ins["x"].rearrange("o (r p) d -> p (o r) d", p=P)
            sp.dma_start(x[:, :, :], xin).then_inc(x_ready[0].sem, 16)
            sp.dma_start(relb[:, :], ins["rel_bias_2"]).then_inc(bias_loaded, 16)
            sp.dma_start(onehot[:, :], ins["c_onehot"]).then_inc(bias_loaded, 16)
            for dst, src in ((mats[:, :, :], ins["c_mats"]), (masks[:, :, :], ins["c_masks"]),
                             (dft[:, :], ins["c_dft"])):
                sp.dma_start(dst, src).then_inc(const_loaded, 16)
            sp.wait_ge(setup, 1)
            with sp.Fori(0, DEPTH) as l:
                load_gain(0, l, 0, ins["ffn1_norm"])
                param(rows[0:60, :], ins["dn_conv"][bass.ds(l, 1)].rearrange("o k (b p) -> (o k b) p", p=P))
                param(rows[60:96, :], ins["hy_conv"][bass.ds(l, 1)].rearrange("o k (b p) -> (o k b) p", p=P))
                param(rows[96:108, :], layer(ins["hy_conv_bias"], l).rearrange("(b p) -> b p", p=P))
                param(rows[108:109, :], ins["dn_norm"][bass.ds(l, 1)])
                param(rows[109:113, :], layer(ins["hy_norm"], l).rearrange("(b p) -> b p", p=P))
                for n, name in enumerate(("hy_f_b1", "hy_f_b2", "hy_f_b3", "hy_f_freq")):
                    param(rows[113 + n:114 + n, 0:HID], ins[name][bass.ds(l, 1)])
                param(fw[0:EMB, 0, :], layer(ins["hy_f_w1"], l))
                param(fw[:, 1, :], layer(ins["hy_f_w2"], l))
                param(fw[:, 2, :], layer(ins["hy_f_w3"], l))
                param(fw[:, 3, :], layer(ins["hy_f_w2"], l))
                param(featsT[:, :], ins["c_feats"])
                param(wfilt[:, :], layer(ins["hy_f_wout"], l))
                param(decay[:, :, :], ins["c_decay"])
                param(w_ba[:, :, :], ins["w_in"].rearrange("l k n -> (l k) n")[bass.ds(l * D, D), COL_BA:COL_HY]
                      .rearrange("(c p) n -> p c n", p=P))
                param(small[:, 0:8], ins["dn_a_log"][bass.ds(l, 1)].rearrange("o d h -> (o d h)").partition_broadcast(P))
                param(small[:, 8:16], ins["dn_dt_bias"][bass.ds(l, 1)].rearrange("o d h -> (o d h)").partition_broadcast(P))
                param(skip[:, :, :], ins["hy_skip"][bass.ds(l, 1)].rearrange("o a c -> (o a) c").partition_broadcast(P))
                ffn_units(0, l, 0, ins["ffn1_w_gate"], ins["ffn1_w_up"], ins["ffn1_w_down"],
                          next_gain=ins["mix_norm"])
                order = [2 * P * i for i in range(6)] + [COL_HY + 2 * P * i for i in range(6)] \
                    + [3 * DN + 2 * P * i for i in range(2)]
                for i, c0 in enumerate(order):
                    unit(l, 0, 33 + i, columns(ins["w_in"], l, c0))
                    if i == 4:
                        load_gain(0, l, 2, ins["ffn2_norm"])
                for i in range(4):
                    unit(l, 0, 47 + i, two_rows(ins["w_out"], l, 2 * P * i))
                ffn_units(0, l, 51, ins["ffn2_w_gate"], ins["ffn2_w_up"], ins["ffn2_w_down"])
            sp.wait_ge(n_xn[1].sem, n_xn[1].due(0, 0))
            sp.dma_start(gain[:, :], ins["final_norm"].partition_broadcast(P)).then_inc(gain_loaded[0].sem, 16)
            sp.wait_ge(x_ready[1].sem, x_ready[1].due(0, 0))
            sp.dma_start(rotary[:, :, :], ins["c_rotary"]).then_inc(const_loaded, 16)
            sp.dma_start(retdecay[:, :, :], ins["c_retdecay"]).then_inc(const_loaded, 16)
            with sp.Fori(0, DEPTH) as l:
                load_gain(1, l, 0, ins["norm_mix_g_2"])
                for n, name in enumerate(("da_q_norm_g_2", "da_k_norm_g_2", "ret_norm_g_2")):
                    for m in range(2):
                        param(rows[n:n + 1, 64 * m:64 * m + 64], ins[name][bass.ds(l, 1)])
                param(rows[3:4, :], ins["da_subln_g_2"][bass.ds(l, 1)])
                param(rows[4:10, :], ins["sc_conv_w_2"][bass.ds(l, 1)].rearrange("o k (b p) -> (o k b) p", p=P))
                param(rows[10:12, :], layer(ins["sc_conv_b_2"], l).rearrange("(b p) -> b p", p=P))
                param(rows[12:36, :], layer(ins["b_gate_2"], l).rearrange("(b p) -> b p", p=P))
                param(rows[36:102, :], ins["ffn_conv_w_2"][bass.ds(l, 1)].rearrange("o k (b p) -> (o k b) p", p=P))
                param(rows[102:124, :], layer(ins["ffn_conv_b_2"], l).rearrange("(b p) -> b p", p=P))
                param(small[:, 0:256], ins["da_lambda_2"][bass.ds(l, 1)].rearrange("o a d -> (o a d)").partition_broadcast(P))
                for i in range(25):
                    unit(l, 1, i, columns(ins["w_in_2"], l, 2 * P * i))
                    if i == 0:
                        param(stat[:, 24:26], layer(ins["c_lam"], l).partition_broadcast(P))
                    if i == 6:
                        load_gain(1, l, 1, ins["norm_ffn_g_2"])
                for i in range(2):
                    unit(l, 1, 25 + i, two_rows(ins["w_branch_da_2"], l, 2 * P * i))
                unit(l, 1, 27, two_rows(ins["w_branch_ret_2"], l, 0))
                unit(l, 1, 28, two_rows(ins["w_branch_sc_2"], l, 0))
                for i in range(4):
                    unit(l, 1, 29 + i, two_rows(ins["w_out_2"], l, 2 * P * i))
                ffn_units(1, l, 33, ins["w_ffn_in_2"], ins["w_ffn_in_2"], ins["w_ffn_out_2"], up0=FF)
            sp.wait_ge(x_ready[1].sem, x_ready[1].due(DEPTH - 1, 8))
            sp.dma_start(out.rearrange("o (r p) d -> p (o r) d", p=P), x[:, :, :]).then_inc(out_stored, 16)
            sp.wait_ge(out_stored, 16)

        @block.scalar
        def _(act):
            A = nc.scalar.activation

            def round_half(st, l, n):
                kinds = (KIND1, KIND2)[st]
                if n >= len(kinds):
                    return
                if n % 2 == 0:
                    arrived = raw_loaded[n // 2 % RAW][st]
                    act.wait_ge(arrived.sem, arrived.due(l, 16 * (n // 2 // RAW + 1)))
                act.wait_ge(half_used[st].sem, half_used[st].due(l, n + 1 - SLOTS))
                A(split_half(w_hi, n, kinds[n]), raw_half(n, kinds[n]), ACT.Copy).then_inc(hi_done[st].sem, 1)

            def root(l, ch, dst, src, scale, bias):
                A(dst, src, ACT.Ln, scale=scale, bias=bias).then_inc(ch.sem, 1)
                act.wait_ge(ch.sem, ch.step(l))
                return A(dst, dst, ACT.Exp, scale=-0.5)

            def norm_stats(st, l, q, x0):
                for rb in range(RB):
                    act.wait_ge(x_ready[st].sem, x_ready[st].due(l, 0 if x0 < 0 else x0 + 2 * (rb + 1)))
                    A(xn[:, rb, :], x[:, rb, :], ACT.Square, accum_out=ss[:, rb:rb + 1]).then_inc(n_ss[st].sem, 1)
                act.wait_ge(n_ss[st].sem, n_ss[st].due(l, 2 * q + 2))
                ch = act_chain[st]
                A(lnv, ss, ACT.Ln, scale=1.0 / D, bias=eps).then_inc(ch.sem, 1)
                act.wait_ge(ch.sem, ch.step(l))
                A(r0, lnv, ACT.Exp, scale=-0.5).then_inc(n_r0[st].sem, 1)

            def norm_out(st, l, q):
                for i in range(4):
                    act.wait_ge(n_tp[st].sem, n_tp[st].due(l, 4 * q + i + 1))
                    A(xT_hi[:, 2 * i:2 * i + 2, :], psA[:, i, :].rearrange("p (c n) -> p c n", c=2),
                      ACT.Copy).then_inc(n_hi[st].sem, 1)

            def ffn(st, l, f, s0):
                for j in range(NF // 2):
                    for i in range(2):
                        n = 2 * j + i
                        round_half(st, l, s0 + 4 * j + i + AHEAD)
                        if st == 0:
                            act.wait_ge(half_used[st].sem, half_used[st].due(l, s0 + 4 * j + i + 1))
                            A(sg[:, i, :], psA[:, i, 0:L], ACT.Silu).then_inc(f_act[st].sem, 1)
                        else:
                            act.wait_ge(f_conv[st].sem, f_conv[st].due(l, NF * f + n + 1))
                            A(sg[:, i, :], gconv[:, i, :], ACT.Silu).then_inc(f_act[st].sem, 1)
                    for i in range(2):
                        n = 2 * j + i
                        round_half(st, l, s0 + 4 * j + 2 + i + AHEAD)
                        act.wait_ge(f_prod[st].sem, f_prod[st].due(l, NF * f + n + 1))
                        A(hT_hi[:, n, :], hfull[:, i, :], ACT.Copy).then_inc(f_hi[st].sem, 1)
                    if st == 0 and f == 0 and j in (2, 4, 6):
                        mlp_sin(l, j // 2 - 1)
                for k in range(NF):
                    round_half(st, l, s0 + 2 * NF + k + AHEAD)

            def mlp_sin(l, k):
                act.wait_ge(s1["mlp_arg"].sem, s1["mlp_arg"].due(l, k + 1))
                A(hdn[:, :], farg[:, 0, :], ACT.Sin).then_inc(s1["mlp_sin"].sem, 1)

            def stack1_mixer(l):
                ch = act_chain[0]
                g = lambda a, b: small[:, a:b]
                for k in range(10):
                    act.wait_ge(s1["spec_mm"].sem, s1["spec_mm"].due(l, k + 1))
                    A(spec[:, k // 5, k % 5, :], psA[:, k % 4, :], ACT.Copy).then_inc(s1["spec"].sem, 1)
                norm_out(0, l, 1)
                for i in range(28):
                    round_half(0, l, 66 + i + AHEAD)
                    if i < 12:
                        act.wait_ge(s1["conv"].sem, s1["conv"].due(l, i + 1))
                        A(qkvT[:, i, :], qkvT[:, i, :], ACT.Silu).then_inc(s1["qkv_silu"].sem, 1)
                    if i >= 24:
                        act.wait_ge(half_used[0].sem, half_used[0].due(l, 66 + i + 1))
                        A(zT[:, i - 24, :], psA[:, i % 4, 0:L], ACT.Silu).then_inc(s1["z_silu"].sem, 1)
                for k in range(6):
                    act.wait_ge(s1["hy_turned"].sem, s1["hy_turned"].due(l, k + 1))
                    A(hynat[:, k % 2, k // 2, :], psB[:, 1 + k % 3, :], ACT.Copy).then_inc(s1["hy_nat"].sem, 1)
                for rb in range(RB):
                    act.wait_ge(s1["zz"].sem, s1["zz"].due(l, 2 + rb + 1))
                    A(ytmp[:, rb, :], zz[:, rb, :], ACT.Square, accum_out=g(288 + rb, 289 + rb)).then_inc(s1["hy_ss"].sem, 1)
                act.wait_ge(s1["hy_ss"].sem, s1["hy_ss"].due(l, 2))
                root(l, ch, g(290, 292), g(288, 290), 1.0 / HYW, eps).then_inc(s1["hy_r0"].sem, 1)
                for b in range(4):
                    if b % 2 == 0:
                        act.wait_ge(s1["hy_back"].sem, s1["hy_back"].due(l, b // 2 + 1))
                    A(xT_hi[:, 4 + b, :], psA[:, b // 2, (b % 2) * L:(b % 2 + 1) * L], ACT.Copy,
                      scale=cols[:, 109 + b:110 + b]).then_inc(s1["y_hi"].sem, 1)
                act.wait_ge(s1["qkv_silu"].sem, s1["qkv_silu"].due(l, 12))
                A(sq[:, :, :], qkvT[:, 0:8, :], ACT.Square).then_inc(s1["qk_sq"].sem, 1)
                act.wait_ge(s1["g_arg"].sem, s1["g_arg"].due(l, 1))
                A(g(168, 184).rearrange("p (r n) -> p r n", r=RB),
                  psB[:, 0, 0:32].rearrange("p (r n) -> p r n", r=RB)[:, :, 0:8], ACT.Exp, scale=-1.0)
                A(g(48, 64), g(32, 48), ACT.Exp, scale=-1.0)
                A(g(280, 288), g(0, 8), ACT.Exp).then_inc(s1["g_exp"].sem, 1)
                act.wait_ge(s1["g_sum"].sem, s1["g_sum"].due(l, 1))
                A(g(80, 96), g(64, 80), ACT.Ln).then_inc(s1["g_ln"].sem, 1)
                act.wait_ge(s1["qk_mm"].sem, s1["qk_mm"].due(l, 1))
                A(rr[:, 0:4, :], psA[:, 0:2, :].rearrange("p a (b n) -> p (a b) n", b=2), ACT.Ln, scale=float(P), bias=eps128)
                A(rr[:, 4:8, :], psA[:, 2:4, :].rearrange("p a (b n) -> p (a b) n", b=2), ACT.Ln, bias=eps).then_inc(ch.sem, 1)
                act.wait_ge(ch.sem, ch.step(l))
                A(rr[:, :, :], rr[:, :, :], ACT.Exp, scale=-0.5).then_inc(s1["qk_root"].sem, 1)
                for k in range(4):
                    act.wait_ge(s1["kv_turned"].sem, s1["kv_turned"].due(l, k + 1))
                    dst = (knat, vnat)[k // 2]
                    A(dst[:, k % 2, :, :], psB[:, k, :].rearrange("p (h n) -> p h n", h=4), ACT.Copy).then_inc(s1["kv_nat"].sem, 1)
                act.wait_ge(s1["g_decays"].sem, s1["g_decays"].due(l, 1))
                A(g(232, 248), g(216, 232), ACT.Exp)
                A(g(248, 264), g(200, 216), ACT.Exp).then_inc(s1["g_col"].sem, 1)
                for d in range(DIRS):
                    c1 = 1 - d
                    act.wait_ge(s1["row_arg"].sem, s1["row_arg"].due(l, 2 * d + c1 + 1))
                    A(qdecT[:, d, :, :], psA[:, 2 * d + c1, :].rearrange("p (h n) -> p h n", h=4), ACT.Exp).then_inc(s1["q_exp"].sem, 1)
                for k in range(4):
                    act.wait_ge(s1["row_arg"].sem, s1["row_arg"].due(l, k + 1))
                    A(DT[:, k, :, :], DT[:, k, :, :], ACT.Exp).then_inc(s1["row_exp"].sem, 1)
                for b in range(1, LEVELS):
                    for k in range(4):
                        act.wait_ge(s1["p_mm"].sem, s1["p_mm"].due(l, 4 * b + k + 1))
                        A(Pp[:, k, :, :], psA[:, k, :].rearrange("p (h n) -> p h n", h=4), ACT.Copy).then_inc(s1["p_copy"].sem, 1)
                    if b < LEVELS - 1:
                        for k in range(4):
                            act.wait_ge(s1["u_tp"].sem, s1["u_tp"].due(l, 4 * (b - 1) + k + 1))
                            A(U[:, k, :, :], psA[:, k, :].rearrange("p (h n) -> p h n", h=4), ACT.Copy).then_inc(s1["u_act"].sem, 1)
                for d in range(DIRS):
                    act.wait_ge(s1["s_mm"].sem, s1["s_mm"].due(l, d + 1))
                    A(Sst[:, d, :, :], psA[:, 2 + d, :].rearrange("p (h n) -> p h n", h=4), ACT.Copy).then_inc(s1["s_copy"].sem, 1)
                act.wait_ge(s1["o_mm"].sem, s1["o_mm"].due(l, 2))
                oT = psA[:, 0:2, :].rearrange("p a (b n) -> p (a b) n", b=2)
                A(osq[:, :, :], oT, ACT.Square).then_inc(s1["o_sq"].sem, 1)
                act.wait_ge(s1["o_ss"].sem, s1["o_ss"].due(l, 1))
                root(l, ch, orr[:, :, :], psB[:, 0:2, :].rearrange("p a (b n) -> p (a b) n", b=2), 1.0 / P, eps).then_inc(s1["o_root"].sem, 1)
                act.wait_ge(s1["o_y"].sem, s1["o_y"].due(l, 1))
                A(xT_hi[:, 0:4, :], oy[:, :, :], ACT.Copy).then_inc(s1["y_hi"].sem, 1)
                for k in range(8):
                    round_half(0, l, 94 + k + AHEAD)

            def stack2_mixer(l):
                ch = act_chain[1]
                g = lambda a, b: small[:, a:b]
                act.wait_ge(s2["lam_sum"].sem, s2["lam_sum"].due(l, 1))
                A(stat[:, 28:30], stat[:, 26:28], ACT.Exp).then_inc(s2["lam_exp"].sem, 1)
                act.wait_ge(s2["cols2"].sem, s2["cols2"].due(l, 1))
                for i in range(50):
                    round_half(1, l, i + AHEAD)
                    ps = psA[:, i % 4, 0:L]
                    done = s2["ev_act"].sem
                    if i < 8:
                        act.wait_ge(half_used[1].sem, half_used[1].due(l, i + 1))
                        A(qkT[:, i, :], ps, ACT.Copy).then_inc(done, 1)
                    elif 12 <= i < 16:
                        act.wait_ge(half_used[1].sem, half_used[1].due(l, i + 1))
                        A(rqk[:, i - 12, :], ps, ACT.Copy).then_inc(done, 1)
                    elif 18 <= i < 20:
                        act.wait_ge(half_used[1].sem, half_used[1].due(l, i + 1))
                        A(rgs[:, i - 18, :], ps, ACT.Sigmoid).then_inc(s2["rg_sig"].sem, 1)
                    elif 22 <= i < 24:
                        act.wait_ge(half_used[1].sem, half_used[1].due(l, i + 1))
                        A(scc[:, i - 22, :], ps, ACT.Copy).then_inc(done, 1)
                    elif i >= 26:
                        act.wait_ge(half_used[1].sem, half_used[1].due(l, i + 1))
                        A(gates[:, i - 26, :], ps, ACT.Sigmoid, bias=cols[:, 12 + i - 26:13 + i - 26]).then_inc(done, 1)
                act.wait_ge(s2["ev_act"].sem, s2["ev_act"].due(l, 38))
                A(sq2[:, :, :], qkT[:, :, :], ACT.Square).then_inc(s2["a_sq"].sem, 1)
                act.wait_ge(s2["a_mm"].sem, s2["a_mm"].due(l, 1))
                A(rr2[:, 0:4, :], psB[:, 0:2, :].rearrange("p a (b n) -> p (a b) n", b=2), ACT.Ln, bias=eps64)
                A(rr2[:, 4:8, :], psB[:, 2:4, :].rearrange("p a (b n) -> p (a b) n", b=2), ACT.Ln, scale=1.0 / 64, bias=eps).then_inc(ch.sem, 1)
                act.wait_ge(ch.sem, ch.step(l))
                A(rr2[:, :, :], rr2[:, :, :], ACT.Exp, scale=-0.5).then_inc(s2["a_root"].sem, 1)
                for k in range(8):
                    ps = (psA, psB)[k % 2][:, k // 2, :]
                    act.wait_ge(s2["sc_max"].sem, s2["sc_max"].due(l, k + 1))
                    A(prob[:, k, 0:L], ps[:, 0:L], ACT.Exp, bias=g(320 + 2 * k, 321 + 2 * k), accum_out=g(336 + 2 * k, 337 + 2 * k))
                    A(prob[:, k, L:3 * P], ps[:, L:3 * P], ACT.Exp, bias=g(321 + 2 * k, 322 + 2 * k),
                      accum_out=g(337 + 2 * k, 338 + 2 * k)).then_inc(s2["sc_exp"].sem, 1)
                for h in range(4):
                    act.wait_ge(s2["a_turned"].sem, s2["a_turned"].due(l, h + 1))
                    A(aT[:, h, :], psA[:, h, 0:3 * P], ACT.Copy).then_inc(s2["a_copy"].sem, 1)
                act.wait_ge(s2["oa_mm"].sem, s2["oa_mm"].due(l, 2))
                A(sq2[:, 0:4, :], psB[:, 0:2, :].rearrange("p a (b n) -> p (a b) n", b=2), ACT.Square).then_inc(s2["oa_sq"].sem, 1)
                act.wait_ge(s2["oa_ss"].sem, s2["oa_ss"].due(l, 1))
                root(l, ch, rr2[:, 0:4, :], psB[:, 2:4, :].rearrange("p a (b n) -> p (a b) n", b=2), 1.0 / P, eps).then_inc(s2["oa_root"].sem, 1)
                act.wait_ge(s2["sc_y"].sem, s2["sc_y"].due(l, 1))
                A(xT_hi[:, 6:8, :], sco[:, :, :], ACT.Copy).then_inc(s2["o_hi"].sem, 1)
                act.wait_ge(s2["oa_y"].sem, s2["oa_y"].due(l, 1))
                A(xT_hi[:, 0:4, :], rr2[:, 0:4, :], ACT.Copy).then_inc(s2["o_hi"].sem, 1)
                act.wait_ge(s2["or_mm"].sem, s2["or_mm"].due(l, 1))
                A(sq2[:, 4:6, :], psA[:, 0, :].rearrange("p (b n) -> p b n", b=2), ACT.Square).then_inc(s2["or_sq"].sem, 1)
                act.wait_ge(s2["or_ss"].sem, s2["or_ss"].due(l, 1))
                root(l, ch, rr2[:, 4:6, :], psA[:, 1, :].rearrange("p (b n) -> p b n", b=2), 1.0 / 64, eps).then_inc(s2["or_root"].sem, 1)
                act.wait_ge(s2["or_y"].sem, s2["or_y"].due(l, 1))
                A(xT_hi[:, 4:6, :], rr2[:, 4:6, :], ACT.Copy).then_inc(s2["o_hi"].sem, 1)
                for k in range(8):
                    round_half(1, l, 50 + k + AHEAD)
                for n in range(KC):
                    act.wait_ge(s2["br"].sem, s2["br"].due(l, 16 + n + 1))
                    A(yT_hi[:, n, :], yacc[:, n, :], ACT.Copy).then_inc(s2["yb_hi"].sem, 1)
                for k in range(8):
                    round_half(1, l, 58 + k + AHEAD)

            act.wait_ge(setup, 1)
            with act.Fori(0, DEPTH) as l:
                for n in range(AHEAD):
                    round_half(0, l, n)
                norm_stats(0, l, 0, -4)
                norm_out(0, l, 0)
                ffn(0, l, 0, 0)
                norm_stats(0, l, 1, 0)
                stack1_mixer(l)
                norm_stats(0, l, 2, 4)
                norm_out(0, l, 2)
                ffn(0, l, 1, 102)
            steps["act_chain"] = [act_chain[0].n, 0, 1]
            for rb in range(RB):
                act.wait_ge(x_ready[0].sem, x_ready[0].due(DEPTH - 1, 8 + 2 * (rb + 1)))
                A(xn[:, rb, :], x[:, rb, :], ACT.Square, accum_out=ss[:, rb:rb + 1]).then_inc(n_ss[0].sem, 1)
            act.wait_ge(n_ss[0].sem, n_ss[0].due(DEPTH, 2))
            A(lnv, ss, ACT.Ln, scale=1.0 / D, bias=eps).then_inc(act_chain[2].sem, 1)
            act.wait_ge(act_chain[2].sem, act_chain[2].step(0))
            A(r0, lnv, ACT.Exp, scale=-0.5).then_inc(n_r0[0].sem, 1)
            with act.Fori(0, DEPTH) as l:
                for n in range(AHEAD):
                    round_half(1, l, n)
                norm_stats(1, l, 0, -4)
                norm_out(1, l, 0)
                stack2_mixer(l)
                norm_stats(1, l, 1, 0)
                norm_out(1, l, 1)
                ffn(1, l, 0, 66)
            steps["act_chain"][1] = act_chain[1].n

        @block.gpsimd
        def _(pool):
            pool.sem_inc(lo_done[0].sem, 2 * RAW)
            pool.wait_ge(bias_row, 1)
            pool.dma_start(scratch, brow[:, :]).then_inc(bias_stored, 16)
            pool.wait_ge(bias_stored, 16)
            pool.dma_start(hankel[:, :, :], bass.AP(scratch.tensor, 0, [[1, P], [HK, 4], [1, L]])).then_inc(hankel_loaded, 16)
            for st, kinds in ((0, KIND1), (1, KIND2)):
                with pool.Fori(0, DEPTH) as l:
                    for n, kind in enumerate(kinds):
                        pool.wait_ge(hi_done[st].sem, hi_done[st].due(l, n + 1))
                        nc.gpsimd.tensor_tensor(split_half(w_lo, n, kind), raw_half(n, kind),
                                                split_half(w_hi, n, kind).bitcast(F32), ALU.subtract)\
                            .then_inc(lo_done[st].sem, 1)

        @block.vector
        def _(dve):
            V = nc.vector

            def newton(l, ch, dst, mean, first, scale, n):
                V.tensor_scalar(nv[:, 0:n], mean, scale, EPS, ALU.mult, ALU.add).then_inc(ch.sem, 1)
                dve.wait_ge(ch.sem, ch.step(l))
                V.tensor_tensor(ny[:, 0:n], first, first, ALU.mult).then_inc(ch.sem, 1)
                dve.wait_ge(ch.sem, ch.step(l))
                V.tensor_tensor(ny[:, 0:n], ny[:, 0:n], nv[:, 0:n], ALU.mult).then_inc(ch.sem, 1)
                dve.wait_ge(ch.sem, ch.step(l))
                V.tensor_scalar(ny[:, 0:n], ny[:, 0:n], -0.5, 1.5, ALU.mult, ALU.add).then_inc(ch.sem, 1)
                dve.wait_ge(ch.sem, ch.step(l))
                V.tensor_tensor(dst, first, ny[:, 0:n], ALU.mult).then_inc(ch.sem, 1)
                dve.wait_ge(ch.sem, ch.step(l))

            def norm_scale(st, l, q):
                dve.wait_ge(n_r0[st].sem, n_r0[st].due(l, q + 1))
                newton(l, dve_chain[st], rstd, ss, r0, 1.0 / D, RB)
                dve.wait_ge(gain_loaded[st].sem, gain_loaded[st].due(l, 16 * (q + 1)))
                for rb in range(RB):
                    V.scalar_tensor_tensor(xn[:, rb, :], x[:, rb, :], rstd[:, rb:rb + 1], gain[:, :],
                                           ALU.mult, ALU.mult).then_inc(n_xn[st].sem, 1)

            def norm_rest(st, l, q):
                for i in range(4):
                    dve.wait_ge(n_hi[st].sem, n_hi[st].due(l, 4 * q + i + 1))
                    v = xT_hi[:, 2 * i:2 * i + 2, :].bitcast(F32)
                    V.tensor_tensor(xT_lo[:, 2 * i:2 * i + 2, :], psA[:, i, :].rearrange("p (c n) -> p c n", c=2), v,
                                    ALU.subtract).then_inc(n_lo[st].sem, 1)

            def add_to_x(st, l, s, scale):
                dve.wait_ge(half_used[st].sem, half_used[st].due(l, s + 1))
                for rb in range(RB):
                    for c in range(2):
                        v = x[:, rb, c * 512:(c + 1) * 512]
                        V.scalar_tensor_tensor(v, psB[:, 2 * rb + c, :], scale, v, ALU.mult, ALU.add)\
                            .then_inc(x_ready[st].sem, 1)

            def ffn(st, l, f, s0):
                ch = dve_chain[st]

                def convolve(n, i):
                    dve.wait_ge(half_used[st].sem, half_used[st].due(l, s0 + 4 * (n // 2) + i + 1))
                    ps, o = psA[:, i, 0:L], gconv[:, i, :]
                    c = lambda k: cols[:, 36 + k * NF + n:37 + k * NF + n]
                    V.tensor_scalar(o, ps, c(2), cols[:, 102 + n:103 + n], ALU.mult, ALU.add).then_inc(ch.sem, 1)
                    dve.wait_ge(ch.sem, ch.step(l))
                    V.scalar_tensor_tensor(o[:, 1:L], ps[:, 0:L - 1], c(1), o[:, 1:L], ALU.mult, ALU.add).then_inc(ch.sem, 1)
                    dve.wait_ge(ch.sem, ch.step(l))
                    V.scalar_tensor_tensor(o[:, 2:L], ps[:, 0:L - 2], c(0), o[:, 2:L], ALU.mult, ALU.add)\
                        .then_inc(f_conv[st].sem, 1)

                for j in range(NF // 2):
                    if st == 1:
                        for i in range(2):
                            convolve(2 * j + i, i)
                    for i in range(2):
                        n = 2 * j + i
                        dve.wait_ge(half_used[st].sem, half_used[st].due(l, s0 + 4 * j + 2 + i + 1))
                        dve.wait_ge(f_act[st].sem, f_act[st].due(l, NF * f + n + 1))
                        if n >= 2:
                            dve.wait_ge(f_lo[st].sem, f_lo[st].due(l, NF * f + n - 1))
                        V.tensor_tensor(hfull[:, i, :], sg[:, i, :], psA[:, 2 + i, 0:L], ALU.mult).then_inc(f_prod[st].sem, 1)
                    for i in range(2):
                        n = 2 * j + i
                        dve.wait_ge(f_hi[st].sem, f_hi[st].due(l, NF * f + n + 1))
                        V.tensor_tensor(hT_lo[:, n, :], hfull[:, i, :], hT_hi[:, n, :].bitcast(F32), ALU.subtract)\
                            .then_inc(f_lo[st].sem, 1)
                    if st == 0 and f == 0:
                        if j == 0:
                            columns_of_rows(l)
                        if j in (2, 4, 6):
                            mlp_argument(l, j // 2 - 1)

            def columns_of_rows(l):
                dve.wait_ge(s1["cols_tp"].sem, s1["cols_tp"].due(l, 1))
                V.tensor_copy(cols[:, 0:117], psB[:, 2, 0:117]).then_inc(s1["cols"].sem, 1)

            def mlp_argument(l, k):
                ch = dve_chain[0]
                dve.wait_ge(s1["mlp_mm"].sem, s1["mlp_mm"].due(l, k + 1))
                a, n = farg[:, 0, :], farg[:, 1, :]
                big = 12582912.0
                c1 = 6.28125
                c2 = float(np.float32(np.round((2 * math.pi - c1) * 2 ** 20) / 2 ** 20))
                c3 = float(np.float32(2 * math.pi - c1 - c2))
                V.tensor_scalar(a, psB[0:HID, 3, 0:L], cols[0:HID, 113 + k:114 + k],
                                                cols[0:HID, 116:117], ALU.add, ALU.mult).then_inc(ch.sem, 1)
                dve.wait_ge(ch.sem, ch.step(l))
                V.tensor_scalar(n, a, 1 / (2 * math.pi), big, ALU.mult, ALU.add).then_inc(ch.sem, 1)
                dve.wait_ge(ch.sem, ch.step(l))
                V.tensor_scalar(n, n, big, None, ALU.subtract).then_inc(ch.sem, 1)
                dve.wait_ge(ch.sem, ch.step(l))
                for c in (c1, c2, c3):
                    V.scalar_tensor_tensor(a, n, -c, a, ALU.mult, ALU.add).then_inc(ch.sem, 1)
                    dve.wait_ge(ch.sem, ch.step(l))
                pi = float(np.nextafter(np.float32(math.pi), np.float32(0)))
                V.tensor_scalar(a, a, pi, -pi, ALU.min, ALU.max).then_inc(s1["mlp_arg"].sem, 1)

            def filters(l):
                for k in range(8):
                    dve.wait_ge(s1["filt_mm"].sem, s1["filt_mm"].due(l, k + 1))
                    V.tensor_tensor(filt[:, k // 4, k % 4, :], psA[:, k % 4, :], decay[:, k // 4, :], ALU.mult)\
                        .then_inc(s1["filt"].sem, 1)

            def stack1_projections(l):
                ch = dve_chain[0]
                for i in range(24):
                    dve.wait_ge(half_used[0].sem, half_used[0].due(l, 66 + i + 1))
                    ps = psA[:, i % 4, 0:L]
                    if i < 12:
                        o = qkvT[:, i, :]
                        w = [cols[:, k * 12 + i:k * 12 + i + 1] for k in range(CONV1)]
                        V.tensor_scalar(o, ps, w[2], None, ALU.mult).then_inc(ch.sem, 1)
                        dve.wait_ge(ch.sem, ch.step(l))
                    else:
                        b = i - 12
                        o = hyT[:, b, :]
                        w = [cols[:, 60 + k * 12 + b:61 + k * 12 + b] for k in range(CONV_HY)]
                        V.tensor_scalar(o, ps, w[1], cols[:, 96 + b:97 + b], ALU.mult, ALU.add).then_inc(ch.sem, 1)
                        dve.wait_ge(ch.sem, ch.step(l))
                    taps = [k - len(w) // 2 for k in range(len(w)) if k != len(w) // 2]
                    for t in taps:
                        a, z = max(0, -t), L - max(0, t)
                        ins_ = V.scalar_tensor_tensor(o[:, a:z], ps[:, a + t:z + t], w[t + len(w) // 2], o[:, a:z],
                                                      ALU.mult, ALU.add)
                        if t == taps[-1]:
                            ins_.then_inc(s1["conv"].sem, 1)
                        else:
                            ins_.then_inc(ch.sem, 1)
                            dve.wait_ge(ch.sem, ch.step(l))

            def hyena(l):
                ch = dve_chain[0]
                for o in range(2):
                    src = (hynat[:, :, 0, :], zz[:, :, :])[o]
                    for b in range(2):
                        k_re, k_im = spec[:, o, b, :], spec[:, o, 2 + b, :]
                        k_re2 = spec[:, o, 4 if b == 0 else 1, :]
                        if b == 0:
                            dve.wait_ge(s1["z_mm"].sem, s1["z_mm"].due(l, 4 * o + 4))
                            if o:
                                dve.wait_ge(s1["inv_mm"].sem, s1["inv_mm"].due(l, 2))
                        z_re, z_im = psA[:, b, :], psA[:, 2 + b, :]
                        V.tensor_tensor(ytmp[:, 0, :], z_im, k_im, ALU.mult).then_inc(ch.sem, 1)
                        dve.wait_ge(ch.sem, ch.step(l))
                        V.tensor_tensor(Ysp[:, b, :], z_re, k_re, ALU.mult).then_inc(ch.sem, 1)
                        dve.wait_ge(ch.sem, ch.step(l))
                        V.tensor_tensor(Ysp[:, b, :], Ysp[:, b, :], ytmp[:, 0, :], ALU.subtract)
                        V.tensor_tensor(ytmp[:, 1, :], z_im, k_re2, ALU.mult).then_inc(ch.sem, 1)
                        dve.wait_ge(ch.sem, ch.step(l))
                        V.tensor_tensor(Ysp[:, 2 + b, :], z_re, k_im, ALU.mult).then_inc(ch.sem, 1)
                        dve.wait_ge(ch.sem, ch.step(l))
                        V.tensor_tensor(Ysp[:, 2 + b, :], Ysp[:, 2 + b, :], ytmp[:, 1, :], ALU.add).then_inc(s1["y_spec"].sem, 1)
                    for rb in range(RB):
                        V.tensor_tensor(ytmp[:, rb, :], src[:, rb, :], skip[:, o, :], ALU.mult).then_inc(ch.sem, 1)
                        dve.wait_ge(ch.sem, ch.step(l))
                        dve.wait_ge(s1["inv_mm"].sem, s1["inv_mm"].due(l, 2 * o + rb + 1))
                        V.tensor_tensor(ytmp[:, rb, :], ytmp[:, rb, :], psB[:, 1 + rb, :], ALU.add).then_inc(ch.sem, 1)
                        dve.wait_ge(ch.sem, ch.step(l))
                        V.tensor_tensor(zz[:, rb, :], ytmp[:, rb, :], hynat[:, rb, 1 + o, :], ALU.mult).then_inc(s1["zz"].sem, 1)
                dve.wait_ge(s1["hy_r0"].sem, s1["hy_r0"].due(l, 1))
                newton(l, ch, small[:, 292:294], small[:, 288:290], small[:, 290:292], 1.0 / HYW, RB)
                for rb in range(RB):
                    ins_ = V.tensor_scalar(zz[:, rb, :], zz[:, rb, :], small[:, 292 + rb:293 + rb], None, ALU.mult)
                ins_.then_inc(s1["hy_zn"].sem, 1)
                for b in range(4):
                    dve.wait_ge(s1["y_hi"].sem, s1["y_hi"].due(l, b // 2 * 2 + 2))
                    V.scalar_tensor_tensor(xT_lo[:, 4 + b, :], psA[:, b // 2, (b % 2) * L:(b % 2 + 1) * L],
                                           cols[:, 109 + b:110 + b], xT_hi[:, 4 + b, :].bitcast(F32),
                                           ALU.mult, ALU.subtract).then_inc(s1["y_lo"].sem, 1)

            def deltanet(l):
                ch = dve_chain[0]
                g = lambda a, b: small[:, a:b]
                ba = psB[:, 0, 0:32].rearrange("p (r n) -> p r n", r=RB)
                dve.wait_ge(s1["ba_mm"].sem, s1["ba_mm"].due(l, 1))
                for rb in range(RB):
                    V.tensor_tensor(g(16 + 8 * rb, 24 + 8 * rb), ba[:, rb, 8:16], g(8, 16), ALU.add).then_inc(ch.sem, 1)
                    dve.wait_ge(ch.sem, ch.step(l))
                V.scalar_tensor_tensor(g(32, 48), g(16, 32), -1.0, g(16, 32), ALU.mult, ALU.max).then_inc(s1["g_arg"].sem, 1)
                dve.wait_ge(s1["g_exp"].sem, s1["g_exp"].due(l, 1))
                V.tensor_scalar(g(64, 80), g(48, 64), 1.0, None, ALU.add).then_inc(s1["g_sum"].sem, 1)
                dve.wait_ge(s1["g_sum"].sem, s1["g_sum"].due(l, 1))
                V.tensor_scalar(g(96, 112), g(64, 80), 1.0, None, ALU.subtract).then_inc(ch.sem, 1)
                dve.wait_ge(ch.sem, ch.step(l))
                V.tensor_tensor(g(96, 112), g(48, 64), g(96, 112), ALU.subtract).then_inc(ch.sem, 1)
                dve.wait_ge(ch.sem, ch.step(l))
                V.reciprocal(g(112, 128), g(64, 80)).then_inc(ch.sem, 1)
                dve.wait_ge(ch.sem, ch.step(l))
                V.tensor_tensor(g(128, 144), g(96, 112), g(112, 128), ALU.mult).then_inc(ch.sem, 1)
                dve.wait_ge(ch.sem, ch.step(l))
                dve.wait_ge(s1["g_ln"].sem, s1["g_ln"].due(l, 1))
                V.tensor_tensor(g(128, 144), g(128, 144), g(80, 96), ALU.add).then_inc(ch.sem, 1)
                dve.wait_ge(ch.sem, ch.step(l))
                V.scalar_tensor_tensor(g(128, 144), g(16, 32), 0.0, g(128, 144), ALU.max, ALU.add).then_inc(ch.sem, 1)
                dve.wait_ge(ch.sem, ch.step(l))
                for rb in range(RB):
                    V.scalar_tensor_tensor(g(152 + 8 * rb, 160 + 8 * rb), g(280, 288), -1.0,
                                                           g(128 + 8 * rb, 136 + 8 * rb), ALU.mult, ALU.mult).then_inc(ch.sem, 1)
                    dve.wait_ge(ch.sem, ch.step(l))
                V.tensor_scalar(g(168, 184), g(168, 184), 1.0, None, ALU.add).then_inc(ch.sem, 1)
                dve.wait_ge(ch.sem, ch.step(l))
                V.reciprocal(g(184, 200), g(168, 184)).then_inc(s1["g_ready"].sem, 1)
                dve.wait_ge(s1["qk_root"].sem, s1["qk_root"].due(l, 1))
                V.tensor_tensor(qkvT[:, 0:8, :], qkvT[:, 0:8, :], rr[:, :, :], ALU.mult).then_inc(s1["qk_norm"].sem, 1)
                dve.wait_ge(s1["g_cum"].sem, s1["g_cum"].due(l, 1))
                V.tensor_copy(g(200, 216), psB[:, 0, 0:16]).then_inc(ch.sem, 1)
                dve.wait_ge(ch.sem, ch.step(l))
                V.tensor_tensor(g(216, 232), psB[:, 0, 16:32], g(200, 216), ALU.subtract).then_inc(s1["g_decays"].sem, 1)
                for k in range(4):
                    d, c = k // 2, k % 2
                    dve.wait_ge(s1["row_mm"].sem, s1["row_mm"].due(l, k + 1))
                    for h in range(4):
                        n = 200 + 8 * c + 4 * d + h
                        ins_ = V.scalar_tensor_tensor(DT[:, k, h, :], psA[:, k, h * P:(h + 1) * P], g(n, n + 1), masks[:, d, :],
                                                      ALU.subtract, ALU.min)
                    ins_.then_inc(s1["row_arg"].sem, 1)
                dve.wait_ge(s1["g_col"].sem, s1["g_col"].due(l, 1))
                V.tensor_scalar(g(264, 280), g(248, 264), -1.0, None, ALU.mult).then_inc(s1["g_neg"].sem, 1)
                for d in range(DIRS):
                    dve.wait_ge(s1["q_exp"].sem, s1["q_exp"].due(l, d + 1))
                    c1 = 1 - d
                    V.tensor_tensor(qdecT[:, d, :, :], qdecT[:, d, :, :], qkvT[:, 0:4, c1 * P:(c1 + 1) * P], ALU.mult)\
                        .then_inc(s1["q_dec"].sem, 1)
                dve.wait_ge(s1["kk_mm"].sem, s1["kk_mm"].due(l, 1))
                for k in range(4):
                    d, c = k // 2, k % 2
                    dve.wait_ge(s1["row_exp"].sem, s1["row_exp"].due(l, k + 1))
                    V.tensor_tensor(attnT[:, k, :, :], psB[:, 2 + c, :].rearrange("p (h n) -> p h n", h=4), DT[:, k, :, :],
                                    ALU.mult).then_inc(s1["attn"].sem, 1)
                    for h in range(4):
                        n = 184 + 8 * c + 4 * d + h
                        ins_ = V.scalar_tensor_tensor(MT[:, k, h, :], psB[:, c, h * P:(h + 1) * P], g(n, n + 1), DT[:, k, h, :],
                                                      ALU.mult, ALU.mult)
                    ins_.then_inc(s1["mt"].sem, 1)
                wide = lambda v: v.unsqueeze(1).to_broadcast([P, 4, P])
                four = lambda ps: ps.rearrange("p (h n) -> p h n", h=4)
                for b in range(LEVELS):
                    for k in range(4):
                        d = k // 2
                        if b == 0:
                            dve.wait_ge(s1["mt"].sem, s1["mt"].due(l, k + 1))
                        else:
                            dve.wait_ge(s1["p_mm"].sem, s1["p_mm"].due(l, 4 * (b - 1) + k + 1))
                            if b == 1:
                                dve.wait_ge(s1["u_dve"].sem, s1["u_dve"].due(l, k + 1))
                        V.tensor_tensor(Mm[:, k, :, :], MT[:, k, :, :], wide(masks[:, 2 + d * LEVELS + b, :]), ALU.mult)\
                            .then_inc(s1["masked"].sem, 1)
                    for k in range(4):
                        if b == 0:
                            dve.wait_ge(s1["masked"].sem, s1["masked"].due(l, k + 1))
                            V.tensor_tensor(U[:, k, :, :], wide(ident), Mm[:, k, :, :], ALU.subtract).then_inc(s1["u_dve"].sem, 1)
                            dve.wait_ge(s1["p_mm"].sem, s1["p_mm"].due(l, k + 1))
                            V.tensor_tensor(T[:, k, :, :], wide(ident), four(psA[:, k, :]), ALU.subtract).then_inc(s1["t_new"].sem, 1)
                        elif b < LEVELS - 1:
                            dve.wait_ge(s1["tp_mm"].sem, s1["tp_mm"].due(l, 4 * (b - 1) + k + 1))
                            V.tensor_tensor(T[:, k, :, :], T[:, k, :, :], four(psB[:, k, :]), ALU.subtract).then_inc(s1["t_new"].sem, 1)
                        else:
                            dve.wait_ge(s1["tp_mm"].sem, s1["tp_mm"].due(l, 4 * (b - 1) + k + 1))
                            V.tensor_tensor(U[:, k, :, :], U[:, k, :, :], four(psB[:, k, :]), ALU.subtract).then_inc(s1["u_dve"].sem, 1)
                idx = lambda d, c, h: 8 * c + 4 * d + h
                for d in range(DIRS):
                    for h in range(4):
                        n = 232 + idx(d, d, h)
                        ins_ = V.tensor_scalar(kdec[:, d, h, :], knat[:, d, h, :], g(n, n + 1), None, ALU.mult)
                    ins_.then_inc(s1["k_dec"].sem, 1)
                for d in range(DIRS):
                    dve.wait_ge(s1["v1_mm"].sem, s1["v1_mm"].due(l, d + 1))
                    for h in range(4):
                        n = 184 + idx(d, d, h)
                        ins_ = V.tensor_scalar(v1[:, d, h, :], psA[:, d, h * P:(h + 1) * P], g(n, n + 1), None, ALU.mult)
                    ins_.then_inc(s1["v1"].sem, 1)
                for d in range(DIRS):
                    dve.wait_ge(s1["ks_mm"].sem, s1["ks_mm"].due(l, d + 1))
                    for h in range(4):
                        n = 264 + idx(d, 1 - d, h)
                        ins_ = V.scalar_tensor_tensor(Rr[:, d, h, :], psB[:, d, h * P:(h + 1) * P], g(n, n + 1),
                                                      vnat[:, 1 - d, h, :], ALU.mult, ALU.add)
                    ins_.then_inc(s1["rest"].sem, 1)
                for d in range(DIRS):
                    dve.wait_ge(s1["v2_mm"].sem, s1["v2_mm"].due(l, d + 1))
                    for h in range(4):
                        n = 184 + idx(d, 1 - d, h)
                        ins_ = V.tensor_scalar(v2[:, d, h, :], psB[:, 2 + d, h * P:(h + 1) * P], g(n, n + 1), None, ALU.mult)
                    ins_.then_inc(s1["v2"].sem, 1)
                dve.wait_ge(s1["z_silu"].sem, s1["z_silu"].due(l, 4))
                dve.wait_ge(s1["o_root"].sem, s1["o_root"].due(l, 1))
                V.scalar_tensor_tensor(orr[:, :, :], orr[:, :, :], cols[:, 108:109], zT[:, :, :], ALU.mult, ALU.mult).then_inc(ch.sem, 1)
                dve.wait_ge(ch.sem, ch.step(l))
                V.tensor_tensor(oy[:, :, :], orr[:, :, :], psA[:, 0:2, :].rearrange("p a (b n) -> p (a b) n", b=2), ALU.mult)\
                    .then_inc(s1["o_y"].sem, 1)
                dve.wait_ge(s1["y_hi"].sem, s1["y_hi"].due(l, 5))
                V.tensor_tensor(xT_lo[:, 0:4, :], oy[:, :, :], xT_hi[:, 0:4, :].bitcast(F32), ALU.subtract).then_inc(s1["y_lo"].sem, 1)

            def stack2_mixer(l):
                ch = dve_chain[1]
                g = lambda a, b: small[:, a:b]
                dve.wait_ge(s2["cols2_tp"].sem, s2["cols2_tp"].due(l, 1))
                V.tensor_copy(cols[:, 0:124], psB[:, 0, 0:124]).then_inc(s2["cols2"].sem, 1)
                dve.wait_ge(param_loaded, l * (16 * NPAR2) + 16 * (DEPTH * NPAR1 + NPAR2))
                lp = g(0, 256).rearrange("p (a b n) -> p a b n", a=2, b=2)
                lq = g(256, 384).rearrange("p (a n) -> p a n", a=2)
                V.tensor_tensor(lq, lp[:, :, 0, :], lp[:, :, 1, :], ALU.mult).then_inc(ch.sem, 1)
                dve.wait_ge(ch.sem, ch.step(l))
                V.tensor_reduce(stat[:, 26:28], lq, AX_X, ALU.add).then_inc(s2["lam_sum"].sem, 1)
                dve.wait_ge(s2["lam_exp"].sem, s2["lam_exp"].due(l, 1))
                V.tensor_tensor(stat[:, 30:31], stat[:, 29:30], stat[:, 28:29], ALU.subtract).then_inc(ch.sem, 1)
                dve.wait_ge(ch.sem, ch.step(l))
                V.tensor_tensor(stat[:, 30:31], stat[:, 30:31], stat[:, 24:25], ALU.subtract).then_inc(ch.sem, 1)
                dve.wait_ge(ch.sem, ch.step(l))
                dve.wait_ge(s2["cols2"].sem, s2["cols2"].due(l, 1))
                V.tensor_tensor(stat[:, 31:32], cols[:, 3:4], stat[:, 25:26], ALU.mult).then_inc(ch.sem, 1)
                dve.wait_ge(ch.sem, ch.step(l))
                done = s2["ev_dve"].sem
                for i in range(26):
                    ps = psA[:, i % 4, 0:L]
                    if 8 <= i < 12 or 16 <= i < 18:
                        dve.wait_ge(half_used[1].sem, half_used[1].due(l, i + 1))
                        dst, c = (v_da, i - 8) if i < 12 else (v_ret, i - 16)
                        V.tensor_copy(dst[:, :, c * P:(c + 1) * P], ps.rearrange("p (r n) -> p r n", r=RB)).then_inc(done, 1)
                    elif 18 <= i < 20:
                        dve.wait_ge(s2["rg_sig"].sem, s2["rg_sig"].due(l, i - 17))
                        V.tensor_tensor(rg[:, i - 18, :], rgs[:, i - 18, :], ps, ALU.mult).then_inc(done, 1)
                    elif 20 <= i < 22:
                        dve.wait_ge(half_used[1].sem, half_used[1].due(l, i + 1))
                        V.tensor_copy(scb[:, i - 20, :], ps).then_inc(done, 1)
                    elif i >= 24:
                        b = i - 24
                        dve.wait_ge(half_used[1].sem, half_used[1].due(l, i + 1))
                        dve.wait_ge(s2["ev_act"].sem, s2["ev_act"].due(l, 12 + b + 1))
                        V.tensor_tensor(scx[:, b, :], scc[:, b, :], ps, ALU.mult).then_inc(done, 1)
                dve.wait_ge(s2["ev_dve"].sem, s2["ev_dve"].due(l, 12))
                for b in range(2):
                    w = lambda k: cols[:, 4 + 2 * k + b:5 + 2 * k + b]
                    o, v = sco[:, b, :], scx[:, b, :]
                    V.tensor_scalar(o, v, w(2), cols[:, 10 + b:11 + b], ALU.mult, ALU.add).then_inc(ch.sem, 1)
                    dve.wait_ge(ch.sem, ch.step(l))
                    V.scalar_tensor_tensor(o[:, 1:L], v[:, 0:L - 1], w(1), o[:, 1:L], ALU.mult, ALU.add).then_inc(ch.sem, 1)
                    dve.wait_ge(ch.sem, ch.step(l))
                    V.scalar_tensor_tensor(o[:, 2:L], v[:, 0:L - 2], w(0), o[:, 2:L], ALU.mult, ALU.add).then_inc(ch.sem, 1)
                    dve.wait_ge(ch.sem, ch.step(l))
                    ins_ = V.tensor_tensor(o, o, scb[:, b, :], ALU.mult)
                ins_.then_inc(s2["sc_y"].sem, 1)
                dve.wait_ge(s2["a_root"].sem, s2["a_root"].due(l, 1))
                for k in range(2):
                    v = qkT[:, 4 * k:4 * k + 4, :]
                    ins_ = V.scalar_tensor_tensor(v, v, cols[:, k:k + 1], rr2[:, 4 * k:4 * k + 4, :], ALU.mult, ALU.mult)
                ins_.then_inc(s2["a_qk"].sem, 1)
                dve.wait_ge(s2["rot_mm"].sem, s2["rot_mm"].due(l, 1))
                dve.wait_ge(const_loaded, 80)
                for k in range(2):
                    two = lambda n: rotary[:, n, :].unsqueeze(1).to_broadcast([P, 2, L])
                    v = slice(2 * k, 2 * k + 2)
                    V.tensor_tensor(rtmp[:, :, :], psB[:, k, :].rearrange("p (b n) -> p b n", b=2), two(2 * k + 1), ALU.mult)
                    V.tensor_tensor(rqkr[:, v, :], rqk[:, v, :], two(2 * k), ALU.mult).then_inc(ch.sem, 1)
                    dve.wait_ge(ch.sem, ch.step(l))
                    ins_ = V.tensor_tensor(rqkr[:, v, :], rqkr[:, v, :], rtmp[:, :, :], ALU.add)
                    if k == 0:
                        ins_.then_inc(ch.sem, 1)
                        dve.wait_ge(ch.sem, ch.step(l))
                ins_.then_inc(s2["rot"].sem, 1)
                for k in range(8):
                    ps = (psA, psB)[k % 2][:, k // 2, :]
                    dve.wait_ge(s2["sc_mm"].sem, s2["sc_mm"].due(l, k + 1))
                    V.tensor_reduce(g(304 + 2 * k, 305 + 2 * k), ps[:, 0:L], AX_X, ALU.max)
                    V.tensor_reduce(g(305 + 2 * k, 306 + 2 * k), ps[:, L:3 * P], AX_X, ALU.max).then_inc(ch.sem, 1)
                    dve.wait_ge(ch.sem, ch.step(l))
                    V.tensor_scalar(g(320 + 2 * k, 322 + 2 * k), g(304 + 2 * k, 306 + 2 * k), -1.0, None, ALU.mult).then_inc(s2["sc_max"].sem, 1)
                for h in range(4):
                    dve.wait_ge(s2["sc_exp"].sem, s2["sc_exp"].due(l, 2 * h + 2))
                    V.reciprocal(g(352 + 4 * h, 356 + 4 * h), g(336 + 4 * h, 340 + 4 * h)).then_inc(ch.sem, 1)
                    dve.wait_ge(ch.sem, ch.step(l))
                    V.tensor_scalar(g(354 + 4 * h, 356 + 4 * h), g(354 + 4 * h, 356 + 4 * h), stat[:, 30:31], None, ALU.mult).then_inc(ch.sem, 1)
                    dve.wait_ge(ch.sem, ch.step(l))
                    for q, (a, z) in enumerate(((0, L), (L, 3 * P))):
                        p0, p1 = prob[:, 2 * h, a:z], prob[:, 2 * h + 1, a:z]
                        n = 352 + 4 * h + q
                        V.tensor_scalar(p1, p1, g(n + 2, n + 3), None, ALU.mult).then_inc(ch.sem, 1)
                        dve.wait_ge(ch.sem, ch.step(l))
                        ins_ = V.scalar_tensor_tensor(p0, p0, g(n, n + 1), p1, ALU.mult, ALU.add)
                    ins_.then_inc(s2["sc_a"].sem, 1)
                dve.wait_ge(s2["o_hi"].sem, s2["o_hi"].due(l, 1))
                V.tensor_tensor(xT_lo[:, 6:8, :], sco[:, :, :], xT_hi[:, 6:8, :].bitcast(F32), ALU.subtract).then_inc(s2["o_lo"].sem, 1)
                for h in range(4):
                    dve.wait_ge(s2["rs_mm"].sem, s2["rs_mm"].due(l, h + 1))
                    V.tensor_tensor(iT[:, h, :], psA[:, h, 0:3 * P], retdecay[:, h, :], ALU.mult).then_inc(s2["rs_dec"].sem, 1)
                dve.wait_ge(s2["oa_root"].sem, s2["oa_root"].due(l, 1))
                V.scalar_tensor_tensor(rr2[:, 0:4, :], rr2[:, 0:4, :], stat[:, 31:32],
                                       psB[:, 0:2, :].rearrange("p a (b n) -> p (a b) n", b=2), ALU.mult, ALU.mult).then_inc(s2["oa_y"].sem, 1)
                dve.wait_ge(s2["o_hi"].sem, s2["o_hi"].due(l, 2))
                V.tensor_tensor(xT_lo[:, 0:4, :], rr2[:, 0:4, :], xT_hi[:, 0:4, :].bitcast(F32), ALU.subtract).then_inc(s2["o_lo"].sem, 1)
                dve.wait_ge(s2["or_root"].sem, s2["or_root"].due(l, 1))
                V.scalar_tensor_tensor(rr2[:, 4:6, :], rr2[:, 4:6, :], cols[:, 2:3], rg[:, :, :], ALU.mult, ALU.mult).then_inc(ch.sem, 1)
                dve.wait_ge(ch.sem, ch.step(l))
                V.tensor_tensor(rr2[:, 4:6, :], rr2[:, 4:6, :], psA[:, 0, :].rearrange("p (b n) -> p b n", b=2), ALU.mult).then_inc(s2["or_y"].sem, 1)
                dve.wait_ge(s2["o_hi"].sem, s2["o_hi"].due(l, 3))
                V.tensor_tensor(xT_lo[:, 4:6, :], rr2[:, 4:6, :], xT_hi[:, 4:6, :].bitcast(F32), ALU.subtract).then_inc(s2["o_lo"].sem, 1)
                for r in range(3):
                    dve.wait_ge(half_used[1].sem, half_used[1].due(l, (53, 55, 57)[r] + 1))
                    for n in range(KC):
                        ps = (psA, psB)[n // 4][:, n % 4, 0:L]
                        if r == 0:
                            V.tensor_tensor(yacc[:, n, :], gates[:, n, :], ps, ALU.mult).then_inc(s2["br"].sem, 1)
                        else:
                            V.tensor_tensor(ytm[:, n % 2, :], gates[:, 8 * r + n, :], ps, ALU.mult).then_inc(ch.sem, 1)
                            dve.wait_ge(ch.sem, ch.step(l))
                            V.tensor_tensor(yacc[:, n, :], yacc[:, n, :], ytm[:, n % 2, :], ALU.add).then_inc(s2["br"].sem, 1)
                for n in range(KC):
                    dve.wait_ge(s2["yb_hi"].sem, s2["yb_hi"].due(l, n + 1))
                    V.tensor_tensor(yT_lo[:, n, :], yacc[:, n, :], yT_hi[:, n, :].bitcast(F32), ALU.subtract).then_inc(s2["yb_lo"].sem, 1)

            V.memset(rows[:, :], 0.0)
            for col, value in ((eps, EPS), (eps64, 64 * EPS), (eps128, 128 * EPS)):
                ins_ = V.memset(col, value)
            ins_.then_inc(setup, 1)
            V.memset(brow[:, L:HK], MASKED)
            dve.wait_ge(bias_mm, 1)
            V.tensor_copy(brow[:, 0:L], psB[0:4, 0, 0:L]).then_inc(bias_row, 1)
            dve.sem_inc(n_xn[0].sem, 1)
            dve.wait_ge(const_loaded, 48)
            with dve.Fori(0, DEPTH) as l:
                norm_scale(0, l, 0)
                norm_rest(0, l, 0)
                dve.wait_ge(param_loaded, l * (16 * NPAR1) + 16 * NPAR1)
                V.tensor_copy(wba_hi[:, :, :], w_ba[:, :, :]).then_inc(dve_chain[0].sem, 1)
                dve.wait_ge(dve_chain[0].sem, dve_chain[0].step(l))
                V.tensor_tensor(wba_lo[:, :, :], w_ba[:, :, :], wba_hi[:, :, :].bitcast(F32), ALU.subtract).then_inc(s1["wba"].sem, 1)
                ffn(0, l, 0, 0)
                add_to_x(0, l, 65, 0.5)
                filters(l)
                norm_scale(0, l, 1)
                norm_rest(0, l, 1)
                stack1_projections(l)
                hyena(l)
                deltanet(l)
                add_to_x(0, l, 101, 1.0)
                norm_scale(0, l, 2)
                norm_rest(0, l, 2)
                ffn(0, l, 1, 102)
                add_to_x(0, l, 167, 0.5)
            steps["dve_chain"] = [dve_chain[0].n, 0, 5]
            dve.wait_ge(n_r0[0].sem, n_r0[0].due(DEPTH, 1))
            newton(0, dve_chain[2], rstd, ss, r0, 1.0 / D, RB)
            dve.wait_ge(gain_loaded[0].sem, gain_loaded[0].due(DEPTH, 16))
            for rb in range(RB):
                V.scalar_tensor_tensor(x[:, rb, :], x[:, rb, :], rstd[:, rb:rb + 1], gain[:, :],
                                       ALU.mult, ALU.mult).then_inc(x_ready[0].sem, 2)
            with dve.Fori(0, DEPTH) as l:
                norm_scale(1, l, 0)
                norm_rest(1, l, 0)
                stack2_mixer(l)
                add_to_x(1, l, 65, 1.0)
                norm_scale(1, l, 1)
                norm_rest(1, l, 1)
                ffn(1, l, 0, 66)
                add_to_x(1, l, 131, 1.0)
            steps["dve_chain"][1] = dve_chain[1].n

        @block.tensor
        def _(pe):
            M = nc.tensor.matmul

            def turn_x(st, l, q):
                for i in range(4):
                    if i == 0:
                        pe.wait_ge(n_xn[st].sem, n_xn[st].due(l, 2 * q + 2))
                    for kc in (2 * i, 2 * i + 1):
                        for rb in range(RB):
                            c = (kc % 2) * L + rb * P
                            ins_ = nc.tensor.transpose(psA[:, i, c:c + P], xn[:, rb, kc * P:(kc + 1) * P], ident)
                    ins_.then_inc(n_tp[st].sem, 1)

            def project_T(st, l, s, o):
                pe.wait_ge(lo_done[st].sem, lo_done[st].due(l, s + 1))
                hi, lo = split_half(w_hi, s, "A"), split_half(w_lo, s, "A")
                for kc in range(KC):
                    ins_ = product(o, hi[:, kc, :], lo[:, kc, :], xT_hi[:, kc, :], xT_lo[:, kc, :], kc == 0, kc == KC - 1)
                ins_.then_inc(half_used[st].sem, 1)

            def project(st, l, s, o):
                pe.wait_ge(lo_done[st].sem, lo_done[st].due(l, s + 1))
                hi, lo = split_half(w_hi, s, "A"), split_half(w_lo, s, "A")
                for rb in range(RB):
                    t = slice(rb * P, (rb + 1) * P)
                    for kc in range(KC):
                        ins_ = product(o[:, t], xT_hi[:, kc, t], xT_lo[:, kc, t], hi[:, kc, :], lo[:, kc, :],
                                       kc == 0, kc == KC - 1)
                ins_.then_inc(half_used[st].sem, 1)

            def into_x(st, l, s0, a_hi, a_lo, made=None, first=0):
                nk = a_hi.shape[1]
                for k in range(nk):
                    pe.wait_ge(lo_done[st].sem, lo_done[st].due(l, s0 + k + 1))
                    if made:
                        pe.wait_ge(made.sem, made.due(l, first + k + 1))
                    hi, lo = split_half(w_hi, s0 + k, "B"), split_half(w_lo, s0 + k, "B")
                    for rb in range(RB):
                        t = slice(rb * P, (rb + 1) * P)
                        for c in range(2):
                            v = slice(c * 512, (c + 1) * 512)
                            ins_ = product(psB[:, 2 * rb + c, :], a_hi[:, k, t], a_lo[:, k, t], hi[:, v], lo[:, v],
                                           k == 0, k == nk - 1)
                    ins_.then_inc(half_used[st].sem, 1)

            def ffn(st, l, f, s0, q):
                freed = f_act[0] if st == 0 else f_conv[1]
                pe.wait_ge(n_lo[st].sem, n_lo[st].due(l, 4 * q + 4))
                for j in range(NF // 2):
                    for i in range(2):
                        if j:
                            pe.wait_ge(freed.sem, freed.due(l, NF * f + 2 * (j - 1) + i + 1))
                        project_T(st, l, s0 + 4 * j + i, psA[:, i, 0:L])
                    for i in range(2):
                        if j:
                            pe.wait_ge(f_prod[st].sem, f_prod[st].due(l, NF * f + 2 * (j - 1) + i + 1))
                        project_T(st, l, s0 + 4 * j + 2 + i, psA[:, 2 + i, 0:L])
                    if st == 0 and f == 0:
                        if j == 0:
                            turn_rows1(l)
                        if j in (1, 3, 5):
                            mlp(l, j // 2)
                into_x(st, l, s0 + 2 * NF, hT_hi, hT_lo, f_lo[st], NF * f)

            def turn_rows1(l):
                pe.wait_ge(param_loaded, l * (16 * NPAR1) + 16 * NPAR1)
                nc.tensor.transpose(psB[:, 2, 0:117], rows[0:117, :], ident[0:117, 0:117]).then_inc(s1["cols_tp"].sem, 1)

            def mlp(l, k):
                if k == 0:
                    pe.wait_ge(s1["cols"].sem, s1["cols"].due(l, 1))
                else:
                    pe.wait_ge(s1["mlp_sin"].sem, s1["mlp_sin"].due(l, k))
                n, rhs = (EMB, featsT[:, :]) if k == 0 else (HID, hdn[:, :])
                M(psB[:, 3, 0:L], fw[0:n, k:k + 2, :].rearrange("p a b -> p (a b)"), rhs, start=True, stop=True)\
                    .then_inc(s1["mlp_mm"].sem, 1)

            def filters(l):
                pe.wait_ge(s1["mlp_sin"].sem, s1["mlp_sin"].due(l, 3))
                for k in range(8):
                    if k >= 4:
                        pe.wait_ge(s1["filt"].sem, s1["filt"].due(l, k - 3))
                    rb, n = k // 4, k % 4
                    M(psA[:, n, :], hdn[:, rb * P:(rb + 1) * P], wfilt[:, n * HYW:(n + 1) * HYW], start=True, stop=True)\
                        .then_inc(s1["filt_mm"].sem, 1)
                for k in range(10):
                    o, b = k // 5, k % 5
                    pe.wait_ge(s1["filt"].sem, s1["filt"].due(l, 8))
                    if k >= 4:
                        pe.wait_ge(s1["spec"].sem, s1["spec"].due(l, k - 3))
                    for n, (table, d) in enumerate(((dft_f, 0), (dft_b, 1))):
                        for rb in range(RB):
                            ins_ = M(psA[:, k % 4, :], table[:, rb, b, :], filt[:, rb, 2 * d + o, :],
                                     start=(n == 0 and rb == 0), stop=(n == 1 and rb == 1))
                    ins_.then_inc(s1["spec_mm"].sem, 1)
                pe.wait_ge(s1["spec"].sem, s1["spec"].due(l, 10))

            def stack1_projections(l):
                pe.wait_ge(n_lo[0].sem, n_lo[0].due(l, 8))
                for i in range(28):
                    if 4 <= i < 28:
                        pe.wait_ge(s1["conv"].sem, s1["conv"].due(l, i - 3))
                    project_T(0, l, 66 + i, psA[:, i % 4, 0:L])
                    if i == 11:
                        pe.wait_ge(s1["wba"].sem, s1["wba"].due(l, 1))
                        for rb in range(RB):
                            t = slice(rb * P, (rb + 1) * P)
                            for kc in range(KC):
                                ins_ = product(psB[:, 0, 16 * rb:16 * rb + 16], xT_hi[:, kc, t], xT_lo[:, kc, t],
                                               wba_hi[:, kc, :], wba_lo[:, kc, :], kc == 0, kc == KC - 1)
                        ins_.then_inc(s1["ba_mm"].sem, 1)
                pe.wait_ge(s1["conv"].sem, s1["conv"].due(l, 24))
                for k in range(6):
                    if k >= 3:
                        pe.wait_ge(s1["hy_nat"].sem, s1["hy_nat"].due(l, k - 2))
                    for b in range(4):
                        ins_ = nc.tensor.transpose(psB[:, 1 + k % 3, b * P:(b + 1) * P],
                                                   hyT[:, 4 * (k // 2) + b, (k % 2) * P:(k % 2 + 1) * P], ident)
                    ins_.then_inc(s1["hy_turned"].sem, 1)

            def hyena(l):
                pe.wait_ge(s1["z_silu"].sem, s1["z_silu"].due(l, 4))
                pe.wait_ge(s1["hy_nat"].sem, s1["hy_nat"].due(l, 6))
                for o in range(2):
                    src = (hynat[:, :, 0, :], zz[:, :, :])[o]
                    if o:
                        pe.wait_ge(s1["y_spec"].sem, s1["y_spec"].due(l, 2))
                        pe.wait_ge(s1["zz"].sem, s1["zz"].due(l, 2))
                    for b, table in enumerate((0, 1, 5, 3)):
                        for rb in range(RB):
                            ins_ = M(psA[:, b, :], dft_f[:, rb, table, :], src[:, rb, :], start=(rb == 0), stop=(rb == RB - 1))
                        ins_.then_inc(s1["z_mm"].sem, 1)
                    pe.wait_ge(s1["y_spec"].sem, s1["y_spec"].due(l, 2 * o + 2))
                    for rb in range(RB):
                        for b in range(4):
                            ins_ = M(psB[:, 1 + rb, :], dft_i[:, b, rb * P:(rb + 1) * P], Ysp[:, b, :], start=(b == 0), stop=(b == 3))
                        ins_.then_inc(s1["inv_mm"].sem, 1)
                pe.wait_ge(s1["hy_zn"].sem, s1["hy_zn"].due(l, 1))
                for b in range(4):
                    for rb in range(RB):
                        c = (b % 2) * L + rb * P
                        ins_ = nc.tensor.transpose(psA[:, b // 2, c:c + P], zz[:, rb, b * P:(b + 1) * P], ident)
                    if b % 2:
                        ins_.then_inc(s1["hy_back"].sem, 1)

            def deltanet(l):
                g = lambda n: small[:, 152 + n:153 + n]
                pe.wait_ge(s1["y_lo"].sem, s1["y_lo"].due(l, 4))
                pe.wait_ge(s1["qk_sq"].sem, s1["qk_sq"].due(l, 1))
                for k in range(4):
                    ins_ = M(psA[:, k, :], ones, sq[:, 2 * k:2 * k + 2, :].rearrange("p b n -> p (b n)"), start=True, stop=True)
                ins_.then_inc(s1["qk_mm"].sem, 1)
                pe.wait_ge(s1["g_ready"].sem, s1["g_ready"].due(l, 1))
                pe.wait_ge(s1["qk_norm"].sem, s1["qk_norm"].due(l, 1))
                for k in range(4):
                    for h in range(4):
                        ins_ = nc.tensor.transpose(psB[:, k, h * P:(h + 1) * P],
                                                   qkvT[:, 4 + 4 * (k // 2) + h, (k % 2) * P:(k % 2 + 1) * P], ident)
                    ins_.then_inc(s1["kv_turned"].sem, 1)
                pe.wait_ge(s1["kv_nat"].sem, s1["kv_nat"].due(l, 4))
                for c in range(RB):
                    for d in range(DIRS):
                        n = 8 * c + 4 * d
                        M(psB[:, 0, n:n + 4], cum[d], small[:, 152 + n:156 + n], start=True, stop=True)
                    ins_ = M(psB[:, 0, 16 + 8 * c:24 + 8 * c], ones, small[:, 152 + 8 * c:160 + 8 * c], start=True, stop=True)
                ins_.then_inc(s1["g_cum"].sem, 1)
                pe.wait_ge(s1["qk_root"].sem, s1["qk_root"].due(l, 1))
                for k in range(4):
                    d, c = k // 2, k % 2
                    for h in range(4):
                        ins_ = M(psA[:, k, h * P:(h + 1) * P], g(8 * c + 4 * d + h).to_broadcast([P, P]), cum[d], start=True, stop=True)
                    ins_.then_inc(s1["row_mm"].sem, 1)
                pe.wait_ge(s1["g_decays"].sem, s1["g_decays"].due(l, 1))
                for c in range(RB):
                    t = slice(c * P, (c + 1) * P)
                    for h in range(4):
                        o = slice(h * P, (h + 1) * P)
                        M(psB[:, c, o], qkvT[:, 4 + h, t], qkvT[:, 4 + h, t], start=True, stop=True)
                        ins_ = M(psB[:, 2 + c, o], qkvT[:, 4 + h, t], qkvT[:, h, t], start=True, stop=True)
                ins_.then_inc(s1["kk_mm"].sem, 1)
                pe.wait_ge(s1["q_exp"].sem, s1["q_exp"].due(l, 2))
                for k in range(4):
                    pe.wait_ge(s1["row_arg"].sem, s1["row_arg"].due(l, k + 1))
                for b in range(LEVELS):
                    for k in range(4):
                        pe.wait_ge(s1["masked"].sem, s1["masked"].due(l, 4 * b + k + 1))
                        if b == 1:
                            pe.wait_ge(s1["t_new"].sem, s1["t_new"].due(l, k + 1))
                        elif b > 1:
                            pe.wait_ge(s1["u_act"].sem, s1["u_act"].due(l, 4 * (b - 2) + k + 1))
                        for h in range(4):
                            o = psA[:, k, h * P:(h + 1) * P]
                            if b == 0:
                                ins_ = nc.tensor.transpose(o, Mm[:, k, h, :], ident)
                            else:
                                ins_ = M(o, Mm[:, k, h, :], T[:, k, h, :], start=True, stop=True)
                        ins_.then_inc(s1["p_mm"].sem, 1)
                    if b == 0:
                        continue
                    for k in range(4):
                        pe.wait_ge(s1["p_copy"].sem, s1["p_copy"].due(l, 4 * (b - 1) + k + 1))
                        if b == 1:
                            pe.wait_ge(s1["u_dve"].sem, s1["u_dve"].due(l, k + 1))
                        for h in range(4):
                            o = psB[:, k, h * P:(h + 1) * P]
                            if b < LEVELS - 1:
                                ins_ = M(o, U[:, k, h, :], Pp[:, k, h, :], start=True, stop=True)
                            else:
                                ins_ = M(o, Pp[:, k, h, :], U[:, k, h, :], start=True, stop=True)
                        ins_.then_inc(s1["tp_mm"].sem, 1)
                    if b < LEVELS - 1:
                        for k in range(4):
                            pe.wait_ge(s1["t_new"].sem, s1["t_new"].due(l, 4 * b + k + 1))
                            for h in range(4):
                                ins_ = nc.tensor.transpose(psA[:, k, h * P:(h + 1) * P], T[:, k, h, :], ident)
                            ins_.then_inc(s1["u_tp"].sem, 1)
                part = lambda ps, h: ps[:, h * P:(h + 1) * P]
                for d in range(DIRS):
                    pe.wait_ge(s1["u_dve"].sem, s1["u_dve"].due(l, 4 + 2 * d + d + 1))
                    for h in range(4):
                        ins_ = M(part(psA[:, d, :], h), U[:, 2 * d + d, h, :], vnat[:, d, h, :], start=True, stop=True)
                    ins_.then_inc(s1["v1_mm"].sem, 1)
                for d in range(DIRS):
                    pe.wait_ge(s1["v1"].sem, s1["v1"].due(l, d + 1))
                    pe.wait_ge(s1["k_dec"].sem, s1["k_dec"].due(l, d + 1))
                    for h in range(4):
                        ins_ = M(part(psA[:, 2 + d, :], h), kdec[:, d, h, :], v1[:, d, h, :], start=True, stop=True)
                    ins_.then_inc(s1["s_mm"].sem, 1)
                pe.wait_ge(s1["u_dve"].sem, s1["u_dve"].due(l, 8))
                for d in range(DIRS):
                    c1 = 1 - d
                    pe.wait_ge(s1["s_copy"].sem, s1["s_copy"].due(l, d + 1))
                    for h in range(4):
                        ins_ = M(part(psB[:, d, :], h), qkvT[:, 4 + h, c1 * P:(c1 + 1) * P], Sst[:, d, h, :], start=True, stop=True)
                    ins_.then_inc(s1["ks_mm"].sem, 1)
                for d in range(DIRS):
                    pe.wait_ge(s1["rest"].sem, s1["rest"].due(l, d + 1))
                    for h in range(4):
                        ins_ = M(part(psB[:, 2 + d, :], h), U[:, 2 * d + 1 - d, h, :], Rr[:, d, h, :], start=True, stop=True)
                    ins_.then_inc(s1["v2_mm"].sem, 1)
                pe.wait_ge(s1["q_dec"].sem, s1["q_dec"].due(l, 2))
                pe.wait_ge(s1["attn"].sem, s1["attn"].due(l, 4))
                pe.wait_ge(s1["v2"].sem, s1["v2"].due(l, 2))
                for h in range(4):
                    for c in range(RB):
                        o = psA[:, h // 2, (h % 2) * L + c * P:(h % 2) * L + (c + 1) * P]
                        a, b = c, 1 - c
                        M(o, v1[:, a, h, :], attnT[:, 2 * a + c, h, :], start=True, stop=False)
                        M(o, Sst[:, b, h, :], qdecT[:, b, h, :], start=False, stop=False)
                        ins_ = M(o, v2[:, b, h, :], attnT[:, 2 * b + c, h, :], start=False, stop=True)
                    if h % 2:
                        ins_.then_inc(s1["o_mm"].sem, 1)
                pe.wait_ge(s1["o_sq"].sem, s1["o_sq"].due(l, 1))
                for k in range(2):
                    ins_ = M(psB[:, k, :], ones, osq[:, 2 * k:2 * k + 2, :].rearrange("p b n -> p (b n)"), start=True, stop=True)
                ins_.then_inc(s1["o_ss"].sem, 1)

            def stack2_mixer(l):
                pe.wait_ge(param_loaded, l * (16 * NPAR2) + 16 * (DEPTH * NPAR1 + NPAR2))
                nc.tensor.transpose(psB[:, 0, 0:124], rows[0:124, :], ident[0:124, 0:124]).then_inc(s2["cols2_tp"].sem, 1)
                by_dve = set(range(8, 12)) | set(range(16, 22)) | {24, 25}
                released = {}
                na = nd = 0
                for i in range(50):
                    if i in by_dve:
                        nd += 1
                        released[i] = (s2["ev_dve"], nd)
                    else:
                        na += 1
                        released[i] = (s2["ev_act"], na)
                pe.wait_ge(n_lo[1].sem, n_lo[1].due(l, 4))
                for i in range(50):
                    if i >= 4:
                        pe.wait_ge(released[i - 4][0].sem, released[i - 4][0].due(l, released[i - 4][1]))
                    if 8 <= i < 12 or 16 <= i < 18:
                        project(1, l, i, psA[:, i % 4, 0:L])
                    else:
                        project_T(1, l, i, psA[:, i % 4, 0:L])
                pe.wait_ge(s2["a_sq"].sem, s2["a_sq"].due(l, 1))
                pe.wait_ge(s2["cols2"].sem, s2["cols2"].due(l, 1))
                for k in range(4):
                    ins_ = M(psB[:, k, :], blockones, sq2[:, 2 * k:2 * k + 2, :].rearrange("p b n -> p (b n)"), start=True, stop=True)
                ins_.then_inc(s2["a_mm"].sem, 1)
                pe.wait_ge(s2["a_root"].sem, s2["a_root"].due(l, 1))
                pe.wait_ge(s2["ev_act"].sem, s2["ev_act"].due(l, 12))
                for b in range(4):
                    ins_ = M(psB[:, b // 2, (b % 2) * L:(b % 2 + 1) * L], rot, rqk[:, b, :], start=True, stop=True)
                ins_.then_inc(s2["rot_mm"].sem, 1)
                pe.wait_ge(s2["a_qk"].sem, s2["a_qk"].due(l, 1))
                pe.wait_ge(s2["rot"].sem, s2["rot"].due(l, 1))
                pe.wait_ge(s2["ev_act"].sem, s2["ev_act"].due(l, 38))
                pe.wait_ge(hankel_loaded, 16)
                for k in range(8):
                    h, m = k // 2, k % 2
                    ps = (psA, psB)[m][:, h, :]
                    r = slice(64 * m, 64 * m + 64)
                    M(ps[:, 0:L], flip, hankel[:, h, :], start=True, stop=False)
                    M(ps[:, 0:L], qkT[r, h, P:L], qkT[r, 4 + h, :], start=False, stop=True)
                    M(ps[:, L:3 * P], flip, hankel[:, h, P:L], start=True, stop=False)
                    ins_ = M(ps[:, L:3 * P], qkT[r, h, 0:P], qkT[r, 4 + h, 0:P], start=False, stop=True)
                    ins_.then_inc(s2["sc_mm"].sem, 1)
                for h in range(4):
                    pe.wait_ge(s2["sc_a"].sem, s2["sc_a"].due(l, h + 1))
                    a = prob[:, 2 * h, :]
                    nc.tensor.transpose(psA[:, h, 0:P], a[:, L:3 * P], ident)
                    nc.tensor.transpose(psA[:, h, P:2 * P], a[:, 0:P], ident)
                    nc.tensor.transpose(psA[:, h, 2 * P:3 * P], a[:, P:2 * P], ident).then_inc(s2["a_turned"].sem, 1)
                for h in range(4):
                    pe.wait_ge(s2["a_copy"].sem, s2["a_copy"].due(l, h + 1))
                    o = psB[:, h // 2, (h % 2) * L:(h % 2 + 1) * L]
                    M(o, v_da[:, 0, h * P:(h + 1) * P], aT[:, h, 0:L], start=True, stop=False)
                    ins_ = M(o[:, P:L], v_da[:, 1, h * P:(h + 1) * P], aT[:, h, L:3 * P], start=False, stop=True)
                    if h % 2:
                        ins_.then_inc(s2["oa_mm"].sem, 1)
                for h in range(4):
                    b, r = h // 2, slice(64 * (h % 2), 64 * (h % 2) + 64)
                    M(psA[:, h, 0:L], rqkr[r, 2 + b, 0:P], rqkr[r, b, :], start=True, stop=True)
                    M(psA[:, h, L:3 * P], rqkr[r, 2 + b, P:L], rqkr[r, b, P:L], start=True, stop=True).then_inc(s2["rs_mm"].sem, 1)
                pe.wait_ge(s2["oa_sq"].sem, s2["oa_sq"].due(l, 1))
                for k in range(2):
                    ins_ = M(psB[:, 2 + k, :], ones, sq2[:, 2 * k:2 * k + 2, :].rearrange("p b n -> p (b n)"), start=True, stop=True)
                ins_.then_inc(s2["oa_ss"].sem, 1)
                pe.wait_ge(s2["rs_dec"].sem, s2["rs_dec"].due(l, 4))
                for h in range(4):
                    b, r = h // 2, slice(64 * (h % 2), 64 * (h % 2) + 64)
                    o = psA[r, 0, b * L:(b + 1) * L]
                    v = v_ret[:, :, h * 64:(h + 1) * 64]
                    M(o, v[:, 0, :], iT[:, h, 0:L], start=True, stop=False)
                    ins_ = M(o[:, P:L], v[:, 1, :], iT[:, h, L:3 * P], start=False, stop=True)
                ins_.then_inc(s2["or_mm"].sem, 1)
                pe.wait_ge(s2["or_sq"].sem, s2["or_sq"].due(l, 1))
                M(psA[:, 1, :], blockones, sq2[:, 4:6, :].rearrange("p b n -> p (b n)"), start=True, stop=True).then_inc(s2["or_ss"].sem, 1)
                pe.wait_ge(s2["o_lo"].sem, s2["o_lo"].due(l, 3))
                k = 0
                for r, n in enumerate((4, 2, 2)):
                    for i in range(n):
                        pe.wait_ge(lo_done[1].sem, lo_done[1].due(l, 50 + k + 1))
                        hi, lo = split_half(w_hi, 50 + k, "B"), split_half(w_lo, 50 + k, "B")
                        for c in range(KC):
                            if r and i == 0:
                                pe.wait_ge(s2["br"].sem, s2["br"].due(l, 8 * (r - 1) + c + 1))
                            o = (psA, psB)[c // 4][:, c % 4, 0:L]
                            v = slice(c * P, (c + 1) * P)
                            ins_ = product(o, hi[:, v], lo[:, v], xT_hi[:, k, :], xT_lo[:, k, :], i == 0, i == n - 1)
                        ins_.then_inc(half_used[1].sem, 1)
                        k += 1
                pe.wait_ge(s2["br"].sem, s2["br"].due(l, 24))
                into_x(1, l, 58, yT_hi, yT_lo, s2["yb_lo"])

            pe.sem_inc(half_used[0].sem, SLOTS)
            pe.wait_ge(const_loaded, 48)
            pe.wait_ge(bias_loaded, 32)
            M(psB[0:4, 0, 0:HK], relb[:, :], onehot[:, :], start=True, stop=True).then_inc(bias_mm, 1)
            with pe.Fori(0, DEPTH) as l:
                turn_x(0, l, 0)
                ffn(0, l, 0, 0, 0)
                filters(l)
                turn_x(0, l, 1)
                stack1_projections(l)
                hyena(l)
                deltanet(l)
                pe.wait_ge(s1["y_lo"].sem, s1["y_lo"].due(l, 5))
                into_x(0, l, 94, xT_hi, xT_lo)
                turn_x(0, l, 2)
                ffn(0, l, 1, 102, 2)
            with pe.Fori(0, DEPTH) as l:
                turn_x(1, l, 0)
                stack2_mixer(l)
                turn_x(1, l, 1)
                ffn(1, l, 0, 66, 1)

    return steps


_INS = ["x", "ffn1_norm", "ffn1_w_gate", "ffn1_w_up", "ffn1_w_down", "mix_norm", "w_in", "dn_conv", "dn_a_log",
        "dn_dt_bias", "dn_norm", "hy_conv", "hy_conv_bias", "hy_f_w1", "hy_f_b1", "hy_f_w2", "hy_f_b2", "hy_f_w3",
        "hy_f_b3", "hy_f_freq", "hy_f_wout", "hy_skip", "hy_norm", "w_out", "ffn2_norm", "ffn2_w_gate", "ffn2_w_up",
        "ffn2_w_down", "final_norm", "rel_bias_2", "norm_mix_g_2", "w_in_2", "b_gate_2", "da_q_norm_g_2",
        "da_k_norm_g_2", "da_lambda_2", "da_subln_g_2", "ret_norm_g_2", "sc_conv_w_2", "sc_conv_b_2",
        "w_branch_da_2", "w_branch_ret_2", "w_branch_sc_2", "w_out_2", "norm_ffn_g_2", "w_ffn_in_2", "ffn_conv_w_2",
        "ffn_conv_b_2", "w_ffn_out_2"]


def kernel(**inputs):
    import concourse.bacc as bacc
    from concourse.bass_utils import run_bass_kernel_spmd

    arrays = {n: np.ascontiguousarray(inputs[n]) for n in _INS}
    arrays |= {"c_" + n: np.ascontiguousarray(a) for n, a in constants().items()}
    arrays["c_dft"] = arrays["c_dft"].reshape(P, -1)
    count = {}
    for last in (False, True):
        nc = bacc.Bacc("TRN2", target_bir_lowering=False, num_devices=1)
        ins = {n: nc.dram_tensor("in_" + n, a.shape, mybir.dt.from_np(a.dtype), kind="ExternalInput").ap()
               for n, a in arrays.items()}
        out = nc.dram_tensor("out_x", (1, L, D), F32, kind="ExternalOutput").ap()
        count = emit(nc, ins, out, count)
    r = run_bass_kernel_spmd(nc, [{"in_" + n: a for n, a in arrays.items()}], core_ids=[0])
    return r.results[0]["out_x"]
```

```python
import math
from contextlib import ExitStack

import numpy as np

import concourse.bass as bass
import concourse.mybir as mybir

F32 = mybir.dt.float32
F32R = mybir.dt.float32r
I32 = mybir.dt.int32
F16 = mybir.dt.float16
ALU = mybir.AluOpType
ACT = mybir.ActivationFunctionType
AX_X = mybir.AxisListType.X

P = 128
D = 1024
L = 256
RB = L // P
KC = D // P
DEPTH = 2
FF = 2816
NF = FF // P
EPS = 1e-6
KB = 1024

HEADS, DIRS, DN = 4, 2, 512
HYW, EMB, HID = 512, 33, 64
CONV1, CONV_HY = 5, 3
D_IN = 4 * DN + 2 * DIRS * HEADS + 3 * HYW
COL_BA = 4 * DN
COL_HY = COL_BA + 2 * DIRS * HEADS
LEVELS = 7
DA_W, RET_W, SC_W = 512, 256, 256
IN2 = 3 * DA_W + 4 * RET_W + 3 * SC_W + 3 * D
BUCKETS, MAX_DIST = 32, 128
HK = 384
MASKED = -1e30

RAW, SLOTS = 3, 4
HALF = 1024
AHEAD = 3


def kinds1():
    ffn = ["A"] * (2 * NF) + ["B"] * NF
    return ffn + ["A"] * 28 + ["B"] * 8 + ffn


def kinds2():
    return ["A"] * 50 + ["B"] * 16 + ["A"] * (2 * NF) + ["B"] * NF


KIND1, KIND2 = kinds1(), kinds2()
H1, H2 = len(KIND1), len(KIND2)
assert H1 % (2 * RAW) == 0 and H1 % SLOTS == 0 and H2 % (2 * RAW) == 0 and H2 % SLOTS == 0


def constants():
    f8 = np.float64
    i, j = np.arange(P)[:, None], np.arange(P)[None, :]
    c = {}
    blockones = (i // 64 == j // 64)
    flip = (i + j == P - 1)
    rot = np.zeros((P, P))
    for d in range(P):
        if d % 64 < 32:
            rot[d + 32, d] = -1
        else:
            rot[d - 32, d] = 1
    mats = [np.eye(P), np.ones((P, P)), blockones, flip, rot, i <= j, i >= j]
    c["mats"] = np.stack(mats, 1).astype(np.float32)
    neg = np.stack([np.where(i <= j, 0, -60000.0), np.where(i >= j, 0, -60000.0)], 1)
    lev = []
    for d in range(DIRS):
        for b in range(LEVELS):
            s = 1 << b
            a = (i // s % 2 == 0) & (j // s == i // s + 1)
            lev.append(a if d == 0 else a.T)
    c["masks"] = np.concatenate([neg, np.stack(lev, 1)], 1).astype(np.float16)
    t, f = np.arange(L, dtype=f8)[:, None], np.arange(L, dtype=f8)[None, :]
    th = 2 * math.pi / (2 * L)
    nyq = np.where(f == 0, np.cos(math.pi * t), 0)
    def six(tt, sign, nq):
        co, si = np.cos(th * tt * f), -sign * np.sin(th * tt * f)
        si[:, 0] = 0
        con = co.copy()
        con[:, 0] = nq
        sin_n = si.copy()
        sin_n[:, 0] = nq
        return [co[:, :P], co[:, P:], si[:, :P], si[:, P:], con[:, :P], sin_n[:, :P]]
    fwd = np.stack(six(t, 1, np.cos(math.pi * t[:, 0])), 1)
    inv_re = np.cos(th * f.T * t.T) * np.where(f.T == 0, 1, 2) / (2 * L)
    inv_im = -np.sin(th * f.T * t.T) * 2 / (2 * L)
    inv_im[0] = np.cos(math.pi * t[:, 0]) / (2 * L)
    inv = np.concatenate([inv_re, inv_im], 0)
    lay = lambda a: a.reshape(a.shape[0] // P, P, -1).transpose(1, 0, 2)
    c["dft"] = np.concatenate([lay(fwd).reshape(P, -1), lay(inv).reshape(P, -1)], 1).astype(np.float32)
    tt = np.linspace(0.0, 1.0, L)[:, None]
    bands = (EMB - 1) // 2
    ang = (2 * math.pi / L) * t * np.linspace(1e-4, bands - 1, bands)[None]
    c["feats"] = np.concatenate([tt, np.cos(ang), -np.sin(ang)], 1).T.astype(np.float32).copy()
    deltas = np.abs(np.linspace(math.log(1e-2) / 1.5, math.log(1e-2) / 0.3, HYW))
    dec = np.exp(-tt * deltas)
    c["decay"] = lay(np.stack([dec, np.roll(dec, 1, 0)], 1)).reshape(P, RB, DIRS, HYW).astype(np.float32)
    inv_f = 10000.0 ** (-np.arange(32, dtype=f8) / 32)
    an = inv_f[np.arange(P) % 32][:, None] * np.arange(L)[None]
    co, si = np.cos(an), np.sin(an)
    c["rotary"] = np.stack([co, si, co / 8, si / 8], 1).astype(np.float32)
    lg = np.log(1.0 - 2.0 ** (-5.0 - np.arange(4)))
    dm = np.zeros((P, 4, 3 * P))
    for h in range(4):
        dg = np.where(j >= i, np.exp(lg[h] * np.maximum(j - i, 0)), 0)
        dm[:, h] = np.concatenate([dg, np.exp(lg[h] * (P + j - i)), dg], 1)
    c["retdecay"] = dm.astype(np.float32)
    n = np.arange(L)
    half = BUCKETS // 2
    large = half + (np.log(np.maximum(n, 1) / half) / math.log(MAX_DIST / half) * (BUCKETS - half)).astype(int)
    bucket = np.where(n < half, n, np.minimum(large, BUCKETS - 1))
    oh = np.zeros((BUCKETS, HK))
    oh[bucket[L - 1 - np.arange(L)], np.arange(L)] = 1
    c["onehot"] = oh.astype(np.float32)
    li = np.array([0.8 - 0.6 * math.exp(-0.3 * l) for l in range(DEPTH)])
    c["lam"] = np.stack([li, 1 - li], 1).astype(np.float32)
    return c


class Signal:

    def __init__(self, sem, per, start=0):
        self.sem, self.per, self.start = sem, per, start

    def due(self, l, k):
        return l * self.per + (self.start + k)


class Chain:

    def __init__(self, sem, start, per):
        self.sem, self.start, self.per, self.n = sem, start, per, 0

    def step(self, l):
        self.n += 1
        return l * self.per + (self.start + self.n)


def emit(nc, ins, out, count):
    steps = {}
    with ExitStack() as ctx:
        def sem(name):
            return ctx.enter_context(nc.semaphore(name))

        def sb(name, shape, dt=F32):
            return ctx.enter_context(nc.sbuf_tensor(name, shape, dt))

        def psum(name, shape):
            return ctx.enter_context(nc.psum_tensor(name, shape, F32))

        raw = sb("raw", [P, RAW, 2 * HALF])
        w_hi = sb("w_hi", [P, SLOTS, HALF], F32R)
        w_lo = sb("w_lo", [P, SLOTS, HALF], F32R)
        x = sb("x", [P, RB, D])
        xT_hi = sb("xT_hi", [P, KC, L], F32R)
        xT_lo = sb("xT_lo", [P, KC, L], F32R)
        gain = sb("gain", [P, D])
        mats = sb("mats", [P, 7, P])
        masks = sb("masks", [P, 2 + DIRS * LEVELS, P], F16)
        hankel = sb("hankel", [P, 4, L])
        rows = sb("rows", [P, P])
        cols = sb("cols", [P, P])
        relb = sb("relb", [BUCKETS, 4])
        stat = sb("stat", [P, 48])
        small = sb("small", [P, 400])
        w_ba = sb("w_ba", [P, KC, 16])
        wba_hi = sb("wba_hi", [P, KC, 16], F32R)
        wba_lo = sb("wba_lo", [P, KC, 16], F32R)
        ident, ones, blockones = mats[:, 0, :], mats[:, 1, :], mats[:, 2, :]
        flip, rot = mats[:, 3, :], mats[:, 4, :]
        cum = [mats[:, 5, :], mats[:, 6, :]]
        eps = stat[:, 0:1]
        eps64 = stat[:, 1:2]
        eps128 = stat[:, 2:3]
        ss = stat[:, 4:6]
        nv, ny, rstd = stat[:, 10:12], stat[:, 12:14], stat[:, 14:16]

        ARENA = 107 * KB
        slab = sb("slab", [P, ARENA // 4])
        at0 = nc.sbuf_base - ARENA

        def at(name, kb, shape, dt=F32):
            n = 4 * int(np.prod(shape[1:]))
            assert kb * KB + n <= ARENA, name
            return nc.alloc_sbuf_tensor_at(name, shape, dt, offset=at0 + int(kb * KB))

        hT_hi = at("hT_hi", 0, [P, NF, L], F32R)
        hT_lo = at("hT_lo", 22, [P, NF, L], F32R)
        sg = at("sg", 44, [P, 2, L])
        hfull = at("hfull", 46, [P, 2, L])
        xn = at("xn", 87, [P, RB, D])
        gconv = at("gconv", 48, [P, 2, L])
        spec = at("spec", 0, [P, 2, 5, HYW])
        filt = at("filt", 20, [P, RB, 4, HYW])
        qkvT = at("qkvT", 20, [P, 12, L])
        zT = at("zT", 32, [P, 4, L])
        hyT = at("hyT", 36, [P, 12, L])
        Ysp = at("Ysp", 36, [P, 4, HYW])
        ytmp = at("ytmp", 58, [P, 2, HYW])
        dft = at("dft", 48, [P, 2560])
        dft_f = dft[:, 0:1536].rearrange("p (r b f) -> p r b f", r=RB, b=6)
        dft_i = dft[:, 1536:2560].rearrange("p (b t) -> p b t", b=4)
        wfilt = at("wfilt", 63, [HID, 4 * HYW])
        decay = at("decay", 71, [P, RB, DIRS, HYW])
        even = at("even", 36, [P, RB, 2, HYW])
        hynat = at("hynat", 63, [P, RB, 3, HYW])
        featsT = at("featsT", 99.0, [EMB, L])
        fw = at("fw", 100.0, [HID, 4, HID])
        hdn = at("hdn", 105.0, [HID, L + 1])
        farg = at("farg", 102.0, [HID, 2, L])
        skip = at("skip", 83, [P, 2, HYW])
        zz = at("zz", 103, [P, RB, HYW])
        knat = at("knat", 75, [P, RB, HEADS, P])
        vnat = at("vnat", 79, [P, RB, HEADS, P])
        sq = at("sq", 87, [P, 8, L])
        rr = at("rr", 95, [P, 8, L])
        attnT = at("attnT", 83, [P, 4, 4, P])
        DT = at("DT", 91, [P, 4, 4, P])
        MT = at("MT", 0, [P, 4, 4, P])
        T = at("T", 8, [P, 4, 4, P])
        U = at("U", 36, [P, 4, 4, P])
        Pp = at("Pp", 63, [P, 4, 4, P])
        Mm = [at("Mm_even", 99, [P, 4, 4, P]), at("Mm_odd", 91, [P, 4, 4, P])]
        qdecT = at("qdecT", 44, [P, 2, 4, P])
        v1 = at("v1", 16, [P, 2, 4, P])
        kdec = at("kdec", 63, [P, 2, 4, P])
        Sst = at("Sst", 67, [P, 2, 4, P])
        Rr = at("Rr", 71, [P, 2, 4, P])
        v2 = at("v2", 0, [P, 2, 4, P])
        osq = at("osq", 4, [P, 4, L])
        orr = at("orr", 8, [P, 4, L])
        oy = at("oy", 12, [P, 4, L])
        brow = at("brow", 79, [4, HK])
        onehot = at("onehot", 80.5, [BUCKETS, HK])
        gates = at("gates", 0, [P, 24, L])
        qkT = at("qkT", 24, [P, 8, L])
        v_da = at("v_da", 32, [P, RB, DA_W])
        rqk = at("rqk", 36, [P, 4, L])
        rqkr = at("rqkr", 40, [P, 4, L])
        v_ret = at("v_ret", 44, [P, RB, RET_W])
        rg = at("rg", 46, [P, 2, L])
        rgs = at("rgs", 48, [P, 2, L])
        scb = at("scb", 50, [P, 2, L])
        scc = at("scc", 52, [P, 2, L])
        scx = at("scx", 54, [P, 2, L])
        sco = at("sco", 56, [P, 2, L])
        rtmp = at("rtmp", 58, [P, 2, L])
        prob = at("prob", 60, [P, 8, 3 * P])
        aT = at("aT", 72, [P, 4, 3 * P])
        iT = [at(f"iT{h}", (104, 105.5, 36, 37.5)[h], [P, 3 * P]) for h in range(4)]
        sq2 = at("sq2", 84, [P, 8, L])
        rr2 = at("rr2", 92, [P, 8, L])
        rotary = at("rotary", 100, [P, 4, L])
        retdecay = at("retdecay", 78, [P, 4, 3 * P])
        daT_hi = at("daT_hi", 60, [P, 4, L], F32R)
        daT_lo = at("daT_lo", 64, [P, 4, L], F32R)
        yT_hi = at("yT_hi", 60, [P, KC, L], F32R)
        yT_lo = at("yT_lo", 68, [P, KC, L], F32R)
        yacc = at("yacc", 84, [P, KC, L])
        ytm = at("ytm", 92, [P, 2, L])

        psA = psum("psA", [P, 4, 512])
        psB = psum("psB", [P, 4, 512])

        def pair(name, per1, per2, start=0, between=0):
            h = sem(name)
            return (Signal(h, per1, start), Signal(h, per2, start + DEPTH * per1 + between))

        raw_loaded = [pair(f"raw_loaded{i}", H1 // 2 // RAW * 16, H2 // 2 // RAW * 16) for i in range(RAW)]
        hi_done = pair("hi_done", H1, H2)
        lo_done = pair("lo_done", H1, H2, start=2 * RAW)
        half_used = pair("half_used", H1, H2, start=SLOTS)
        x_loaded = sem("x_loaded")
        x_ready = pair("x_ready", 12, 8, start=4, between=4)
        first_rows = pair("first_rows", 3, 2)
        gain_loaded = pair("gain_loaded", 48, 32, between=16)
        param_loaded = sem("param_loaded")
        const_loaded = sem("const_loaded")
        tables_loaded = sem("tables_loaded")
        bias_loaded = sem("bias_loaded")
        bias_mm = sem("bias_mm")
        hankel_loaded = sem("hankel_loaded")
        bias_row = sem("bias_row")
        bias_stored = sem("bias_stored")
        setup = sem("setup")
        out_stored = sem("out_stored")
        n_ss = pair("norm_squares", 6, 4, between=2)
        n_xn = pair("norm_scaled", 12, 8, start=1, between=4)
        n_tp = pair("norm_turned", 12, 8)
        n_hi = pair("norm_hi", 12, 8)
        n_lo = pair("norm_lo", 12, 8)
        f_conv = pair("ffn_conv", 0, NF)
        f_act = pair("ffn_silu", 2 * NF, NF)
        f_prod = pair("ffn_product", 2 * NF, NF)
        f_hi = pair("ffn_hi", 2 * NF, NF)
        f_lo = pair("ffn_lo", 2 * NF, NF)

        def one_stack(per):
            return {k: Signal(sem(k), n) for k, n in per.items()}

        NPAR1, NPAR2 = 20, 14
        s1 = one_stack(dict(
            cols_tp=1, cols=1, wba=1, mlp_mm=3, mlp_arg=3, mlp_sin=3, filt_mm=8, filt=8, even=4, odd=4, spec_mm=10, spec=10,
            conv_mid=24, conv=24, qkv_silu=12, z_out=4, z_silu=1, ba_mm=1, ba_out=1, hy_turned=6, hy_nat=6,
            z_mm=8, y_spec=4, inv_mm=4, zz=4, hy_ss=2, hy_zn=1, hy_back=2, y_hi=5, y_lo=5,
            qk_sq=1, qk_mm=1, qk_root=1, qk_norm=1, kv_turned=4, kv_nat=4,
            g_arg=1, g_exp=1, g_sum=1, g_ln=1, g_ready=1, g_cum=1, g_col=1, g_decays=1, g_neg=1,
            row_mm=4, row_arg=4, row_exp=4, q_exp=2, q_dec=2, kk_mm=1, attn=4, mt=4,
            masked=28, p_mm=28, p_copy=24, tp_mm=24, t_new=24, u_tp=20, u_act=20, u_new=8,
            v1_mm=2, v1=2, k_dec=2, s_mm=2, s_copy=2, ks_mm=2, rest=2, v2_mm=2, v2=2, o_mm=2,
            o_sq=1, o_ss=1, o_root=1, o_y=1))
        s2 = one_stack(dict(
            cols2_tp=1, cols2=1, lam_sum=1, lam_exp=1, lam=1, ev_act=14, ev_dve=33, rg_sig=1, gate_sig=3, sc_y=1,
            a_sq=1, a_mm=1, a_root=1, a_qk=1, rot_mm=1, rot=1, sc_mm=8, sc_max=8, sc_exp=8, sc_a=4,
            a_turned=4, a_copy=4, oa_mm=2, oa_sq=1, oa_ss=1, out_root=1, oa_y=1,
            rs_mm=4, rs_dec=4, or_mm=1, or_sq=1, or_ss=1, or_y=1,
            o_hi=3, o_lo=2, br=24, y_sum=8, yb_hi=8, yb_lo=8))

        def chain(name):
            h = sem(name)
            n1, n2, mid = count.get(name, (1, 1, 0))
            return (Chain(h, 0, n1), Chain(h, DEPTH * n1 + mid, n2), Chain(h, DEPTH * n1, 0))

        act_chain, dve_chain = chain("act_chain"), chain("dve_chain")

        def raw_half(s, kind):
            u = raw[:, (s // 2) % RAW, :]
            if kind == "A":
                return u.rearrange("p (c n) -> p c n", c=KC)[:, :, (s % 2) * P:(s % 2 + 1) * P]
            return u[:, (s % 2) * HALF:(s % 2 + 1) * HALF]

        def split_half(t, s, kind):
            v = t[:, s % SLOTS, :]
            return v.rearrange("p (c n) -> p c n", c=KC) if kind == "A" else v

        def product(o, a_hi, a_lo, b_hi, b_lo, start, stop, skip=False):
            nc.tensor.matmul(o, a_lo, b_hi, start=start, stop=False, skip_group_check=skip)
            nc.tensor.matmul(o, a_hi, b_lo, start=False, stop=False, skip_group_check=skip)
            return nc.tensor.matmul(o, a_hi, b_hi, start=False, stop=stop, skip_group_check=skip)

        def layer(ap, l):
            v = ap[bass.ds(l, 1)]
            return v.rearrange("o a -> (o a)") if len(ap.shape) == 2 else v.rearrange("o a b -> (o a) b")

        scratch = nc.dram_tensor("bias_rows", (4, HK), F32, kind="Internal").ap()
        block = ctx.enter_context(nc.Block())

        @block.sync
        def _(sp):
            def unit(l, st, u, src):
                sp.wait_ge(lo_done[st].sem, lo_done[st].due(l, 2 * u + 2 - 2 * RAW))
                dst = raw[:, u % RAW, :].rearrange("p (c n) -> p c n", c=src.shape[1])
                sp.dma_start(dst, src).then_inc(raw_loaded[u % RAW][st].sem, 16)

            def columns(w, l, c0):
                return w[bass.ds(l, 1), :, c0:c0 + 2 * P].rearrange("o (c p) n -> p (o c) n", p=P)

            def two_rows(w, l, r0):
                return w[bass.ds(l, 1), r0:r0 + 2 * P, :].rearrange("o (c p) n -> p (o c) n", p=P)

            def param(dst, src):
                sp.dma_start(dst, src).then_inc(param_loaded, 16)

            def load_gain(st, l, q, w):
                sp.wait_ge(n_xn[st].sem, n_xn[st].due(l, 4 * q))
                sp.dma_start(gain[:, :], layer(w, l).partition_broadcast(P)).then_inc(gain_loaded[st].sem, 16)

            def ffn_units(st, l, u0, wg, wu, wd, up0=0, next_gain=None):
                for j in range(NF // 2):
                    unit(l, st, u0 + 2 * j, columns(wg, l, 2 * P * j))
                    unit(l, st, u0 + 2 * j + 1, columns(wu, l, up0 + 2 * P * j))
                    if st == 0 and u0 == 0 and j == 0:
                        layer_params1(l)
                    if next_gain is not None and j == 4:
                        load_gain(st, l, 1, next_gain)
                for j in range(NF // 2):
                    unit(l, st, u0 + NF + j, two_rows(wd, l, 2 * P * j))

            def layer_params1(l):
                load_gain(0, l, 0, ins["ffn1_norm"])
                param(rows[0:60, :], ins["dn_conv"][bass.ds(l, 1)].rearrange("o k (b p) -> (o k b) p", p=P))
                param(rows[60:96, :], ins["hy_conv"][bass.ds(l, 1)].rearrange("o k (b p) -> (o k b) p", p=P))
                param(rows[96:108, :], layer(ins["hy_conv_bias"], l).rearrange("(b p) -> b p", p=P))
                param(rows[108:109, :], ins["dn_norm"][bass.ds(l, 1)])
                param(rows[109:113, :], layer(ins["hy_norm"], l).rearrange("(b p) -> b p", p=P))
                for n, name in enumerate(("hy_f_b1", "hy_f_b2", "hy_f_b3", "hy_f_freq")):
                    param(rows[113 + n:114 + n, 0:HID], ins[name][bass.ds(l, 1)])
                param(fw[0:EMB, 0, :], layer(ins["hy_f_w1"], l))
                param(fw[:, 1, :], layer(ins["hy_f_w2"], l))
                param(fw[:, 2, :], layer(ins["hy_f_w3"], l))
                param(fw[:, 3, :], layer(ins["hy_f_w2"], l))
                param(featsT[:, :], ins["c_feats"])
                param(wfilt[:, :], layer(ins["hy_f_wout"], l))
                param(decay[:, :, :], ins["c_decay"])
                param(w_ba[:, :, :], ins["w_in"].rearrange("l k n -> (l k) n")[bass.ds(l * D, D), COL_BA:COL_HY]
                      .rearrange("(c p) n -> p c n", p=P))
                param(small[:, 0:8], ins["dn_a_log"][bass.ds(l, 1)].rearrange("o d h -> (o d h)").partition_broadcast(P))
                param(small[:, 8:16], ins["dn_dt_bias"][bass.ds(l, 1)].rearrange("o d h -> (o d h)").partition_broadcast(P))
                param(skip[:, :, :], ins["hy_skip"][bass.ds(l, 1)].rearrange("o a c -> (o a) c").partition_broadcast(P))

            def layer_params2(l):
                load_gain(1, l, 0, ins["norm_mix_g_2"])
                for n, name in enumerate(("da_q_norm_g_2", "da_k_norm_g_2", "ret_norm_g_2")):
                    for m in range(2):
                        param(rows[n:n + 1, 64 * m:64 * m + 64], ins[name][bass.ds(l, 1)])
                param(rows[3:4, :], ins["da_subln_g_2"][bass.ds(l, 1)])
                param(rows[4:10, :], ins["sc_conv_w_2"][bass.ds(l, 1)].rearrange("o k (b p) -> (o k b) p", p=P))
                param(rows[10:12, :], layer(ins["sc_conv_b_2"], l).rearrange("(b p) -> b p", p=P))
                param(rows[12:36, :], layer(ins["b_gate_2"], l).rearrange("(b p) -> b p", p=P))
                param(rows[36:102, :], ins["ffn_conv_w_2"][bass.ds(l, 1)].rearrange("o k (b p) -> (o k b) p", p=P))
                param(rows[102:124, :], layer(ins["ffn_conv_b_2"], l).rearrange("(b p) -> b p", p=P))
                param(small[:, 0:256], ins["da_lambda_2"][bass.ds(l, 1)].rearrange("o a d -> (o a d)").partition_broadcast(P))
                param(stat[:, 24:26], layer(ins["c_lam"], l).partition_broadcast(P))

            xin = ins["x"].rearrange("o (r p) d -> p (o r) d", p=P)
            sp.dma_start(x[:, :, :], xin).then_inc(x_loaded, 16)
            sp.dma_start(relb[:, :], ins["rel_bias_2"]).then_inc(bias_loaded, 16)
            sp.dma_start(onehot[:, :], ins["c_onehot"]).then_inc(bias_loaded, 16)
            sp.dma_start(mats[:, :, :], ins["c_mats"]).then_inc(const_loaded, 16)
            sp.wait_ge(setup, 1)
            with sp.Fori(0, DEPTH) as l:
                ffn_units(0, l, 0, ins["ffn1_w_gate"], ins["ffn1_w_up"], ins["ffn1_w_down"],
                          next_gain=ins["mix_norm"])
                order = [COL_HY + 2 * P * i for i in range(6)] + [2 * P * i for i in range(6)] \
                    + [3 * DN + 2 * P * i for i in range(2)]
                for i, c0 in enumerate(order):
                    if c0 == 0:
                        by_block = ins["w_in"].rearrange("l (c p) n -> (l c) p n", p=P)
                        unit(l, 0, 33 + i, by_block[bass.ds(l * KC, KC), :, 0:2 * P].rearrange("c p n -> p c n"))
                    else:
                        unit(l, 0, 33 + i, columns(ins["w_in"], l, c0))
                    if i == 4:
                        load_gain(0, l, 2, ins["ffn2_norm"])
                w_out = ins["w_out"].rearrange("l (u c p) n -> (l u) p c n", c=2, p=P)
                for i, u in enumerate((2, 3, 0, 1)):
                    unit(l, 0, 47 + i, w_out[bass.ds(l * 4 + u, 1)].rearrange("o p c n -> (o p) c n"))
                ffn_units(0, l, 51, ins["ffn2_w_gate"], ins["ffn2_w_up"], ins["ffn2_w_down"])
            sp.wait_ge(n_xn[0].sem, n_xn[0].due(DEPTH, 0))
            sp.dma_start(gain[:, :], ins["final_norm"].partition_broadcast(P)).then_inc(gain_loaded[0].sem, 16)
            sp.wait_ge(x_ready[0].sem, x_ready[0].due(DEPTH - 1, 8))
            sp.dma_start(rotary[:, :, :], ins["c_rotary"]).then_inc(const_loaded, 16)
            sp.dma_start(retdecay[:, :, :], ins["c_retdecay"]).then_inc(const_loaded, 16)
            with sp.Fori(0, DEPTH) as l:
                for i in range(25):
                    unit(l, 1, i, columns(ins["w_in_2"], l, 2 * P * i))
                    if i == 1:
                        layer_params2(l)
                    if i == 6:
                        load_gain(1, l, 1, ins["norm_ffn_g_2"])
                for i in range(2):
                    unit(l, 1, 25 + i, two_rows(ins["w_branch_da_2"], l, 2 * P * i))
                unit(l, 1, 27, two_rows(ins["w_branch_ret_2"], l, 0))
                unit(l, 1, 28, two_rows(ins["w_branch_sc_2"], l, 0))
                for i in range(4):
                    unit(l, 1, 29 + i, two_rows(ins["w_out_2"], l, 2 * P * i))
                ffn_units(1, l, 33, ins["w_ffn_in_2"], ins["w_ffn_in_2"], ins["w_ffn_out_2"], up0=FF)
            sp.wait_ge(x_ready[1].sem, x_ready[1].due(DEPTH - 1, 8))
            sp.dma_start(out.rearrange("o (r p) d -> p (o r) d", p=P), x[:, :, :]).then_inc(out_stored, 16)
            sp.wait_ge(out_stored, 16)

        @block.scalar
        def _(act):
            A = nc.scalar.activation

            def round_half(st, l, n):
                kinds = (KIND1, KIND2)[st]
                if n >= len(kinds):
                    return
                if n % 2 == 0:
                    arrived = raw_loaded[n // 2 % RAW][st]
                    act.wait_ge(arrived.sem, arrived.due(l, 16 * (n // 2 // RAW + 1)))
                act.wait_ge(half_used[st].sem, half_used[st].due(l, n + 1 - SLOTS))
                A(split_half(w_hi, n, kinds[n]), raw_half(n, kinds[n]), ACT.Copy).then_inc(hi_done[st].sem, 1)

            def root(l, ch, dst, src, scale, bias):
                A(dst, src, ACT.Ln, scale=scale, bias=bias).then_inc(ch.sem, 1)
                act.wait_ge(ch.sem, ch.step(l))
                return A(dst, dst, ACT.Exp, scale=-0.5)

            def norm_stats(st, l, x0):
                for rb in range(RB):
                    act.wait_ge(x_ready[st].sem, x_ready[st].due(l, x0 + 2 * (rb + 1)))
                    A(xn[:, rb, :], x[:, rb, :], ACT.Square, accum_out=ss[:, rb:rb + 1]).then_inc(n_ss[st].sem, 1)

            def norm_out(st, l, q):
                for i in range(4):
                    act.wait_ge(n_tp[st].sem, n_tp[st].due(l, 4 * q + i + 1))
                    A(xT_hi[:, 2 * i:2 * i + 2, :], psA[:, i, :].rearrange("p (c n) -> p c n", c=2),
                      ACT.Copy).then_inc(n_hi[st].sem, 1)

            def ffn(st, l, f, s0):
                for j in range(NF // 2):
                    for i in range(2):
                        n = 2 * j + i
                        round_half(st, l, s0 + 4 * j + i + AHEAD)
                        if st == 0:
                            act.wait_ge(half_used[st].sem, half_used[st].due(l, s0 + 4 * j + i + 1))
                            A(sg[:, i, :], psA[:, i, 0:L], ACT.Silu).then_inc(f_act[st].sem, 1)
                        else:
                            act.wait_ge(f_conv[st].sem, f_conv[st].due(l, NF * f + n + 1))
                            A(sg[:, i, :], gconv[:, i, :], ACT.Silu).then_inc(f_act[st].sem, 1)
                    for i in range(2):
                        n = 2 * j + i
                        round_half(st, l, s0 + 4 * j + 2 + i + AHEAD)
                        act.wait_ge(f_prod[st].sem, f_prod[st].due(l, NF * f + n + 1))
                        A(hT_hi[:, n, :], hfull[:, i, :], ACT.Copy).then_inc(f_hi[st].sem, 1)
                    if st == 0 and f == 0 and j in (2, 4, 6):
                        mlp_sin(l, j // 2 - 1)
                for k in range(NF):
                    round_half(st, l, s0 + 2 * NF + k + AHEAD)

            def mlp_sin(l, k):
                act.wait_ge(s1["mlp_arg"].sem, s1["mlp_arg"].due(l, k + 1))
                A(hdn[:, 1:L + 1], farg[:, 0, :], ACT.Sin).then_inc(s1["mlp_sin"].sem, 1)

            def stack1_mixer(l):
                ch = act_chain[0]
                g = lambda a, b: small[:, a:b]
                for k in range(10):
                    act.wait_ge(s1["spec_mm"].sem, s1["spec_mm"].due(l, k + 1))
                    A(spec[:, k // 5, k % 5, :], psA[:, k % 4, :], ACT.Copy).then_inc(s1["spec"].sem, 1)
                norm_out(0, l, 1)
                for i in range(28):
                    round_half(0, l, 66 + i + AHEAD)
                    if i < 24:
                        act.wait_ge(half_used[0].sem, half_used[0].due(l, 66 + i + 1))
                        if i < 12:
                            A(hyT[:, i, :], psA[:, i % 3, 0:L], ACT.Identity, scale=cols[:, 72 + i:73 + i], bias=cols[:, 96 + i:97 + i])\
                                .then_inc(s1["conv_mid"].sem, 1)
                        else:
                            b = i - 12
                            A(qkvT[:, b, :], psA[:, i % 3, 0:L], ACT.Copy, scale=cols[:, 24 + b:25 + b]).then_inc(s1["conv_mid"].sem, 1)
                    for k in {6: (0, 1), 10: (2, 3), 14: (4,), 15: (5,)}.get(i, ()):
                        act.wait_ge(s1["hy_turned"].sem, s1["hy_turned"].due(l, k + 1))
                        ps = psB[:, k, :] if k < 4 else psA[:, 3, :]
                        A(hynat[:, k % 2, k // 2, :], ps, ACT.Copy).then_inc(s1["hy_nat"].sem, 1)
                    if 13 <= i < 25:
                        act.wait_ge(s1["conv"].sem, s1["conv"].due(l, i))
                        A(qkvT[:, i - 13, :], qkvT[:, i - 13, :], ACT.Silu).then_inc(s1["qkv_silu"].sem, 1)
                    if i == 21:
                        act.wait_ge(s1["qkv_silu"].sem, s1["qkv_silu"].due(l, 8))
                        A(sq[:, :, :], qkvT[:, 0:8, :], ACT.Square).then_inc(s1["qk_sq"].sem, 1)
                    if i >= 24:
                        act.wait_ge(half_used[0].sem, half_used[0].due(l, 66 + i + 1))
                        A(zT[:, i - 24, :], psA[:, i % 3, 0:L], ACT.Copy).then_inc(s1["z_out"].sem, 1)
                    if i == 18:
                        for rb in range(RB):
                            act.wait_ge(s1["zz"].sem, s1["zz"].due(l, 2 + rb + 1))
                            A(ytmp[:, rb, :], zz[:, rb, :], ACT.Square, accum_out=g(288 + rb, 289 + rb)).then_inc(s1["hy_ss"].sem, 1)
                    if i == 25:
                        act.wait_ge(s1["g_arg"].sem, s1["g_arg"].due(l, 1))
                        A(g(168, 184).rearrange("p (r n) -> p r n", r=RB),
                          g(304, 336).rearrange("p (r n) -> p r n", r=RB)[:, :, 0:8], ACT.Exp, scale=-1.0)
                        A(g(48, 64), g(32, 48), ACT.Exp, scale=-1.0)
                        A(g(280, 288), g(0, 8), ACT.Exp).then_inc(s1["g_exp"].sem, 1)
                        act.wait_ge(s1["qk_mm"].sem, s1["qk_mm"].due(l, 1))
                        A(rr[:, 0:4, :], psB[:, 0:2, :].rearrange("p a (b n) -> p (a b) n", b=2), ACT.Ln, scale=float(P), bias=eps128)
                        A(rr[:, 4:8, :], psB[:, 2:4, :].rearrange("p a (b n) -> p (a b) n", b=2), ACT.Ln, bias=eps).then_inc(ch.sem, 1)
                        act.wait_ge(ch.sem, ch.step(l))
                        act.wait_ge(s1["g_sum"].sem, s1["g_sum"].due(l, 1))
                        A(g(80, 96), g(64, 80), ACT.Ln).then_inc(s1["g_ln"].sem, 1)
                        A(rr[:, :, :], rr[:, :, :], ACT.Exp, scale=-0.5).then_inc(s1["qk_root"].sem, 1)
                round_half(0, l, 94 + AHEAD)
                for b in range(4):
                    if b % 2 == 0:
                        act.wait_ge(s1["hy_back"].sem, s1["hy_back"].due(l, b // 2 + 1))
                    A(xT_hi[:, 4 + b, :], psA[:, 1 + b // 2 * 2, (b % 2) * L:(b % 2 + 1) * L], ACT.Copy,
                      scale=cols[:, 109 + b:110 + b]).then_inc(s1["y_hi"].sem, 1)
                for k in range(4):
                    act.wait_ge(s1["kv_turned"].sem, s1["kv_turned"].due(l, k + 1))
                    dst = (knat, vnat)[k // 2]
                    A(dst[:, k % 2, :, :], psB[:, k, :].rearrange("p (h n) -> p h n", h=4), ACT.Copy).then_inc(s1["kv_nat"].sem, 1)
                act.wait_ge(s1["g_decays"].sem, s1["g_decays"].due(l, 1))
                A(g(232, 248), g(216, 232), ACT.Exp)
                A(g(248, 264), g(200, 216), ACT.Exp).then_inc(s1["g_col"].sem, 1)
                for d in range(DIRS):
                    c1 = 1 - d
                    act.wait_ge(s1["row_arg"].sem, s1["row_arg"].due(l, 2 * d + c1 + 1))
                    A(qdecT[:, d, :, :], psA[:, 2 * d + c1, :].rearrange("p (h n) -> p h n", h=4), ACT.Exp).then_inc(s1["q_exp"].sem, 1)
                for k in range(4):
                    act.wait_ge(s1["row_arg"].sem, s1["row_arg"].due(l, k + 1))
                    A(DT[:, k, :, :], DT[:, k, :, :], ACT.Exp).then_inc(s1["row_exp"].sem, 1)
                for b in range(1, LEVELS):
                    for k in range(4):
                        if b > 1:
                            act.wait_ge(s1["u_tp"].sem, s1["u_tp"].due(l, 4 * (b - 2) + k + 1))
                            A(U[:, k, :, :], psA[:, k, :].rearrange("p (h n) -> p h n", h=4), ACT.Copy).then_inc(s1["u_act"].sem, 1)
                        act.wait_ge(s1["p_mm"].sem, s1["p_mm"].due(l, 4 * b + k + 1))
                        A(Pp[:, k, :, :], psB[:, k, :].rearrange("p (h n) -> p h n", h=4), ACT.Copy).then_inc(s1["p_copy"].sem, 1)
                    if b == 3:
                        act.wait_ge(s1["z_out"].sem, s1["z_out"].due(l, 4))
                        A(zT[:, :, :], zT[:, :, :], ACT.Silu).then_inc(s1["z_silu"].sem, 1)
                for d in range(DIRS):
                    act.wait_ge(s1["s_mm"].sem, s1["s_mm"].due(l, d + 1))
                    A(Sst[:, d, :, :], psA[:, 2 + d, :].rearrange("p (h n) -> p h n", h=4), ACT.Copy).then_inc(s1["s_copy"].sem, 1)
                for k in range(1, 5):
                    round_half(0, l, 94 + k + AHEAD)
                act.wait_ge(s1["o_mm"].sem, s1["o_mm"].due(l, 2))
                oT = psA[:, 0:2, :].rearrange("p a (b n) -> p (a b) n", b=2)
                A(osq[:, :, :], oT, ACT.Square).then_inc(s1["o_sq"].sem, 1)
                act.wait_ge(s1["o_ss"].sem, s1["o_ss"].due(l, 1))
                root(l, ch, orr[:, :, :], psA[:, 2:4, :].rearrange("p a (b n) -> p (a b) n", b=2), 1.0 / P, eps).then_inc(s1["o_root"].sem, 1)
                act.wait_ge(s1["o_y"].sem, s1["o_y"].due(l, 1))
                A(xT_hi[:, 0:4, :], oy[:, :, :], ACT.Copy).then_inc(s1["y_hi"].sem, 1)
                for k in range(5, 8):
                    round_half(0, l, 94 + k + AHEAD)

            def exp_scores(l, k):
                act.wait_ge(s2["sc_max"].sem, s2["sc_max"].due(l, k + 1))
                ps = psB[:, (k + 2) % 4, :]
                for q, (a, z) in enumerate(((0, L), (L, 3 * P))):
                    n = 2 * k + q
                    ins_ = A(prob[:, k, a:z], ps[:, a:z], ACT.Exp, bias=small[:, 320 + n:321 + n], accum_out=small[:, 336 + n:337 + n])
                ins_.then_inc(s2["sc_exp"].sem, 1)

            def stack2_mixer(l):
                ch = act_chain[1]
                act.wait_ge(s2["cols2"].sem, s2["cols2"].due(l, 1))
                projected = [i for i in range(50) if i not in (9, 11, 17)]
                for i in range(50):
                    round_half(1, l, i + AHEAD)
                    if i < 8 or 12 <= i < 16 or 22 <= i < 24:
                        act.wait_ge(half_used[1].sem, half_used[1].due(l, i + 1))
                        dst = qkT[:, i, :] if i < 8 else rqk[:, i - 12, :] if i < 16 else scc[:, i - 22, :]
                        A(dst, psA[:, projected.index(i) % 2, 0:L], ACT.Copy).then_inc(s2["ev_act"].sem, 1)
                    if i == 8:
                        act.wait_ge(s2["ev_act"].sem, s2["ev_act"].due(l, 8))
                        A(sq2[:, :, :], qkT[:, :, :], ACT.Square).then_inc(s2["a_sq"].sem, 1)
                    if i == 12:
                        act.wait_ge(s2["a_mm"].sem, s2["a_mm"].due(l, 1))
                        A(rr2[:, 0:4, :], psB[:, 0:2, :].rearrange("p a (b n) -> p (a b) n", b=2), ACT.Ln, bias=eps64)
                        A(rr2[:, 4:8, :], psB[:, 2:4, :].rearrange("p a (b n) -> p (a b) n", b=2), ACT.Ln, scale=1.0 / 64,
                          bias=eps).then_inc(ch.sem, 1)
                        act.wait_ge(ch.sem, ch.step(l))
                    if i == 13:
                        A(rr2[:, :, :], rr2[:, :, :], ACT.Exp, scale=-0.5).then_inc(s2["a_root"].sem, 1)
                        act.wait_ge(s2["lam_sum"].sem, s2["lam_sum"].due(l, 1))
                        A(stat[:, 28:30], stat[:, 26:28], ACT.Exp).then_inc(s2["lam_exp"].sem, 1)
                    for k in {26: (0, 1), 27: (2, 3), 29: (4, 5), 30: (6, 7)}.get(i, ()):
                        exp_scores(l, k)
                    if 33 <= i < 37:
                        h = i - 33
                        act.wait_ge(s2["a_turned"].sem, s2["a_turned"].due(l, h + 1))
                        A(aT[:, h, :], psB[:, (h + 2) % 4, 0:3 * P], ACT.Copy).then_inc(s2["a_copy"].sem, 1)
                    if i == 35:
                        act.wait_ge(s2["or_mm"].sem, s2["or_mm"].due(l, 1))
                        A(sq2[:, 4:6, :], psA[:, 2, :].rearrange("p (b n) -> p b n", b=2), ACT.Square).then_inc(s2["or_sq"].sem, 1)
                    if i == 39:
                        act.wait_ge(s2["oa_mm"].sem, s2["oa_mm"].due(l, 2))
                        A(sq2[:, 0:4, :], psB[:, 2:4, :].rearrange("p a (b n) -> p (a b) n", b=2), ACT.Square).then_inc(s2["oa_sq"].sem, 1)
                    if i == 41:
                        act.wait_ge(s2["or_ss"].sem, s2["or_ss"].due(l, 1))
                        act.wait_ge(s2["oa_ss"].sem, s2["oa_ss"].due(l, 1))
                        A(rr2[:, 4:6, :], psA[:, 3, :].rearrange("p (b n) -> p b n", b=2), ACT.Ln, scale=1.0 / 64, bias=eps)
                        A(rr2[:, 0:4, :], psB[:, 0:2, :].rearrange("p a (b n) -> p (a b) n", b=2), ACT.Ln, scale=1.0 / P, bias=eps)\
                            .then_inc(ch.sem, 1)
                        act.wait_ge(ch.sem, ch.step(l))
                        A(rr2[:, 0:6, :], rr2[:, 0:6, :], ACT.Exp, scale=-0.5).then_inc(s2["out_root"].sem, 1)
                    if i == 42:
                        act.wait_ge(s2["ev_dve"].sem, s2["ev_dve"].due(l, 5))
                        A(rgs[:, :, :], rg[:, :, :], ACT.Sigmoid).then_inc(s2["rg_sig"].sem, 1)
                    if i in (43, 44):
                        r = i - 43
                        act.wait_ge(s2["ev_dve"].sem, s2["ev_dve"].due(l, 9 + 8 * r + 8))
                        A(gates[:, 8 * r:8 * r + 8, :], gates[:, 8 * r:8 * r + 8, :], ACT.Sigmoid).then_inc(s2["gate_sig"].sem, 1)
                    if i == 46:
                        act.wait_ge(s2["oa_y"].sem, s2["oa_y"].due(l, 1))
                        A(daT_hi[:, :, :], rr2[:, 0:4, :], ACT.Copy).then_inc(s2["o_hi"].sem, 1)
                act.wait_ge(half_used[1].sem, half_used[1].due(l, 50))
                act.wait_ge(s2["or_y"].sem, s2["or_y"].due(l, 1))
                A(xT_hi[:, 4:6, :], rr2[:, 4:6, :], ACT.Copy).then_inc(s2["o_hi"].sem, 1)
                A(xT_hi[:, 6:8, :], sco[:, :, :], ACT.Copy).then_inc(s2["o_hi"].sem, 1)
                act.wait_ge(s2["ev_dve"].sem, s2["ev_dve"].due(l, 33))
                A(gates[:, 16:24, :], gates[:, 16:24, :], ACT.Sigmoid).then_inc(s2["gate_sig"].sem, 1)
                for k in range(8):
                    round_half(1, l, 50 + k + AHEAD)
                for n in range(KC):
                    act.wait_ge(s2["y_sum"].sem, s2["y_sum"].due(l, n + 1))
                    A(yT_hi[:, n, :], yacc[:, n, :], ACT.Copy).then_inc(s2["yb_hi"].sem, 1)
                for k in range(8):
                    round_half(1, l, 58 + k + AHEAD)

            act.wait_ge(setup, 1)
            with act.Fori(0, DEPTH) as l:
                norm_stats(0, l, -4)
                for n in range(AHEAD):
                    round_half(0, l, n)
                norm_out(0, l, 0)
                ffn(0, l, 0, 0)
                norm_stats(0, l, 0)
                stack1_mixer(l)
                norm_stats(0, l, 4)
                norm_out(0, l, 2)
                ffn(0, l, 1, 102)
            steps["act_chain"] = [act_chain[0].n, 0, 0]
            norm_stats(0, DEPTH - 1, 8)
            with act.Fori(0, DEPTH) as l:
                norm_stats(1, l, -4)
                for n in range(AHEAD):
                    round_half(1, l, n)
                norm_out(1, l, 0)
                stack2_mixer(l)
                norm_stats(1, l, 0)
                norm_out(1, l, 1)
                ffn(1, l, 0, 66)
            steps["act_chain"][1] = act_chain[1].n

        @block.gpsimd
        def _(pool):
            pool.sem_inc(lo_done[0].sem, 2 * RAW)
            pool.dma_start(masks[:, :, :], ins["c_masks"]).then_inc(tables_loaded, 16)
            pool.dma_start(dft[:, :], ins["c_dft"]).then_inc(tables_loaded, 16)
            pool.wait_ge(bias_row, 1)
            pool.dma_start(scratch, brow[:, :]).then_inc(bias_stored, 16)
            pool.wait_ge(bias_stored, 16)
            pool.dma_start(hankel[:, :, :], bass.AP(scratch.tensor, 0, [[1, P], [HK, 4], [1, L]])).then_inc(hankel_loaded, 16)
            def level_masks(l):
                pool.wait_ge(tables_loaded, 32)
                for b in range(LEVELS):
                    for k in range(4):
                        if b == 0:
                            pool.wait_ge(s1["mt"].sem, s1["mt"].due(l, k + 1))
                        elif b == 1:
                            pool.wait_ge(s1["attn"].sem, s1["attn"].due(l, k + 1))
                        else:
                            pool.wait_ge(s1["p_mm"].sem, s1["p_mm"].due(l, 4 * (b - 2) + k + 1))
                        if b == 2:
                            pool.wait_ge(s1["u_new"].sem, s1["u_new"].due(l, k + 1))
                        mask = masks[:, 2 + k // 2 * LEVELS + b, :].unsqueeze(1).to_broadcast([P, 4, P])
                        nc.gpsimd.tensor_tensor(Mm[b % 2][:, k, :, :], MT[:, k, :, :], mask, ALU.mult).then_inc(s1["masked"].sem, 1)

            for st, kinds in ((0, KIND1), (1, KIND2)):
                with pool.Fori(0, DEPTH) as l:
                    for n, kind in enumerate(kinds):
                        pool.wait_ge(hi_done[st].sem, hi_done[st].due(l, n + 1))
                        nc.gpsimd.tensor_tensor(split_half(w_lo, n, kind), raw_half(n, kind),
                                                split_half(w_hi, n, kind).bitcast(F32), ALU.subtract)\
                            .then_inc(lo_done[st].sem, 1)
                        if st == 0 and n == 94 + AHEAD:
                            level_masks(l)
        @block.vector
        def _(dve):
            V = nc.vector

            def inverse_root(l, ch, dst, total, scale):
                as_int = dst.bitcast(I32)
                V.tensor_scalar(nv, total, scale, EPS, ALU.mult, ALU.add).then_inc(ch.sem, 1)
                dve.wait_ge(ch.sem, ch.step(l))
                V.tensor_scalar(as_int, nv.bitcast(I32), 1, None, ALU.logical_shift_right).then_inc(ch.sem, 1)
                dve.wait_ge(ch.sem, ch.step(l))
                V.tensor_scalar(as_int, as_int, -1, 0x5F3759DF, ALU.mult, ALU.add)
                V.tensor_scalar(nv, nv, -0.5, None, ALU.mult).then_inc(ch.sem, 1)
                dve.wait_ge(ch.sem, ch.step(l))
                for k in range(3):
                    V.tensor_tensor(ny, dst, dst, ALU.mult).then_inc(ch.sem, 1)
                    dve.wait_ge(ch.sem, ch.step(l))
                    V.tensor_tensor(ny, ny, nv, ALU.mult).then_inc(ch.sem, 1)
                    dve.wait_ge(ch.sem, ch.step(l))
                    V.scalar_tensor_tensor(dst, ny, 1.5, dst, ALU.add, ALU.mult).then_inc(ch.sem, 1)
                    dve.wait_ge(ch.sem, ch.step(l))

            def norm_scale(st, l, q):
                dve.wait_ge(n_ss[st].sem, n_ss[st].due(l, 2 * q + 2))
                inverse_root(l, dve_chain[st], rstd, ss, 1.0 / D)
                dve.wait_ge(gain_loaded[st].sem, gain_loaded[st].due(l, 16 * (q + 1)))
                for c in range(2):
                    v = slice(c * 512, (c + 1) * 512)
                    for rb in range(RB):
                        V.scalar_tensor_tensor(xn[:, rb, v], x[:, rb, v], rstd[:, rb:rb + 1], gain[:, v],
                                               ALU.mult, ALU.mult).then_inc(n_xn[st].sem, 1)

            def norm_rest(st, l, q):
                for i in range(4):
                    dve.wait_ge(n_hi[st].sem, n_hi[st].due(l, 4 * q + i + 1))
                    v = xT_hi[:, 2 * i:2 * i + 2, :].bitcast(F32)
                    V.tensor_tensor(xT_lo[:, 2 * i:2 * i + 2, :], psA[:, i, :].rearrange("p (c n) -> p c n", c=2), v,
                                    ALU.subtract).then_inc(n_lo[st].sem, 1)

            def add_to_x(st, l, q, s, scale):
                for rb in range(RB):
                    if rb == 0:
                        dve.wait_ge(first_rows[st].sem, first_rows[st].due(l, q + 1))
                    else:
                        dve.wait_ge(half_used[st].sem, half_used[st].due(l, s + 1))
                    for c in range(2):
                        v = x[:, rb, c * 512:(c + 1) * 512]
                        V.scalar_tensor_tensor(v, psB[:, 2 * rb + c, :], scale, v, ALU.mult, ALU.add)\
                            .then_inc(x_ready[st].sem, 1)

            def ffn(st, l, f, s0):
                ch = dve_chain[st]

                def convolve(n, i):
                    dve.wait_ge(half_used[st].sem, half_used[st].due(l, s0 + 4 * (n // 2) + i + 1))
                    ps, o = psA[:, i, 0:L], gconv[:, i, :]
                    c = lambda k: cols[:, 36 + k * NF + n:37 + k * NF + n]
                    V.tensor_scalar(o, ps, c(2), cols[:, 102 + n:103 + n], ALU.mult, ALU.add).then_inc(ch.sem, 1)
                    dve.wait_ge(ch.sem, ch.step(l))
                    V.scalar_tensor_tensor(o[:, 1:L], ps[:, 0:L - 1], c(1), o[:, 1:L], ALU.mult, ALU.add).then_inc(ch.sem, 1)
                    dve.wait_ge(ch.sem, ch.step(l))
                    V.scalar_tensor_tensor(o[:, 2:L], ps[:, 0:L - 2], c(0), o[:, 2:L], ALU.mult, ALU.add)\
                        .then_inc(f_conv[st].sem, 1)

                for j in range(NF // 2):
                    if st == 1:
                        for i in range(2):
                            convolve(2 * j + i, i)
                    for i in range(2):
                        n = 2 * j + i
                        dve.wait_ge(half_used[st].sem, half_used[st].due(l, s0 + 4 * j + 2 + i + 1))
                        dve.wait_ge(f_act[st].sem, f_act[st].due(l, NF * f + n + 1))
                        if n >= 2:
                            dve.wait_ge(f_lo[st].sem, f_lo[st].due(l, NF * f + n - 1))
                        V.tensor_tensor(hfull[:, i, :], sg[:, i, :], psA[:, 2 + i, 0:L], ALU.mult).then_inc(f_prod[st].sem, 1)
                    for i in range(2):
                        n = 2 * j + i
                        dve.wait_ge(f_hi[st].sem, f_hi[st].due(l, NF * f + n + 1))
                        V.tensor_tensor(hT_lo[:, n, :], hfull[:, i, :], hT_hi[:, n, :].bitcast(F32), ALU.subtract)\
                            .then_inc(f_lo[st].sem, 1)
                    if st == 0 and f == 0:
                        if j == 0:
                            columns_of_rows(l)
                        if j in (2, 4, 6):
                            mlp_argument(l, j // 2 - 1)

            def columns_of_rows(l):
                V.memset(hdn[:, 0:1], 0.0)
                dve.wait_ge(s1["cols_tp"].sem, s1["cols_tp"].due(l, 1))
                V.tensor_copy(cols[:, 0:117], psB[:, 2, 0:117]).then_inc(s1["cols"].sem, 1)

            def mlp_argument(l, k):
                ch = dve_chain[0]
                dve.wait_ge(s1["mlp_mm"].sem, s1["mlp_mm"].due(l, k + 1))
                a, n = farg[:, 0, :], farg[:, 1, :]
                big = 12582912.0
                c1 = 6.28125
                c2 = float(np.float32(np.round((2 * math.pi - c1) * 2 ** 20) / 2 ** 20))
                c3 = float(np.float32(2 * math.pi - c1 - c2))
                V.tensor_scalar(a, psB[0:HID, 3, 0:L], cols[0:HID, 113 + k:114 + k],
                                                cols[0:HID, 116:117], ALU.add, ALU.mult).then_inc(ch.sem, 1)
                dve.wait_ge(ch.sem, ch.step(l))
                V.tensor_scalar(n, a, 1 / (2 * math.pi), big, ALU.mult, ALU.add).then_inc(ch.sem, 1)
                dve.wait_ge(ch.sem, ch.step(l))
                V.tensor_scalar(n, n, big, None, ALU.subtract).then_inc(ch.sem, 1)
                dve.wait_ge(ch.sem, ch.step(l))
                for c in (c1, c2, c3):
                    V.scalar_tensor_tensor(a, n, -c, a, ALU.mult, ALU.add).then_inc(ch.sem, 1)
                    dve.wait_ge(ch.sem, ch.step(l))
                pi = float(np.nextafter(np.float32(math.pi), np.float32(0)))
                V.tensor_scalar(a, a, pi, -pi, ALU.min, ALU.max).then_inc(s1["mlp_arg"].sem, 1)

            def filters(l):
                for k in range(8):
                    dve.wait_ge(s1["filt_mm"].sem, s1["filt_mm"].due(l, k + 1))
                    V.tensor_tensor(filt[:, k // 4, k % 4, :], psA[:, k % 4, :], decay[:, k // 4, k % 4 // 2, :], ALU.mult)\
                        .then_inc(s1["filt"].sem, 1)
                for k in range(4):
                    rb, o = k // 2, k % 2
                    dve.wait_ge(s1["filt"].sem, s1["filt"].due(l, 4 * rb + 4))
                    f, b = filt[:, rb, o, :], filt[:, rb, 2 + o, :]
                    V.tensor_tensor(even[:, rb, o, :], f, b, ALU.add).then_inc(s1["even"].sem, 1)
                    dve.wait_ge(s1["even"].sem, s1["even"].due(l, k + 1))
                    V.tensor_tensor(b, f, b, ALU.subtract).then_inc(s1["odd"].sem, 1)

            def convolve1(l, i):
                ch = dve_chain[0]
                dve.wait_ge(s1["conv_mid"].sem, s1["conv_mid"].due(l, i + 1))
                ps = psA[:, i % 3, 0:L]
                if i < 12:
                    o = hyT[:, i, :]
                    w = [cols[:, 60 + k * 12 + i:61 + k * 12 + i] for k in range(CONV_HY)]
                else:
                    o = qkvT[:, i - 12, :]
                    w = [cols[:, k * 12 + i - 12:k * 12 + i - 11] for k in range(CONV1)]
                taps = [k - len(w) // 2 for k in range(len(w)) if k != len(w) // 2]
                for t in taps:
                    a, z = max(0, -t), L - max(0, t)
                    ins_ = V.scalar_tensor_tensor(o[:, a:z], ps[:, a + t:z + t], w[t + len(w) // 2], o[:, a:z], ALU.mult, ALU.add)
                    if t == taps[-1]:
                        ins_.then_inc(s1["conv"].sem, 1)
                    else:
                        ins_.then_inc(ch.sem, 1)
                        dve.wait_ge(ch.sem, ch.step(l))

            def spectral_product(l, o, b):
                ch = dve_chain[0]
                k_re, k_im = spec[:, o, b, :], spec[:, o, 2 + b, :]
                k_re2 = spec[:, o, 4 if b == 0 else 1, :]
                dve.wait_ge(s1["z_mm"].sem, s1["z_mm"].due(l, 4 * o + 2 * b + 2))
                z_re, z_im = psB[:, b, :], psB[:, 2 + b, :]
                V.tensor_tensor(ytmp[:, 0, :], z_im, k_im, ALU.mult).then_inc(ch.sem, 1)
                dve.wait_ge(ch.sem, ch.step(l))
                V.tensor_tensor(Ysp[:, b, :], z_re, k_re, ALU.mult).then_inc(ch.sem, 1)
                dve.wait_ge(ch.sem, ch.step(l))
                V.tensor_tensor(Ysp[:, b, :], Ysp[:, b, :], ytmp[:, 0, :], ALU.subtract)
                V.tensor_tensor(ytmp[:, 1, :], z_im, k_re2, ALU.mult).then_inc(ch.sem, 1)
                dve.wait_ge(ch.sem, ch.step(l))
                V.tensor_tensor(Ysp[:, 2 + b, :], z_re, k_im, ALU.mult).then_inc(ch.sem, 1)
                dve.wait_ge(ch.sem, ch.step(l))
                V.tensor_tensor(Ysp[:, 2 + b, :], Ysp[:, 2 + b, :], ytmp[:, 1, :], ALU.add).then_inc(s1["y_spec"].sem, 1)

            def hyena_gate(l, o, rb):
                ch = dve_chain[0]
                if rb == 0:
                    dve.wait_ge(s1["y_spec"].sem, s1["y_spec"].due(l, 2 * o + 2))
                    dve.wait_ge(s1["hy_nat"].sem, s1["hy_nat"].due(l, 4 + 2 * o))
                src = hynat[:, rb, 0, :] if o == 0 else zz[:, rb, :]
                V.tensor_tensor(ytmp[:, rb, :], src, skip[:, o, :], ALU.mult).then_inc(ch.sem, 1)
                dve.wait_ge(ch.sem, ch.step(l))
                dve.wait_ge(s1["inv_mm"].sem, s1["inv_mm"].due(l, 2 * o + rb + 1))
                V.tensor_tensor(ytmp[:, rb, :], ytmp[:, rb, :], psB[:, rb, :], ALU.add).then_inc(ch.sem, 1)
                dve.wait_ge(ch.sem, ch.step(l))
                V.tensor_tensor(zz[:, rb, :], ytmp[:, rb, :], hynat[:, rb, 1 + o, :], ALU.mult).then_inc(s1["zz"].sem, 1)

            def stack1_projections(l):
                ch = dve_chain[0]
                for i in range(24):
                    convolve1(l, i)
                    if i in (10, 13):
                        spectral_product(l, i // 13, 0)
                        spectral_product(l, i // 13, 1)
                    if i in (12, 15):
                        hyena_gate(l, i // 15, 0)
                        hyena_gate(l, i // 15, 1)
                    if i == 17:
                        dve.wait_ge(s1["ba_mm"].sem, s1["ba_mm"].due(l, 1))
                        V.tensor_copy(small[:, 304:336], psA[:, 3, 0:32]).then_inc(s1["ba_out"].sem, 1)
                    if i == 19:
                        dve.wait_ge(s1["hy_ss"].sem, s1["hy_ss"].due(l, 2))
                        inverse_root(l, ch, small[:, 292:294], small[:, 288:290], 1.0 / HYW)
                        for rb in range(RB):
                            ins_ = V.tensor_scalar(zz[:, rb, :], zz[:, rb, :], small[:, 292 + rb:293 + rb], None, ALU.mult)
                        ins_.then_inc(s1["hy_zn"].sem, 1)

            def deltanet(l):
                ch = dve_chain[0]
                g = lambda a, b: small[:, a:b]
                ba = g(304, 336).rearrange("p (r n) -> p r n", r=RB)
                dve.wait_ge(s1["ba_out"].sem, s1["ba_out"].due(l, 1))
                for rb in range(RB):
                    V.tensor_tensor(g(16 + 8 * rb, 24 + 8 * rb), ba[:, rb, 8:16], g(8, 16), ALU.add).then_inc(ch.sem, 1)
                    dve.wait_ge(ch.sem, ch.step(l))
                V.scalar_tensor_tensor(g(32, 48), g(16, 32), -1.0, g(16, 32), ALU.mult, ALU.max).then_inc(s1["g_arg"].sem, 1)
                dve.wait_ge(s1["g_exp"].sem, s1["g_exp"].due(l, 1))
                V.tensor_scalar(g(64, 80), g(48, 64), 1.0, None, ALU.add).then_inc(s1["g_sum"].sem, 1)
                dve.wait_ge(s1["g_sum"].sem, s1["g_sum"].due(l, 1))
                V.tensor_scalar(g(96, 112), g(64, 80), 1.0, None, ALU.subtract).then_inc(ch.sem, 1)
                dve.wait_ge(ch.sem, ch.step(l))
                V.tensor_tensor(g(96, 112), g(48, 64), g(96, 112), ALU.subtract).then_inc(ch.sem, 1)
                dve.wait_ge(ch.sem, ch.step(l))
                V.reciprocal(g(112, 128), g(64, 80)).then_inc(ch.sem, 1)
                dve.wait_ge(ch.sem, ch.step(l))
                V.tensor_tensor(g(128, 144), g(96, 112), g(112, 128), ALU.mult).then_inc(ch.sem, 1)
                dve.wait_ge(ch.sem, ch.step(l))
                dve.wait_ge(s1["g_ln"].sem, s1["g_ln"].due(l, 1))
                V.tensor_tensor(g(128, 144), g(128, 144), g(80, 96), ALU.add).then_inc(ch.sem, 1)
                dve.wait_ge(ch.sem, ch.step(l))
                V.scalar_tensor_tensor(g(128, 144), g(16, 32), 0.0, g(128, 144), ALU.max, ALU.add).then_inc(ch.sem, 1)
                dve.wait_ge(ch.sem, ch.step(l))
                for rb in range(RB):
                    V.scalar_tensor_tensor(g(152 + 8 * rb, 160 + 8 * rb), g(280, 288), -1.0,
                                                           g(128 + 8 * rb, 136 + 8 * rb), ALU.mult, ALU.mult).then_inc(ch.sem, 1)
                    dve.wait_ge(ch.sem, ch.step(l))
                V.tensor_scalar(g(168, 184), g(168, 184), 1.0, None, ALU.add).then_inc(ch.sem, 1)
                dve.wait_ge(ch.sem, ch.step(l))
                V.reciprocal(g(184, 200), g(168, 184)).then_inc(s1["g_ready"].sem, 1)
                dve.wait_ge(s1["qk_root"].sem, s1["qk_root"].due(l, 1))
                V.tensor_tensor(qkvT[:, 0:8, :], qkvT[:, 0:8, :], rr[:, :, :], ALU.mult).then_inc(s1["qk_norm"].sem, 1)
                for b in range(4):
                    dve.wait_ge(s1["y_hi"].sem, s1["y_hi"].due(l, b // 2 * 2 + 2))
                    V.scalar_tensor_tensor(xT_lo[:, 4 + b, :], psA[:, 1 + b // 2 * 2, (b % 2) * L:(b % 2 + 1) * L],
                                           cols[:, 109 + b:110 + b], xT_hi[:, 4 + b, :].bitcast(F32),
                                           ALU.mult, ALU.subtract).then_inc(s1["y_lo"].sem, 1)
                dve.wait_ge(s1["g_cum"].sem, s1["g_cum"].due(l, 1))
                V.tensor_copy(g(200, 216), psB[:, 0, 0:16]).then_inc(ch.sem, 1)
                dve.wait_ge(ch.sem, ch.step(l))
                V.tensor_tensor(g(216, 232), psB[:, 0, 16:32], g(200, 216), ALU.subtract).then_inc(s1["g_decays"].sem, 1)
                dve.wait_ge(tables_loaded, 32)
                for k in range(4):
                    d, c = k // 2, k % 2
                    dve.wait_ge(s1["row_mm"].sem, s1["row_mm"].due(l, k + 1))
                    for h in range(4):
                        n = 200 + 8 * c + 4 * d + h
                        ins_ = V.scalar_tensor_tensor(DT[:, k, h, :], psA[:, k, h * P:(h + 1) * P], g(n, n + 1), masks[:, d, :],
                                                      ALU.subtract, ALU.min)
                    ins_.then_inc(s1["row_arg"].sem, 1)
                dve.wait_ge(s1["g_col"].sem, s1["g_col"].due(l, 1))
                V.tensor_scalar(g(264, 280), g(248, 264), -1.0, None, ALU.mult).then_inc(s1["g_neg"].sem, 1)
                for d in range(DIRS):
                    dve.wait_ge(s1["q_exp"].sem, s1["q_exp"].due(l, d + 1))
                    c1 = 1 - d
                    V.tensor_tensor(qdecT[:, d, :, :], qdecT[:, d, :, :], qkvT[:, 0:4, c1 * P:(c1 + 1) * P], ALU.mult)\
                        .then_inc(s1["q_dec"].sem, 1)
                dve.wait_ge(s1["kk_mm"].sem, s1["kk_mm"].due(l, 1))
                for k in range(4):
                    d, c = k // 2, k % 2
                    dve.wait_ge(s1["row_exp"].sem, s1["row_exp"].due(l, k + 1))
                    for h in range(4):
                        n = 184 + 8 * c + 4 * d + h
                        ins_ = V.scalar_tensor_tensor(MT[:, k, h, :], psB[:, c, h * P:(h + 1) * P], g(n, n + 1), DT[:, k, h, :],
                                                      ALU.mult, ALU.mult)
                    ins_.then_inc(s1["mt"].sem, 1)
                wide = lambda v: v.unsqueeze(1).to_broadcast([P, 4, P])
                four = lambda ps: ps.rearrange("p (h n) -> p h n", h=4)
                for k in range(4):
                    dve.wait_ge(s1["masked"].sem, s1["masked"].due(l, k + 1))
                    V.tensor_tensor(U[:, k, :, :], wide(ident), Mm[0][:, k, :, :], ALU.subtract).then_inc(s1["u_new"].sem, 1)
                    dve.wait_ge(s1["p_mm"].sem, s1["p_mm"].due(l, k + 1))
                    V.tensor_tensor(T[:, k, :, :], wide(ident), four(psA[:, k, :]), ALU.subtract).then_inc(s1["t_new"].sem, 1)
                    V.tensor_tensor(attnT[:, k, :, :], four(psB[:, 2 + k % 2, :]), DT[:, k, :, :], ALU.mult).then_inc(s1["attn"].sem, 1)
                for b in range(1, LEVELS - 1):
                    for k in range(4):
                        dve.wait_ge(s1["tp_mm"].sem, s1["tp_mm"].due(l, 4 * (b - 1) + k + 1))
                        V.tensor_tensor(T[:, k, :, :], T[:, k, :, :], four(psB[:, k, :]), ALU.subtract).then_inc(s1["t_new"].sem, 1)
                for k in range(4):
                    dve.wait_ge(s1["tp_mm"].sem, s1["tp_mm"].due(l, 4 * (LEVELS - 2) + k + 1))
                    V.tensor_tensor(U[:, k, :, :], U[:, k, :, :], four(psB[:, k, :]), ALU.subtract).then_inc(s1["u_new"].sem, 1)
                idx = lambda d, c, h: 8 * c + 4 * d + h
                for d in range(DIRS):
                    for h in range(4):
                        n = 232 + idx(d, d, h)
                        ins_ = V.tensor_scalar(kdec[:, d, h, :], knat[:, d, h, :], g(n, n + 1), None, ALU.mult)
                    ins_.then_inc(s1["k_dec"].sem, 1)
                for d in range(DIRS):
                    dve.wait_ge(s1["v1_mm"].sem, s1["v1_mm"].due(l, d + 1))
                    for h in range(4):
                        n = 184 + idx(d, d, h)
                        ins_ = V.tensor_scalar(v1[:, d, h, :], psA[:, d, h * P:(h + 1) * P], g(n, n + 1), None, ALU.mult)
                    ins_.then_inc(s1["v1"].sem, 1)
                for d in range(DIRS):
                    dve.wait_ge(s1["ks_mm"].sem, s1["ks_mm"].due(l, d + 1))
                    for h in range(4):
                        n = 264 + idx(d, 1 - d, h)
                        ins_ = V.scalar_tensor_tensor(Rr[:, d, h, :], psA[:, d, h * P:(h + 1) * P], g(n, n + 1),
                                                      vnat[:, 1 - d, h, :], ALU.mult, ALU.add)
                    ins_.then_inc(s1["rest"].sem, 1)
                for d in range(DIRS):
                    dve.wait_ge(s1["v2_mm"].sem, s1["v2_mm"].due(l, d + 1))
                    for h in range(4):
                        n = 184 + idx(d, 1 - d, h)
                        ins_ = V.tensor_scalar(v2[:, d, h, :], psA[:, 2 + d, h * P:(h + 1) * P], g(n, n + 1), None, ALU.mult)
                    ins_.then_inc(s1["v2"].sem, 1)
                dve.wait_ge(s1["z_silu"].sem, s1["z_silu"].due(l, 1))
                dve.wait_ge(s1["o_root"].sem, s1["o_root"].due(l, 1))
                V.scalar_tensor_tensor(orr[:, :, :], orr[:, :, :], cols[:, 108:109], zT[:, :, :], ALU.mult, ALU.mult).then_inc(ch.sem, 1)
                dve.wait_ge(ch.sem, ch.step(l))
                V.tensor_tensor(oy[:, :, :], orr[:, :, :], psA[:, 0:2, :].rearrange("p a (b n) -> p (a b) n", b=2), ALU.mult)\
                    .then_inc(s1["o_y"].sem, 1)
                dve.wait_ge(s1["y_hi"].sem, s1["y_hi"].due(l, 5))
                V.tensor_tensor(xT_lo[:, 0:4, :], oy[:, :, :], xT_hi[:, 0:4, :].bitcast(F32), ALU.subtract).then_inc(s1["y_lo"].sem, 1)

            def rotate(l):
                ch = dve_chain[1]
                dve.wait_ge(s2["rot_mm"].sem, s2["rot_mm"].due(l, 1))
                dve.wait_ge(const_loaded, 48)
                for k in range(2):
                    two = lambda n: rotary[:, n, :].unsqueeze(1).to_broadcast([P, 2, L])
                    v = slice(2 * k, 2 * k + 2)
                    V.tensor_tensor(rtmp[:, :, :], psB[:, k, :].rearrange("p (b n) -> p b n", b=2), two(2 * k + 1), ALU.mult)
                    V.tensor_tensor(rqkr[:, v, :], rqk[:, v, :], two(2 * k), ALU.mult).then_inc(ch.sem, 1)
                    dve.wait_ge(ch.sem, ch.step(l))
                    ins_ = V.tensor_tensor(rqkr[:, v, :], rqkr[:, v, :], rtmp[:, :, :], ALU.add)
                    if k == 0:
                        ins_.then_inc(ch.sem, 1)
                        dve.wait_ge(ch.sem, ch.step(l))
                ins_.then_inc(s2["rot"].sem, 1)

            def short_convolution(l):
                ch = dve_chain[1]
                dve.wait_ge(s2["ev_dve"].sem, s2["ev_dve"].due(l, 9))
                for b in range(2):
                    w = lambda k: cols[:, 4 + 2 * k + b:5 + 2 * k + b]
                    o, v = sco[:, b, :], scx[:, b, :]
                    V.tensor_scalar(o, v, w(2), cols[:, 10 + b:11 + b], ALU.mult, ALU.add).then_inc(ch.sem, 1)
                    dve.wait_ge(ch.sem, ch.step(l))
                    V.scalar_tensor_tensor(o[:, 1:L], v[:, 0:L - 1], w(1), o[:, 1:L], ALU.mult, ALU.add).then_inc(ch.sem, 1)
                    dve.wait_ge(ch.sem, ch.step(l))
                    V.scalar_tensor_tensor(o[:, 2:L], v[:, 0:L - 2], w(0), o[:, 2:L], ALU.mult, ALU.add).then_inc(ch.sem, 1)
                    dve.wait_ge(ch.sem, ch.step(l))
                    ins_ = V.tensor_tensor(o, o, scb[:, b, :], ALU.mult)
                ins_.then_inc(s2["sc_y"].sem, 1)

            def row_maxima(l, k):
                ch = dve_chain[1]
                ps, m = psB[:, (k + 2) % 4, :], small[:, 304 + 2 * k:306 + 2 * k]
                dve.wait_ge(s2["sc_mm"].sem, s2["sc_mm"].due(l, k + 1))
                V.tensor_reduce(m[:, 0:1], ps[:, 0:L], AX_X, ALU.max)
                V.tensor_reduce(m[:, 1:2], ps[:, L:3 * P], AX_X, ALU.max).then_inc(ch.sem, 1)
                dve.wait_ge(ch.sem, ch.step(l))
                V.tensor_scalar(small[:, 320 + 2 * k:322 + 2 * k], m, -1.0, None, ALU.mult).then_inc(s2["sc_max"].sem, 1)

            def weigh_maps(l, h):
                ch = dve_chain[1]
                dve.wait_ge(s2["sc_exp"].sem, s2["sc_exp"].due(l, 2 * h + 2))
                f = small[:, 352 + 4 * h:356 + 4 * h]
                V.reciprocal(f, small[:, 336 + 4 * h:340 + 4 * h]).then_inc(ch.sem, 1)
                dve.wait_ge(ch.sem, ch.step(l))
                V.tensor_scalar(f[:, 2:4], f[:, 2:4], stat[:, 30:31], None, ALU.mult).then_inc(ch.sem, 1)
                dve.wait_ge(ch.sem, ch.step(l))
                for q, (a, z) in enumerate(((0, L), (L, 3 * P))):
                    p0, p1 = prob[:, 2 * h, a:z], prob[:, 2 * h + 1, a:z]
                    V.tensor_scalar(p1, p1, f[:, q + 2:q + 3], None, ALU.mult).then_inc(ch.sem, 1)
                    dve.wait_ge(ch.sem, ch.step(l))
                    ins_ = V.scalar_tensor_tensor(p0, p0, f[:, q:q + 1], p1, ALU.mult, ALU.add)
                ins_.then_inc(s2["sc_a"].sem, 1)

            def retention_decay(l, h):
                dve.wait_ge(s2["rs_mm"].sem, s2["rs_mm"].due(l, h + 1))
                V.tensor_tensor(iT[h][:, :], psA[:, 2 + h % 2, 0:3 * P], retdecay[:, h, :], ALU.mult).then_inc(s2["rs_dec"].sem, 1)

            def split_y(l, n):
                dve.wait_ge(s2["yb_hi"].sem, s2["yb_hi"].due(l, n + 1))
                V.tensor_tensor(yT_lo[:, n, :], yacc[:, n, :], yT_hi[:, n, :].bitcast(F32), ALU.subtract).then_inc(s2["yb_lo"].sem, 1)

            def stack2_mixer(l):
                ch = dve_chain[1]
                g = lambda a, b: small[:, a:b]
                dve.wait_ge(s2["cols2_tp"].sem, s2["cols2_tp"].due(l, 1))
                V.tensor_copy(cols[:, 0:124], psB[:, 0, 0:124]).then_inc(s2["cols2"].sem, 1)
                dve.wait_ge(param_loaded, l * (16 * NPAR2) + 16 * (DEPTH * NPAR1 + NPAR2))
                lp = g(0, 256).rearrange("p (a b n) -> p a b n", a=2, b=2)
                lq = g(256, 384).rearrange("p (a n) -> p a n", a=2)
                V.tensor_tensor(lq, lp[:, :, 0, :], lp[:, :, 1, :], ALU.mult).then_inc(ch.sem, 1)
                dve.wait_ge(ch.sem, ch.step(l))
                V.tensor_reduce(stat[:, 26:28], lq, AX_X, ALU.add).then_inc(s2["lam_sum"].sem, 1)
                dve.wait_ge(s2["cols2"].sem, s2["cols2"].due(l, 1))
                V.tensor_tensor(stat[:, 31:32], cols[:, 3:4], stat[:, 25:26], ALU.mult).then_inc(ch.sem, 1)
                dve.wait_ge(ch.sem, ch.step(l))
                projected = [i for i in range(50) if i not in (9, 11, 17)]
                done = s2["ev_dve"].sem
                for i in range(50):
                    ps = psA[:, projected.index(i) % 2, :] if i in projected else None
                    if i in (8, 10, 16):
                        dve.wait_ge(half_used[1].sem, half_used[1].due(l, i + 2))
                        dst = v_ret[:, :, :] if i == 16 else v_da[:, :, (i - 8) * P:(i - 6) * P]
                        V.tensor_copy(dst, ps.rearrange("p (r n) -> p r n", r=RB)).then_inc(done, 1)
                    elif 18 <= i < 22:
                        dve.wait_ge(half_used[1].sem, half_used[1].due(l, i + 1))
                        V.tensor_copy(rg[:, i - 18, :] if i < 20 else scb[:, i - 20, :], ps[:, 0:L]).then_inc(done, 1)
                    elif 24 <= i < 26:
                        dve.wait_ge(half_used[1].sem, half_used[1].due(l, i + 1))
                        dve.wait_ge(s2["ev_act"].sem, s2["ev_act"].due(l, 12 + i - 24 + 1))
                        V.tensor_tensor(scx[:, i - 24, :], scc[:, i - 24, :], ps[:, 0:L], ALU.mult).then_inc(done, 1)
                    elif i >= 26:
                        dve.wait_ge(half_used[1].sem, half_used[1].due(l, i + 1))
                        V.tensor_scalar(gates[:, i - 26, :], ps[:, 0:L], cols[:, 12 + i - 26:13 + i - 26], None, ALU.add).then_inc(done, 1)
                    if i == 15:
                        dve.wait_ge(s2["a_root"].sem, s2["a_root"].due(l, 1))
                        for k in range(2):
                            v = qkT[:, 4 * k:4 * k + 4, :]
                            ins_ = V.scalar_tensor_tensor(v, v, cols[:, k:k + 1], rr2[:, 4 * k:4 * k + 4, :], ALU.mult, ALU.mult)
                        ins_.then_inc(s2["a_qk"].sem, 1)
                        dve.wait_ge(s2["lam_exp"].sem, s2["lam_exp"].due(l, 1))
                        V.tensor_tensor(stat[:, 30:31], stat[:, 29:30], stat[:, 28:29], ALU.subtract).then_inc(ch.sem, 1)
                        dve.wait_ge(ch.sem, ch.step(l))
                        V.tensor_tensor(stat[:, 30:31], stat[:, 30:31], stat[:, 24:25], ALU.subtract).then_inc(ch.sem, 1)
                        dve.wait_ge(ch.sem, ch.step(l))
                    if i == 20:
                        rotate(l)
                    if i == 25:
                        short_convolution(l)
                    for k in {25: (0, 1), 26: (2, 3), 28: (4, 5), 29: (6, 7)}.get(i, ()):
                        row_maxima(l, k)
                    if i in (27, 30):
                        retention_decay(l, i // 3 * 2 - 18)
                        retention_decay(l, i // 3 * 2 - 17)
                    if 28 <= i < 32:
                        weigh_maps(l, i - 28)
                    if i == 43:
                        dve.wait_ge(s2["out_root"].sem, s2["out_root"].due(l, 1))
                        V.scalar_tensor_tensor(rr2[:, 0:4, :], rr2[:, 0:4, :], stat[:, 31:32],
                                               psB[:, 2:4, :].rearrange("p a (b n) -> p (a b) n", b=2), ALU.mult, ALU.mult)\
                            .then_inc(s2["oa_y"].sem, 1)
                    if i == 44:
                        v = rr2[:, 4:6, :]
                        V.scalar_tensor_tensor(v, v, cols[:, 2:3], rg[:, :, :], ALU.mult, ALU.mult).then_inc(ch.sem, 1)
                        dve.wait_ge(ch.sem, ch.step(l))
                        dve.wait_ge(s2["rg_sig"].sem, s2["rg_sig"].due(l, 1))
                        V.tensor_tensor(v, v, rgs[:, :, :], ALU.mult).then_inc(ch.sem, 1)
                        dve.wait_ge(ch.sem, ch.step(l))
                        V.tensor_tensor(v, v, psA[:, 2, :].rearrange("p (b n) -> p b n", b=2), ALU.mult).then_inc(s2["or_y"].sem, 1)
                    if i == 48:
                        dve.wait_ge(s2["o_hi"].sem, s2["o_hi"].due(l, 1))
                        V.tensor_tensor(daT_lo[:, :, :], rr2[:, 0:4, :], daT_hi[:, :, :].bitcast(F32), ALU.subtract)\
                            .then_inc(s2["o_lo"].sem, 1)
                dve.wait_ge(s2["o_hi"].sem, s2["o_hi"].due(l, 2))
                V.tensor_tensor(xT_lo[:, 4:6, :], rr2[:, 4:6, :], xT_hi[:, 4:6, :].bitcast(F32), ALU.subtract)
                dve.wait_ge(s2["o_hi"].sem, s2["o_hi"].due(l, 3))
                V.tensor_tensor(xT_lo[:, 6:8, :], sco[:, :, :], xT_hi[:, 6:8, :].bitcast(F32), ALU.subtract).then_inc(s2["o_lo"].sem, 1)
                for r in range(3):
                    dve.wait_ge(s2["gate_sig"].sem, s2["gate_sig"].due(l, r + 1))
                    dve.wait_ge(half_used[1].sem, half_used[1].due(l, (53, 55, 57)[r] + 1))
                    for half in range(2):
                        for n in range(4 * half, 4 * half + 4):
                            ps, v = (psB, psA)[half][:, n % 4, 0:L], gates[:, 8 * r + n, :]
                            V.tensor_tensor(yacc[:, n, :] if r == 0 else v, v, ps, ALU.mult).then_inc(s2["br"].sem, 1)
                        if r == 0:
                            continue
                        for n in range(4 * half, 4 * half + 4):
                            dve.wait_ge(s2["br"].sem, s2["br"].due(l, 8 * r + n + 1))
                            ins_ = V.tensor_tensor(yacc[:, n, :], yacc[:, n, :], gates[:, 8 * r + n, :], ALU.add)
                            if r == 1:
                                ins_.then_inc(ch.sem, 1)
                                added = ch.step(l)
                                if n == 7:
                                    dve.wait_ge(ch.sem, added)
                                continue
                            ins_.then_inc(s2["y_sum"].sem, 1)
                            if n % 4 == 1:
                                split_y(l, n - 1)
                            if n % 4 == 3:
                                split_y(l, n - 2)
                                split_y(l, n - 1)
                                split_y(l, n)

            V.memset(rows[:, :], 0.0)
            for col, value in ((eps, EPS), (eps64, 64 * EPS), (eps128, 128 * EPS)):
                ins_ = V.memset(col, value)
            ins_.then_inc(setup, 1)
            V.memset(brow[:, L:HK], MASKED)
            dve.wait_ge(bias_mm, 1)
            V.tensor_copy(brow[:, 0:L], psB[0:4, 0, 0:L]).then_inc(bias_row, 1)
            dve.wait_ge(x_loaded, 16)
            dve.sem_inc(x_ready[0].sem, 4)
            dve.sem_inc(n_xn[0].sem, 1)
            with dve.Fori(0, DEPTH) as l:
                norm_scale(0, l, 0)
                norm_rest(0, l, 0)
                dve.wait_ge(param_loaded, l * (16 * NPAR1) + 16 * NPAR1)
                V.tensor_copy(wba_hi[:, :, :], w_ba[:, :, :]).then_inc(dve_chain[0].sem, 1)
                dve.wait_ge(dve_chain[0].sem, dve_chain[0].step(l))
                V.tensor_tensor(wba_lo[:, :, :], w_ba[:, :, :], wba_hi[:, :, :].bitcast(F32), ALU.subtract).then_inc(s1["wba"].sem, 1)
                ffn(0, l, 0, 0)
                add_to_x(0, l, 0, 65, 0.5)
                filters(l)
                norm_scale(0, l, 1)
                norm_rest(0, l, 1)
                stack1_projections(l)
                deltanet(l)
                add_to_x(0, l, 1, 101, 1.0)
                norm_scale(0, l, 2)
                norm_rest(0, l, 2)
                ffn(0, l, 1, 102)
                add_to_x(0, l, 2, 167, 0.5)
            steps["dve_chain"] = [dve_chain[0].n, 0, 12]
            dve.wait_ge(n_ss[0].sem, n_ss[0].due(DEPTH, 2))
            inverse_root(0, dve_chain[2], rstd, ss, 1.0 / D)
            dve.wait_ge(gain_loaded[0].sem, gain_loaded[0].due(DEPTH, 16))
            for rb in range(RB):
                V.scalar_tensor_tensor(x[:, rb, :], x[:, rb, :], rstd[:, rb:rb + 1], gain[:, :],
                                       ALU.mult, ALU.mult).then_inc(x_ready[0].sem, 2)
            dve.wait_ge(x_ready[1].sem, x_ready[1].due(0, 0))
            dve.sem_inc(n_xn[0].sem, 4)
            with dve.Fori(0, DEPTH) as l:
                norm_scale(1, l, 0)
                norm_rest(1, l, 0)
                stack2_mixer(l)
                add_to_x(1, l, 0, 65, 1.0)
                norm_scale(1, l, 1)
                norm_rest(1, l, 1)
                ffn(1, l, 0, 66)
                add_to_x(1, l, 1, 131, 1.0)
            steps["dve_chain"][1] = dve_chain[1].n

        @block.tensor
        def _(pe):
            M = nc.tensor.matmul

            def turn_x(st, l, q):
                for i in range(4):
                    if i % 2 == 0:
                        pe.wait_ge(n_xn[st].sem, n_xn[st].due(l, 4 * q + 2 + i))
                    for kc in (2 * i, 2 * i + 1):
                        for rb in range(RB):
                            c = (kc % 2) * L + rb * P
                            ins_ = nc.tensor.transpose(psA[:, i, c:c + P], xn[:, rb, kc * P:(kc + 1) * P], ident)
                    ins_.then_inc(n_tp[st].sem, 1)

            def project_T(st, l, s, o, q=None):
                pe.wait_ge(lo_done[st].sem, lo_done[st].due(l, s + 1))
                hi, lo = split_half(w_hi, s, "A"), split_half(w_lo, s, "A")
                for kc in range(KC):
                    if q is not None and kc % 2 == 0:
                        pe.wait_ge(n_lo[st].sem, n_lo[st].due(l, 4 * q + kc // 2 + 1))
                    ins_ = product(o, hi[:, kc, :], lo[:, kc, :], xT_hi[:, kc, :], xT_lo[:, kc, :], kc == 0, kc == KC - 1)
                ins_.then_inc(half_used[st].sem, 1)

            def project_two(st, l, s, o):
                pe.wait_ge(lo_done[st].sem, lo_done[st].due(l, s + 2))
                two = lambda w: w[:, s % SLOTS:s % SLOTS + 2, :].rearrange("p s (c n) -> p s c n", c=KC)
                hi, lo = two(w_hi), two(w_lo)
                for rb in range(RB):
                    t = slice(rb * P, (rb + 1) * P)
                    for kc in range(KC):
                        ins_ = product(o[:, rb * L:(rb + 1) * L], xT_hi[:, kc, t], xT_lo[:, kc, t], hi[:, :, kc, :], lo[:, :, kc, :],
                                       kc == 0, kc == KC - 1)
                ins_.then_inc(half_used[st].sem, 2)

            def into_x(st, l, s0, a_hi, a_lo, made=None, counted=0, blocks=None, last=False):
                whole = blocks is None
                blocks = range(a_hi.shape[1]) if whole else blocks
                for n, k in enumerate(blocks):
                    pe.wait_ge(lo_done[st].sem, lo_done[st].due(l, s0 + n + 1))
                    if made:
                        pe.wait_ge(made.sem, made.due(l, counted + k + 1))
                    hi, lo = split_half(w_hi, s0 + n, "B"), split_half(w_lo, s0 + n, "B")
                    starts = n == 0 and (whole or s0 == 94)
                    ends = n == len(blocks) - 1 and (whole or last)
                    for rb in range(RB):
                        t = slice(rb * P, (rb + 1) * P)
                        for c in range(2):
                            v = slice(c * 512, (c + 1) * 512)
                            ins_ = product(psB[:, 2 * rb + c, :], a_hi[:, k, t], a_lo[:, k, t], hi[:, v], lo[:, v], starts, ends)
                        if ends and rb == 0:
                            ins_.then_inc(first_rows[st].sem, 1)
                    ins_.then_inc(half_used[st].sem, 1)

            def ffn(st, l, f, s0, q):
                freed = f_act[0] if st == 0 else f_conv[1]
                for j in range(NF // 2):
                    for i in range(2):
                        if j:
                            pe.wait_ge(freed.sem, freed.due(l, NF * f + 2 * (j - 1) + i + 1))
                        project_T(st, l, s0 + 4 * j + i, psA[:, i, 0:L], q if j == 0 and i == 0 else None)
                    for i in range(2):
                        if j:
                            pe.wait_ge(f_prod[st].sem, f_prod[st].due(l, NF * f + 2 * (j - 1) + i + 1))
                        project_T(st, l, s0 + 4 * j + 2 + i, psA[:, 2 + i, 0:L])
                    if st == 0 and f == 0:
                        if j == 0:
                            turn_rows1(l)
                        if j in (1, 3, 5):
                            mlp(l, j // 2)
                into_x(st, l, s0 + 2 * NF, hT_hi, hT_lo, f_lo[st], NF * f)

            def turn_rows1(l):
                pe.wait_ge(param_loaded, l * (16 * NPAR1) + 16 * NPAR1)
                nc.tensor.transpose(psB[:, 2, 0:117], rows[0:117, :], ident[0:117, 0:117]).then_inc(s1["cols_tp"].sem, 1)

            def mlp(l, k):
                if k == 0:
                    pe.wait_ge(s1["cols"].sem, s1["cols"].due(l, 1))
                else:
                    pe.wait_ge(s1["mlp_sin"].sem, s1["mlp_sin"].due(l, k))
                n, rhs = (EMB, featsT[:, :]) if k == 0 else (HID, hdn[:, 1:L + 1])
                M(psB[:, 3, 0:L], fw[0:n, k:k + 2, :].rearrange("p a b -> p (a b)"), rhs, start=True, stop=True)\
                    .then_inc(s1["mlp_mm"].sem, 1)

            def filters(l):
                pe.wait_ge(s1["mlp_sin"].sem, s1["mlp_sin"].due(l, 3))
                for k in range(8):
                    if k >= 4:
                        pe.wait_ge(s1["filt"].sem, s1["filt"].due(l, k - 3))
                    rb, n = k // 4, k % 4
                    t0 = rb * P + (1 if n < 2 else 0)
                    M(psA[:, n, :], hdn[:, t0:t0 + P], wfilt[:, n * HYW:(n + 1) * HYW], start=True, stop=True)\
                        .then_inc(s1["filt_mm"].sem, 1)
                pe.wait_ge(tables_loaded, 32)
                for k in range(10):
                    o, b = k // 5, k % 5
                    pe.wait_ge(s1["odd"].sem, s1["odd"].due(l, 4))
                    if k >= 4:
                        pe.wait_ge(s1["spec"].sem, s1["spec"].due(l, k - 3))
                    for rb in range(RB):
                        src = filt[:, rb, 2 + o, :] if b in (2, 3) else even[:, rb, o, :]
                        ins_ = M(psA[:, k % 4, :], dft_f[:, rb, b, :], src, start=(rb == 0), stop=(rb == RB - 1))
                    ins_.then_inc(s1["spec_mm"].sem, 1)
                pe.wait_ge(s1["spec"].sem, s1["spec"].due(l, 10))

            def turn_hyena(l, k):
                pe.wait_ge(s1["conv"].sem, s1["conv"].due(l, 4 * (k // 2) + 4))
                if k == 5:
                    pe.wait_ge(s1["hy_nat"].sem, s1["hy_nat"].due(l, 5))
                ps = psB[:, k, :] if k < 4 else psA[:, 3, :]
                for b in range(4):
                    ins_ = nc.tensor.transpose(ps[:, b * P:(b + 1) * P], hyT[:, 4 * (k // 2) + b, (k % 2) * P:(k % 2 + 1) * P], ident)
                ins_.then_inc(s1["hy_turned"].sem, 1)

            def hyena_spectrum(l, o):
                if o == 0:
                    pe.wait_ge(s1["hy_nat"].sem, s1["hy_nat"].due(l, 4))
                else:
                    pe.wait_ge(s1["zz"].sem, s1["zz"].due(l, 2))
                for b, table in ((0, 0), (2, 5), (1, 1), (3, 3)):
                    for rb in range(RB):
                        src = hynat[:, rb, 0, :] if o == 0 else zz[:, rb, :]
                        ins_ = M(psB[:, b, :], dft_f[:, rb, table, :], src, start=(rb == 0), stop=(rb == RB - 1))
                    ins_.then_inc(s1["z_mm"].sem, 1)

            def hyena_inverse(l, o):
                pe.wait_ge(s1["y_spec"].sem, s1["y_spec"].due(l, 2 * o + 2))
                for rb in range(RB):
                    for b in range(4):
                        ins_ = M(psB[:, rb, :], dft_i[:, b, rb * P:(rb + 1) * P], Ysp[:, b, :], start=(b == 0), stop=(b == 3))
                    ins_.then_inc(s1["inv_mm"].sem, 1)

            def gate_columns(l):
                pe.wait_ge(s1["wba"].sem, s1["wba"].due(l, 1))
                pe.wait_ge(s1["hy_nat"].sem, s1["hy_nat"].due(l, 6))
                for rb in range(RB):
                    t = slice(rb * P, (rb + 1) * P)
                    for kc in range(KC):
                        ins_ = product(psA[:, 3, 16 * rb:16 * rb + 16], xT_hi[:, kc, t], xT_lo[:, kc, t],
                                       wba_hi[:, kc, :], wba_lo[:, kc, :], kc == 0, kc == KC - 1)
                ins_.then_inc(s1["ba_mm"].sem, 1)

            def qk_sums(l):
                pe.wait_ge(s1["qk_sq"].sem, s1["qk_sq"].due(l, 1))
                pe.wait_ge(s1["zz"].sem, s1["zz"].due(l, 4))
                for k in range(4):
                    ins_ = M(psB[:, k, :], ones, sq[:, 2 * k:2 * k + 2, :].rearrange("p b n -> p (b n)"), start=True, stop=True)
                ins_.then_inc(s1["qk_mm"].sem, 1)

            def stack1_projections(l):
                for i in range(28):
                    if 3 <= i < 27:
                        pe.wait_ge(s1["conv"].sem, s1["conv"].due(l, i - 2))
                    elif i == 27:
                        pe.wait_ge(s1["z_out"].sem, s1["z_out"].due(l, 1))
                    project_T(0, l, 66 + i, psA[:, i % 3, 0:L], 1 if i == 0 else None)
                    if i == 5:
                        turn_hyena(l, 0)
                        turn_hyena(l, 1)
                    if i == 9:
                        turn_hyena(l, 2)
                        turn_hyena(l, 3)
                    if i == 10:
                        hyena_spectrum(l, 0)
                    if i == 12:
                        hyena_inverse(l, 0)
                    if i == 13:
                        hyena_spectrum(l, 1)
                        turn_hyena(l, 4)
                    if i == 14:
                        turn_hyena(l, 5)
                    if i == 15:
                        hyena_inverse(l, 1)
                    if i == 16:
                        gate_columns(l)
                    if i == 22:
                        qk_sums(l)
                pe.wait_ge(s1["hy_zn"].sem, s1["hy_zn"].due(l, 1))
                pe.wait_ge(s1["z_out"].sem, s1["z_out"].due(l, 2))
                pe.wait_ge(s1["ba_out"].sem, s1["ba_out"].due(l, 1))
                for b in range(4):
                    for rb in range(RB):
                        c = (b % 2) * L + rb * P
                        ins_ = nc.tensor.transpose(psA[:, 1 + b // 2 * 2, c:c + P], zz[:, rb, b * P:(b + 1) * P], ident)
                    if b % 2:
                        ins_.then_inc(s1["hy_back"].sem, 1)

            def deltanet(l):
                g = lambda n: small[:, 152 + n:153 + n]
                pe.wait_ge(s1["qk_norm"].sem, s1["qk_norm"].due(l, 1))
                for k in range(4):
                    for h in range(4):
                        ins_ = nc.tensor.transpose(psB[:, k, h * P:(h + 1) * P],
                                                   qkvT[:, 4 + 4 * (k // 2) + h, (k % 2) * P:(k % 2 + 1) * P], ident)
                    ins_.then_inc(s1["kv_turned"].sem, 1)
                pe.wait_ge(s1["g_ready"].sem, s1["g_ready"].due(l, 1))
                pe.wait_ge(s1["kv_nat"].sem, s1["kv_nat"].due(l, 4))
                for c in range(RB):
                    for d in range(DIRS):
                        n = 8 * c + 4 * d
                        M(psB[:, 0, n:n + 4], cum[d], small[:, 152 + n:156 + n], start=True, stop=True)
                    ins_ = M(psB[:, 0, 16 + 8 * c:24 + 8 * c], ones, small[:, 152 + 8 * c:160 + 8 * c], start=True, stop=True)
                ins_.then_inc(s1["g_cum"].sem, 1)
                pe.wait_ge(s1["z_out"].sem, s1["z_out"].due(l, 4))
                pe.wait_ge(s1["y_lo"].sem, s1["y_lo"].due(l, 4))
                for k in range(4):
                    d, c = k // 2, k % 2
                    for h in range(4):
                        ins_ = M(psA[:, k, h * P:(h + 1) * P], g(8 * c + 4 * d + h).to_broadcast([P, P]), cum[d], start=True, stop=True)
                    ins_.then_inc(s1["row_mm"].sem, 1)
                pe.wait_ge(s1["g_decays"].sem, s1["g_decays"].due(l, 1))
                for c in range(RB):
                    t = slice(c * P, (c + 1) * P)
                    for h in range(4):
                        o = slice(h * P, (h + 1) * P)
                        M(psB[:, c, o], qkvT[:, 4 + h, t], qkvT[:, 4 + h, t], start=True, stop=True)
                        ins_ = M(psB[:, 2 + c, o], qkvT[:, 4 + h, t], qkvT[:, h, t], start=True, stop=True)
                ins_.then_inc(s1["kk_mm"].sem, 1)
                pe.wait_ge(s1["q_exp"].sem, s1["q_exp"].due(l, 2))
                pe.wait_ge(s1["row_arg"].sem, s1["row_arg"].due(l, 4))
                for b in range(LEVELS):
                    for k in range(4):
                        if b > 1:
                            pe.wait_ge(s1["t_new"].sem, s1["t_new"].due(l, 4 * (b - 1) + k + 1))
                            for h in range(4):
                                ins_ = nc.tensor.transpose(psA[:, k, h * P:(h + 1) * P], T[:, k, h, :], ident)
                            ins_.then_inc(s1["u_tp"].sem, 1)
                        if b == 1:
                            pe.wait_ge(s1["t_new"].sem, s1["t_new"].due(l, k + 1))
                        pe.wait_ge(s1["masked"].sem, s1["masked"].due(l, 4 * b + k + 1))
                        if b == 1 and k == 2:
                            pe.wait_ge(s1["attn"].sem, s1["attn"].due(l, 4))
                        for h in range(4):
                            if b == 0:
                                ins_ = nc.tensor.transpose(psA[:, k, h * P:(h + 1) * P], Mm[0][:, k, h, :], ident)
                            else:
                                ins_ = M(psB[:, k, h * P:(h + 1) * P], Mm[b % 2][:, k, h, :], T[:, k, h, :], start=True, stop=True)
                        ins_.then_inc(s1["p_mm"].sem, 1)
                    for k in range(4):
                        if b == 0:
                            continue
                        pe.wait_ge(s1["p_copy"].sem, s1["p_copy"].due(l, 4 * (b - 1) + k + 1))
                        if b == 1:
                            pe.wait_ge(s1["u_new"].sem, s1["u_new"].due(l, k + 1))
                        else:
                            pe.wait_ge(s1["u_act"].sem, s1["u_act"].due(l, 4 * (b - 2) + k + 1))
                        for h in range(4):
                            a, c = (U, Pp) if b < LEVELS - 1 else (Pp, U)
                            ins_ = M(psB[:, k, h * P:(h + 1) * P], a[:, k, h, :], c[:, k, h, :], start=True, stop=True)
                        ins_.then_inc(s1["tp_mm"].sem, 1)
                part = lambda ps, h: ps[:, h * P:(h + 1) * P]
                pe.wait_ge(s1["u_new"].sem, s1["u_new"].due(l, 8))
                for d in range(DIRS):
                    for h in range(4):
                        ins_ = M(part(psA[:, d, :], h), U[:, 2 * d + d, h, :], vnat[:, d, h, :], start=True, stop=True)
                    ins_.then_inc(s1["v1_mm"].sem, 1)
                into_x(0, l, 94, xT_hi, xT_lo, blocks=(4,))
                for d in range(DIRS):
                    pe.wait_ge(s1["v1"].sem, s1["v1"].due(l, d + 1))
                    pe.wait_ge(s1["k_dec"].sem, s1["k_dec"].due(l, d + 1))
                    for h in range(4):
                        ins_ = M(part(psA[:, 2 + d, :], h), kdec[:, d, h, :], v1[:, d, h, :], start=True, stop=True)
                    ins_.then_inc(s1["s_mm"].sem, 1)
                into_x(0, l, 95, xT_hi, xT_lo, blocks=(5,))
                for d in range(DIRS):
                    c1 = 1 - d
                    pe.wait_ge(s1["s_copy"].sem, s1["s_copy"].due(l, d + 1))
                    for h in range(4):
                        ins_ = M(part(psA[:, d, :], h), qkvT[:, 4 + h, c1 * P:(c1 + 1) * P], Sst[:, d, h, :], start=True, stop=True)
                    ins_.then_inc(s1["ks_mm"].sem, 1)
                into_x(0, l, 96, xT_hi, xT_lo, blocks=(6,))
                for d in range(DIRS):
                    pe.wait_ge(s1["rest"].sem, s1["rest"].due(l, d + 1))
                    for h in range(4):
                        ins_ = M(part(psA[:, 2 + d, :], h), U[:, 2 * d + 1 - d, h, :], Rr[:, d, h, :], start=True, stop=True)
                    ins_.then_inc(s1["v2_mm"].sem, 1)
                into_x(0, l, 97, xT_hi, xT_lo, blocks=(7,))
                pe.wait_ge(s1["q_dec"].sem, s1["q_dec"].due(l, 2))
                pe.wait_ge(s1["v2"].sem, s1["v2"].due(l, 2))
                for h in range(4):
                    for c in range(RB):
                        o = psA[:, h // 2, (h % 2) * L + c * P:(h % 2) * L + (c + 1) * P]
                        a, b = c, 1 - c
                        M(o, v1[:, a, h, :], attnT[:, 2 * a + c, h, :], start=True, stop=False)
                        M(o, Sst[:, b, h, :], qdecT[:, b, h, :], start=False, stop=False)
                        ins_ = M(o, v2[:, b, h, :], attnT[:, 2 * b + c, h, :], start=False, stop=True)
                    if h % 2:
                        ins_.then_inc(s1["o_mm"].sem, 1)
                pe.wait_ge(s1["o_sq"].sem, s1["o_sq"].due(l, 1))
                for k in range(2):
                    ins_ = M(psA[:, 2 + k, :], ones, osq[:, 2 * k:2 * k + 2, :].rearrange("p b n -> p (b n)"), start=True, stop=True)
                ins_.then_inc(s1["o_ss"].sem, 1)
                pe.wait_ge(s1["y_lo"].sem, s1["y_lo"].due(l, 5))
                into_x(0, l, 98, xT_hi, xT_lo, blocks=range(4), last=True)

            def scores(l, k):
                h, r = k // 2, slice(64 * (k % 2), 64 * (k % 2) + 64)
                ps = psB[:, (k + 2) % 4, :]
                if k >= 4:
                    pe.wait_ge(s2["sc_exp"].sem, s2["sc_exp"].due(l, k - 3))
                M(ps[:, 0:L], flip, hankel[:, h, :], start=True, stop=False)
                M(ps[:, 0:L], qkT[r, h, P:L], qkT[r, 4 + h, :], start=False, stop=True)
                M(ps[:, L:3 * P], flip, hankel[:, h, P:L], start=True, stop=False)
                ins_ = M(ps[:, L:3 * P], qkT[r, h, 0:P], qkT[r, 4 + h, 0:P], start=False, stop=True)
                ins_.then_inc(s2["sc_mm"].sem, 1)

            def turn_attention(l, h):
                pe.wait_ge(s2["sc_a"].sem, s2["sc_a"].due(l, h + 1))
                pe.wait_ge(s2["sc_exp"].sem, s2["sc_exp"].due(l, (6, 6, 8, 8)[h]))
                a, ps = prob[:, 2 * h, :], psB[:, (h + 2) % 4, :]
                nc.tensor.transpose(ps[:, 0:P], a[:, L:3 * P], ident)
                nc.tensor.transpose(ps[:, P:2 * P], a[:, 0:P], ident)
                nc.tensor.transpose(ps[:, 2 * P:3 * P], a[:, P:2 * P], ident).then_inc(s2["a_turned"].sem, 1)

            def attend(l, h2):
                pe.wait_ge(s2["a_copy"].sem, s2["a_copy"].due(l, 2 * h2 + 2))
                for h in (2 * h2, 2 * h2 + 1):
                    o = psB[:, 2 + h2, (h % 2) * L:(h % 2 + 1) * L]
                    M(o, v_da[:, 0, h * P:(h + 1) * P], aT[:, h, 0:L], start=True, stop=False)
                    ins_ = M(o[:, P:L], v_da[:, 1, h * P:(h + 1) * P], aT[:, h, L:3 * P], start=False, stop=True)
                ins_.then_inc(s2["oa_mm"].sem, 1)

            def retention_scores(l, h):
                b, r = h // 2, slice(64 * (h % 2), 64 * (h % 2) + 64)
                ps = psA[:, 2 + h % 2, :]
                if h >= 2:
                    pe.wait_ge(s2["rs_dec"].sem, s2["rs_dec"].due(l, h - 1))
                M(ps[:, 0:L], rqkr[r, 2 + b, 0:P], rqkr[r, b, :], start=True, stop=True)
                M(ps[:, L:3 * P], rqkr[r, 2 + b, P:L], rqkr[r, b, P:L], start=True, stop=True).then_inc(s2["rs_mm"].sem, 1)

            def retain(l):
                pe.wait_ge(s2["rs_dec"].sem, s2["rs_dec"].due(l, 4))
                for h in range(4):
                    b, r = h // 2, slice(64 * (h % 2), 64 * (h % 2) + 64)
                    o = psA[r, 2, b * L:(b + 1) * L]
                    v = v_ret[:, :, h * 64:(h + 1) * 64]
                    M(o, v[:, 0, :], iT[h][:, 0:L], start=True, stop=False)
                    ins_ = M(o[:, P:L], v[:, 1, :], iT[h][:, L:3 * P], start=False, stop=True)
                ins_.then_inc(s2["or_mm"].sem, 1)

            def stack2_mixer(l):
                pe.wait_ge(param_loaded, l * (16 * NPAR2) + 16 * (DEPTH * NPAR1 + NPAR2))
                nc.tensor.transpose(psB[:, 0, 0:124], rows[0:124, :], ident[0:124, 0:124]).then_inc(s2["cols2_tp"].sem, 1)
                by_act = tuple(range(8)) + (12, 13, 14, 15, 22, 23)
                projected = [i for i in range(50) if i not in (9, 11, 17)]
                by_dve = [i for i in projected if i not in by_act]
                for n, i in enumerate(projected):
                    if n >= 2:
                        before = projected[n - 2]
                        if before in by_act:
                            pe.wait_ge(s2["ev_act"].sem, s2["ev_act"].due(l, by_act.index(before) + 1))
                        else:
                            pe.wait_ge(s2["ev_dve"].sem, s2["ev_dve"].due(l, by_dve.index(before) + 1))
                    if i in (8, 10, 16):
                        project_two(1, l, i, psA[:, n % 2, :])
                    else:
                        project_T(1, l, i, psA[:, n % 2, 0:L], 0 if i == 0 else None)
                    if i == 10:
                        pe.wait_ge(s2["a_sq"].sem, s2["a_sq"].due(l, 1))
                        pe.wait_ge(s2["cols2"].sem, s2["cols2"].due(l, 1))
                        for k in range(4):
                            ins_ = M(psB[:, k, :], blockones, sq2[:, 2 * k:2 * k + 2, :].rearrange("p b n -> p (b n)"),
                                     start=True, stop=True)
                        ins_.then_inc(s2["a_mm"].sem, 1)
                    if i == 18:
                        pe.wait_ge(s2["a_root"].sem, s2["a_root"].due(l, 1))
                        pe.wait_ge(s2["ev_act"].sem, s2["ev_act"].due(l, 12))
                        for b in range(4):
                            ins_ = M(psB[:, b // 2, (b % 2) * L:(b % 2 + 1) * L], rot, rqk[:, b, :], start=True, stop=True)
                        ins_.then_inc(s2["rot_mm"].sem, 1)
                    if i == 25:
                        pe.wait_ge(hankel_loaded, 16)
                        pe.wait_ge(s2["a_qk"].sem, s2["a_qk"].due(l, 1))
                        scores(l, 0)
                        scores(l, 1)
                    if i == 26:
                        pe.wait_ge(s2["rot"].sem, s2["rot"].due(l, 1))
                        scores(l, 2)
                        scores(l, 3)
                    if i in (27, 30):
                        retention_scores(l, i // 3 * 2 - 18)
                        retention_scores(l, i // 3 * 2 - 17)
                    if i in (28, 29):
                        scores(l, 2 * i - 52)
                        scores(l, 2 * i - 51)
                    if 32 <= i < 36:
                        turn_attention(l, i - 32)
                    if i == 33:
                        retain(l)
                    if i == 36:
                        pe.wait_ge(s2["or_sq"].sem, s2["or_sq"].due(l, 1))
                        M(psA[:, 3, :], blockones, sq2[:, 4:6, :].rearrange("p b n -> p (b n)"), start=True, stop=True)\
                            .then_inc(s2["or_ss"].sem, 1)
                    if i in (37, 38):
                        attend(l, i - 37)
                    if i == 40:
                        pe.wait_ge(s2["oa_sq"].sem, s2["oa_sq"].due(l, 1))
                        for k in range(2):
                            ins_ = M(psB[:, k, :], ones, sq2[:, 2 * k:2 * k + 2, :].rearrange("p b n -> p (b n)"), start=True, stop=True)
                        ins_.then_inc(s2["oa_ss"].sem, 1)
                pe.wait_ge(s2["ev_dve"].sem, s2["ev_dve"].due(l, 33))
                k = 0
                for r, n in enumerate((4, 2, 2)):
                    pe.wait_ge(s2["o_lo"].sem, s2["o_lo"].due(l, 1 if r == 0 else 2))
                    x_hi, x_lo = (daT_hi, daT_lo) if r == 0 else (xT_hi, xT_lo)
                    for i in range(n):
                        pe.wait_ge(lo_done[1].sem, lo_done[1].due(l, 50 + k + 1))
                        hi, lo = split_half(w_hi, 50 + k, "B"), split_half(w_lo, 50 + k, "B")
                        for c in range(KC):
                            if r and i == 0:
                                pe.wait_ge(s2["br"].sem, s2["br"].due(l, 8 * (r - 1) + c + 1))
                            o = (psB, psA)[c // 4][:, c % 4, 0:L]
                            v = slice(c * P, (c + 1) * P)
                            ins_ = product(o, hi[:, v], lo[:, v], x_hi[:, k, :], x_lo[:, k, :], i == 0, i == n - 1)
                        ins_.then_inc(half_used[1].sem, 1)
                        k += 1
                pe.wait_ge(s2["br"].sem, s2["br"].due(l, 20))
                into_x(1, l, 58, yT_hi, yT_lo, s2["yb_lo"])

            pe.sem_inc(half_used[0].sem, SLOTS)
            pe.wait_ge(const_loaded, 16)
            pe.wait_ge(bias_loaded, 32)
            M(psB[0:4, 0, 0:HK], relb[:, :], onehot[:, :], start=True, stop=True).then_inc(bias_mm, 1)
            with pe.Fori(0, DEPTH) as l:
                turn_x(0, l, 0)
                ffn(0, l, 0, 0, 0)
                filters(l)
                turn_x(0, l, 1)
                stack1_projections(l)
                deltanet(l)
                turn_x(0, l, 2)
                ffn(0, l, 1, 102, 2)
            with pe.Fori(0, DEPTH) as l:
                turn_x(1, l, 0)
                stack2_mixer(l)
                turn_x(1, l, 1)
                ffn(1, l, 0, 66, 1)

    return steps


_INS = ["x", "ffn1_norm", "ffn1_w_gate", "ffn1_w_up", "ffn1_w_down", "mix_norm", "w_in", "dn_conv", "dn_a_log",
        "dn_dt_bias", "dn_norm", "hy_conv", "hy_conv_bias", "hy_f_w1", "hy_f_b1", "hy_f_w2", "hy_f_b2", "hy_f_w3",
        "hy_f_b3", "hy_f_freq", "hy_f_wout", "hy_skip", "hy_norm", "w_out", "ffn2_norm", "ffn2_w_gate", "ffn2_w_up",
        "ffn2_w_down", "final_norm", "rel_bias_2", "norm_mix_g_2", "w_in_2", "b_gate_2", "da_q_norm_g_2",
        "da_k_norm_g_2", "da_lambda_2", "da_subln_g_2", "ret_norm_g_2", "sc_conv_w_2", "sc_conv_b_2",
        "w_branch_da_2", "w_branch_ret_2", "w_branch_sc_2", "w_out_2", "norm_ffn_g_2", "w_ffn_in_2", "ffn_conv_w_2",
        "ffn_conv_b_2", "w_ffn_out_2"]


def kernel(**inputs):
    import concourse.bacc as bacc
    from concourse.bass_utils import run_bass_kernel_spmd

    arrays = {n: np.ascontiguousarray(inputs[n]) for n in _INS}
    arrays |= {"c_" + n: np.ascontiguousarray(a) for n, a in constants().items()}
    arrays["c_dft"] = arrays["c_dft"].reshape(P, -1)
    count = {}
    for last in (False, True):
        nc = bacc.Bacc("TRN2", target_bir_lowering=False, num_devices=1)
        ins = {n: nc.dram_tensor("in_" + n, a.shape, mybir.dt.from_np(a.dtype), kind="ExternalInput").ap()
               for n, a in arrays.items()}
        out = nc.dram_tensor("out_x", (1, L, D), F32, kind="ExternalOutput").ap()
        count = emit(nc, ins, out, count)
    r = run_bass_kernel_spmd(nc, [{"in_" + n: a for n, a in arrays.items()}], core_ids=[0])
    return r.results[0]["out_x"]
```
